# Optimizing a Trainium2 kernel written in Bass

```python
import math
import jax, jax.numpy as jnp
from jax import lax
import numpy as np

D_MODEL = 1024
BATCH = 1
SEQ = 128
DEPTH = 2
DEC_BATCH = 1
DEC_SEQ = 512
PAST_LEN = 128

GRID_W = 64
HEAD_DIM = 64
N_MIX_HEADS = D_MODEL // HEAD_DIM
A_HEADS = N_MIX_HEADS // 4
A_DK = HEAD_DIM
A_DV = HEAD_DIM
A_CHUNK = 64
B_QHEADS = N_MIX_HEADS // 2
B_KVHEADS = B_QHEADS // 4
B_GROUP = B_QHEADS // B_KVHEADS
B_HD = HEAD_DIM
WINDOW = 128
C_HEADS = N_MIX_HEADS // 4
C_DH = HEAD_DIM // 2
C_DV = HEAD_DIM
A_WIDTH = A_HEADS * A_DV
B_WIDTH = B_QHEADS * B_HD
C_WIDTH = C_HEADS * C_DV
MIX_WIDTH = A_WIDTH + B_WIDTH + C_WIDTH
IN_SIZES = (A_HEADS * A_DK, A_HEADS * A_DK, A_WIDTH, A_WIDTH, 4 * A_HEADS,
            B_WIDTH, B_KVHEADS * B_HD, B_KVHEADS * B_HD,
            C_HEADS * 2 * C_DH, C_HEADS * 2 * C_DH, C_WIDTH)
IN_COLS = sum(IN_SIZES)
IN_SPLITS = tuple(sum(IN_SIZES[:i + 1]) for i in range(len(IN_SIZES) - 1))
A_GATE_START = IN_SPLITS[3]
QB = 128
ROPE_BASE = 10000.0
EPS = 1e-6
N_KEYS = 128
N_EXPERTS = N_KEYS * N_KEYS
PEER_HEADS = 8
PEER_TOPK = 16
PEER_DQ = 256
FORGET_BIAS = 3.0
F32 = jnp.float32

kernel_name = 'hybrid_mlstm_swa_diffattn_peer_dit_step'

def rms_norm(x, gain):
    xf = x.astype(F32)
    y = xf * lax.rsqrt(jnp.mean(xf * xf, axis=-1, keepdims=True) + EPS)
    return (y * gain.astype(F32)).astype(x.dtype)

def ada_modulation(cond, w, b):
    m = jax.nn.silu(cond) @ w + b
    return jnp.split(m[:, None, :], 6, axis=-1)

def axial_rope_tables(n_tokens, dim):
    quarter = dim // 4
    inv = ROPE_BASE ** (-jnp.arange(quarter, dtype=F32) / quarter)
    t = jnp.arange(n_tokens)
    row = (t // GRID_W).astype(F32)
    col = (t % GRID_W).astype(F32)
    ang = jnp.stack([row[:, None] * inv, col[:, None] * inv], axis=1)
    return jnp.cos(ang), jnp.sin(ang)

def apply_axial_rope(x, cos, sin):
    dim = x.shape[-1]
    half, quarter = dim // 2, dim // 4
    shape = (1, x.shape[1]) + (1,) * (x.ndim - 3) + (quarter,)
    xf = x.astype(F32)

    def rot(h, cs, sn):
        h1, h2 = h[..., :quarter], h[..., quarter:]
        return jnp.concatenate([h1 * cs - h2 * sn, h2 * cs + h1 * sn], axis=-1)

    out = jnp.concatenate([
        rot(xf[..., :half], cos[:, 0].reshape(shape), sin[:, 0].reshape(shape)),
        rot(xf[..., half:], cos[:, 1].reshape(shape), sin[:, 1].reshape(shape))], axis=-1)
    return out.astype(x.dtype)

def mlstm_chunkwise(q, k, v, log_i, log_f, C0, n0, m0):
    B, T, H, dk = q.shape
    L = A_CHUNK
    nc = T // L

    def chunks(a):
        a = a.reshape((B, nc, L, H) + a.shape[3:])
        return jnp.swapaxes(jnp.swapaxes(a, 0, 1), 2, 3)

    tri = jnp.tril(jnp.ones((L, L), dtype=bool))

    def step(carry, xs):
        C, n, m = carry
        qc, kc, vc, ic, fc = xs
        b = jnp.cumsum(fc, axis=-1)
        dmat = jnp.where(tri, b[..., :, None] - b[..., None, :] + ic[..., None, :], -jnp.inf)
        m_row = jnp.maximum(b + m[..., None], dmat.max(axis=-1))
        inter = jnp.exp(b + m[..., None] - m_row)
        s = jnp.einsum('bhjd,bhsd->bhjs', qc, kc) * jnp.exp(dmat - m_row[..., None])
        num = inter[..., None] * jnp.einsum('bhjd,bhdv->bhjv', qc, C) + jnp.einsum('bhjs,bhsv->bhjv', s, vc)
        den = inter * jnp.einsum('bhjd,bhd->bhj', qc, n) + s.sum(axis=-1)
        h = num / jnp.maximum(jnp.abs(den), jnp.exp(-m_row))[..., None]
        g = b[..., -1:] - b + ic
        m_new = jnp.maximum(b[..., -1] + m, g.max(axis=-1))
        decay = jnp.exp(b[..., -1] + m - m_new)
        w = jnp.exp(g - m_new[..., None])
        C_new = decay[..., None, None] * C + jnp.einsum('bhs,bhsd,bhsv->bhdv', w, kc, vc)
        n_new = decay[..., None] * n + jnp.einsum('bhs,bhsd->bhd', w, kc)
        return (C_new, n_new, m_new), h

    xs = (chunks(q), chunks(k), chunks(v), chunks(log_i), chunks(log_f))
    (Cf, nf, mf), hs = lax.scan(step, (C0, n0, m0), xs)
    hs = jnp.swapaxes(jnp.swapaxes(hs, 2, 3), 0, 1).reshape(B, T, H, v.shape[-1])
    return hs, (Cf, nf, mf)

def mlstm_prep(aq, ak, av, ag):
    B, T, _ = aq.shape
    q = aq.reshape(B, T, A_HEADS, A_DK).astype(F32)
    k = ak.reshape(B, T, A_HEADS, A_DK).astype(F32) * (A_DK ** -0.5)
    v = av.reshape(B, T, A_HEADS, A_DV).astype(F32)
    g = ag.reshape(B, T, 4, A_HEADS).astype(F32)
    gates = (g[:, :, 0], jax.nn.log_sigmoid(g[:, :, 1]), g[:, :, 2], jax.nn.log_sigmoid(g[:, :, 3]))
    return q, k, v, gates

def mlstm_bidirectional(q, k, v, gates, state_fwd, state_bwd):
    i_f, lf_f, i_b, lf_b = gates
    h_f, st_f = mlstm_chunkwise(q, k, v, i_f, lf_f, *state_fwd)
    rev = lambda a: jnp.flip(a, axis=1)
    h_b, st_b = mlstm_chunkwise(rev(q), rev(k), rev(v), rev(i_b), rev(lf_b), *state_bwd)
    return h_f + rev(h_b), st_f, st_b

def mlstm_output(h, o, gain):
    B, T = h.shape[:2]
    hn = rms_norm(h, gain.reshape(A_HEADS, A_DV)).reshape(B, T, A_WIDTH)
    return (hn * jax.nn.sigmoid(o.astype(F32))).astype(o.dtype)

def dense_gqa_attention(q, k, v, sink):
    B, T, G, R, d = q.shape
    nb = T // QB
    scale = d ** -0.5
    qb = jnp.swapaxes(q.reshape(B, nb, QB, G, R, d), 0, 1)
    sk = sink.reshape(G, R).astype(F32)

    def blk(qi):
        s = jnp.einsum('bqgrd,bkgd->bgrqk', qi, k).astype(F32) * scale
        s_sink = jnp.broadcast_to(sk[None, :, :, None, None], s.shape[:-1] + (1,))
        p = jax.nn.softmax(jnp.concatenate([s, s_sink], axis=-1), axis=-1)[..., :-1]
        return jnp.einsum('bgrqk,bkgd->bqgrd', p.astype(v.dtype), v)

    out = lax.map(blk, qb)
    return jnp.swapaxes(out, 0, 1).reshape(B, T, G * R * d)

def banded_gqa_attention(q, k, v, k_ctx, v_ctx, sink):
    B, T, G, R, d = q.shape
    nb = T // QB
    scale = d ** -0.5
    qb = q.reshape(B, nb, QB, G, R, d)

    def band(a):
        ap = jnp.pad(a, ((0, 0), (QB, QB), (0, 0), (0, 0))).reshape(B, nb + 2, QB, G, d)
        return jnp.concatenate([ap[:, :-2], ap[:, 1:-1], ap[:, 2:]], axis=2)

    kb, vb = band(k), band(v)
    qpos = jnp.arange(T).reshape(nb, QB)
    kpos = (jnp.arange(nb)[:, None] - 1) * QB + jnp.arange(3 * QB)[None, :]
    valid = ((jnp.abs(qpos[:, :, None] - kpos[:, None, :]) <= WINDOW)
             & (kpos >= 0)[:, None, :] & (kpos < T)[:, None, :])
    s_loc = jnp.einsum('bnqgrd,bnkgd->bngrqk', qb, kb).astype(F32) * scale
    s_loc = jnp.where(valid[None, :, None, None], s_loc, -jnp.inf)
    s_ctx = jnp.einsum('bnqgrd,bpgd->bngrqp', qb, k_ctx).astype(F32) * scale
    s_sink = jnp.broadcast_to(sink.reshape(G, R).astype(F32)[None, None, :, :, None, None], s_loc.shape[:-1] + (1,))
    p = jax.nn.softmax(jnp.concatenate([s_loc, s_ctx, s_sink], axis=-1), axis=-1)
    p_loc = p[..., :3 * QB].astype(v.dtype)
    p_ctx = p[..., 3 * QB:-1].astype(v.dtype)
    out = (jnp.einsum('bngrqk,bnkgd->bnqgrd', p_loc, vb)
           + jnp.einsum('bngrqp,bpgd->bnqgrd', p_ctx, v_ctx))
    return out.reshape(B, T, G * R * d)

def diff_lambda(lam_p, lam_init):
    lp = lam_p.astype(F32)
    return jnp.exp(jnp.sum(lp[0] * lp[1])) - jnp.exp(jnp.sum(lp[2] * lp[3])) + lam_init

def diff_attention(q, k, v, lam):
    B, T = q.shape[:2]
    nb = T // QB
    scale = q.shape[-1] ** -0.5
    qb = jnp.swapaxes(q.reshape((B, nb, QB) + q.shape[2:]), 0, 1)
    vf = v.astype(F32)

    def blk(qi):
        s = jnp.einsum('bqhcd,bkhcd->bhcqk', qi, k).astype(F32) * scale
        p = jax.nn.softmax(s, axis=-1)
        a = p[:, :, 0] - lam * p[:, :, 1]
        return jnp.einsum('bhqk,bkhv->bqhv', a, vf)

    out = lax.map(blk, qb)
    return jnp.swapaxes(out, 0, 1).reshape(B, T, q.shape[2], v.shape[-1])

def diff_output(o, gain, lam_init):
    B, T = o.shape[:2]
    return (rms_norm(o, gain) * (1.0 - lam_init)).reshape(B, T, C_WIDTH)

def peer_ffn(x, wq, subkeys, U, V):
    B, T, D = x.shape
    N = B * T
    xf = x.reshape(N, D)
    q = (xf @ wq).reshape(N, PEER_HEADS, 2, PEER_DQ // 2)
    s = jnp.einsum('nhcd,hckd->nhck', q, subkeys).astype(F32)
    s1, i1 = lax.top_k(s[:, :, 0], PEER_TOPK)
    s2, i2 = lax.top_k(s[:, :, 1], PEER_TOPK)
    cand = (s1[..., :, None] + s2[..., None, :]).reshape(N, PEER_HEADS, PEER_TOPK * PEER_TOPK)
    cidx = (i1[..., :, None] * N_KEYS + i2[..., None, :]).reshape(N, PEER_HEADS, PEER_TOPK * PEER_TOPK)
    top_s, pos = lax.top_k(cand, PEER_TOPK)
    eidx = jnp.take_along_axis(cidx, pos, axis=-1)
    g = jax.nn.softmax(top_s, axis=-1)
    nblk = N // QB
    eidx = eidx.reshape(nblk, QB, PEER_HEADS * PEER_TOPK)
    g = g.reshape(nblk, QB, PEER_HEADS * PEER_TOPK).astype(x.dtype)
    xb = xf.reshape(nblk, QB, D)

    def blk(args):
        xi, ei, gi = args
        act = jnp.einsum('tkd,td->tk', U[ei], xi)
        hw = jax.nn.gelu(act, approximate=False) * gi
        return jnp.einsum('tk,tkd->td', hw, V[ei])

    out = lax.map(blk, (xb, eidx, g))
    return out.reshape(B, T, D)

def mixer_inputs(h, p):
    B, T, _ = h.shape
    aq, ak, av, ao, ag, bq, bk, bv, cq, ck, cv = jnp.split(h @ p['w_in'] + p['b_in'], IN_SPLITS, axis=-1)
    mA = mlstm_prep(aq, ak, av, ag)
    qB = rms_norm(bq.reshape(B, T, B_QHEADS, B_HD), p['b_q_gain'])
    kB = rms_norm(bk.reshape(B, T, B_KVHEADS, B_HD), p['b_k_gain'])
    vB = bv.reshape(B, T, B_KVHEADS, B_HD)
    qC = rms_norm(cq.reshape(B, T, C_HEADS, 2, C_DH), p['c_q_gain'])
    kC = rms_norm(ck.reshape(B, T, C_HEADS, 2, C_DH), p['c_k_gain'])
    vC = cv.reshape(B, T, C_HEADS, C_DV)
    return mA, ao, (qB, kB, vB), (qC, kC, vC)

def layer_tail(x, outs, p, g_a, sh_f, sc_f, g_f):
    mix = jnp.concatenate(outs, axis=-1).astype(x.dtype) @ p['w_out']
    x = x + g_a * mix
    h = rms_norm(x, p['norm_gain'][1]) * (1.0 + sc_f) + sh_f
    return x + g_f * peer_ffn(h, p['peer_wq'], p['peer_subkeys'], p['peer_u'], p['peer_v'])

def context_layer(x, c_ctx, p, lam_init):
    B, T, _ = x.shape
    sh_a, sc_a, g_a, sh_f, sc_f, g_f = ada_modulation(c_ctx[None, :], p['w_ada'], p['b_ada'])
    h = rms_norm(x, p['norm_gain'][0]) * (1.0 + sc_a) + sh_a
    (qA, kA, vA, gates), oA, (qB, kB, vB), (qC, kC, vC) = mixer_inputs(h, p)
    zero = (jnp.zeros((B, A_HEADS, A_DK, A_DV), F32), jnp.zeros((B, A_HEADS, A_DK), F32),
            jnp.zeros((B, A_HEADS), F32))
    hA, st_f, st_b = mlstm_bidirectional(qA, kA, vA, gates, zero, zero)
    out_a = mlstm_output(hA, oA, p['a_out_gain'])
    out_b = dense_gqa_attention(qB.reshape(B, T, B_KVHEADS, B_GROUP, B_HD), kB, vB, p['b_sink'])
    lam = diff_lambda(p['c_lambda'], lam_init)
    out_c = diff_output(diff_attention(qC, kC, vC, lam), p['c_out_gain'], lam_init)
    x = layer_tail(x, (out_a, out_b, out_c), p, g_a, sh_f, sc_f, g_f)
    ctx = (kB, vB, kC.reshape(B, T, C_HEADS, 2 * C_DH), vC,
           jnp.stack([st_f[0], st_b[0]], axis=1), jnp.stack([st_f[1], st_b[1]], axis=1),
           jnp.stack([st_f[2], st_b[2]], axis=1))
    return x, ctx

def latent_layer(x, c, p, lam_init, cache, rope_b, rope_c):
    ck_b, cv_b, ck_c, cv_c, sC, sn, sm = cache
    B, T, _ = x.shape
    P = ck_b.shape[1]
    sh_a, sc_a, g_a, sh_f, sc_f, g_f = ada_modulation(c, p['w_ada'], p['b_ada'])
    h = rms_norm(x, p['norm_gain'][0]) * (1.0 + sc_a) + sh_a
    (qA, kA, vA, gates), oA, (qB, kB, vB), (qC, kC, vC) = mixer_inputs(h, p)
    st_f = (sC[:, 0].astype(F32), sn[:, 0].astype(F32), sm[:, 0].astype(F32))
    st_b = (sC[:, 1].astype(F32), sn[:, 1].astype(F32), sm[:, 1].astype(F32))
    hA, _, _ = mlstm_bidirectional(qA, kA, vA, gates, st_f, st_b)
    out_a = mlstm_output(hA, oA, p['a_out_gain'])
    qB = apply_axial_rope(qB, *rope_b)
    kB = apply_axial_rope(kB, *rope_b)
    out_b = banded_gqa_attention(qB.reshape(B, T, B_KVHEADS, B_GROUP, B_HD), kB, vB, ck_b, cv_b, p['b_sink'])
    qC = apply_axial_rope(qC, *rope_c)
    kC = apply_axial_rope(kC, *rope_c)
    k_all = jnp.concatenate([kC, ck_c.reshape(B, P, C_HEADS, 2, C_DH)], axis=1)
    v_all = jnp.concatenate([vC, cv_c], axis=1)
    lam = diff_lambda(p['c_lambda'], lam_init)
    out_c = diff_output(diff_attention(qC, k_all, v_all, lam), p['c_out_gain'], lam_init)
    return layer_tail(x, (out_a, out_b, out_c), p, g_a, sh_f, sc_f, g_f)

def setup_inputs(seed: int = 0) -> dict:
    key = jax.random.key(seed)
    ks = jax.random.split(key, 32)

    def nrm(k, shape, scale):
        return jax.random.normal(k, shape, F32) * scale

    D = D_MODEL
    forget_cols = np.concatenate([A_GATE_START + A_HEADS + np.arange(A_HEADS),
                                  A_GATE_START + 3 * A_HEADS + np.arange(A_HEADS)])
    b_in = nrm(ks[15], (DEPTH, IN_COLS), 0.02).at[:, forget_cols].add(FORGET_BIAS)
    return {
        'x_prompt': nrm(ks[0], (BATCH, SEQ, D), 1.0),
        'x_sample': nrm(ks[1], (DEC_BATCH, DEC_SEQ, D), 1.0),
        'cache_swa_k': nrm(ks[2], (DEC_BATCH, DEPTH, PAST_LEN, B_KVHEADS, B_HD), 1.0),
        'cache_swa_v': nrm(ks[3], (DEC_BATCH, DEPTH, PAST_LEN, B_KVHEADS, B_HD), 1.0),
        'cache_diff_k': nrm(ks[4], (DEC_BATCH, DEPTH, PAST_LEN, C_HEADS, 2 * C_DH), 1.0),
        'cache_diff_v': nrm(ks[5], (DEC_BATCH, DEPTH, PAST_LEN, C_HEADS, C_DV), 1.0),
        'state_mlstm_C': nrm(ks[6], (DEC_BATCH, DEPTH, 2, A_HEADS, A_DK, A_DV), 0.5),
        'state_mlstm_n': nrm(ks[7], (DEC_BATCH, DEPTH, 2, A_HEADS, A_DK), 0.5),
        'state_mlstm_m': nrm(ks[8], (DEC_BATCH, DEPTH, 2, A_HEADS), 1.0),
        'c': nrm(ks[9], (DEC_BATCH, D), 1.0),
        'c_ctx': nrm(ks[10], (D,), 1.0),
        'w_ada': nrm(ks[11], (DEPTH, D, 6 * D), 0.5 * D ** -0.5),
        'b_ada': nrm(ks[12], (DEPTH, 6 * D), 0.02),
        'norm_gain': 1.0 + nrm(ks[13], (DEPTH, 2, D), 0.02),
        'w_in': nrm(ks[14], (DEPTH, D, IN_COLS), D ** -0.5),
        'b_in': b_in,
        'a_out_gain': 1.0 + nrm(ks[16], (DEPTH, A_WIDTH), 0.02),
        'b_q_gain': 1.0 + nrm(ks[17], (DEPTH, B_HD), 0.02),
        'b_k_gain': 1.0 + nrm(ks[18], (DEPTH, B_HD), 0.02),
        'b_sink': nrm(ks[19], (DEPTH, B_QHEADS), 0.5),
        'c_q_gain': 1.0 + nrm(ks[20], (DEPTH, 2, C_DH), 0.02),
        'c_k_gain': 1.0 + nrm(ks[21], (DEPTH, 2, C_DH), 0.02),
        'c_lambda': nrm(ks[22], (DEPTH, 4, C_DH), 0.1),
        'c_out_gain': 1.0 + nrm(ks[23], (DEPTH, C_DV), 0.02),
        'w_out': nrm(ks[24], (DEPTH, MIX_WIDTH, D), MIX_WIDTH ** -0.5),
        'peer_wq': nrm(ks[25], (DEPTH, D, PEER_HEADS * PEER_DQ), D ** -0.5),
        'peer_subkeys': nrm(ks[26], (DEPTH, PEER_HEADS, 2, N_KEYS, PEER_DQ // 2), (PEER_DQ // 2) ** -0.5),
        'peer_u': nrm(ks[27], (DEPTH, N_EXPERTS, D), D ** -0.5),
        'peer_v': nrm(ks[28], (DEPTH, N_EXPERTS, D), 0.5),
    }

def reference(x_prompt, x_sample, cache_swa_k, cache_swa_v, cache_diff_k, cache_diff_v,
              state_mlstm_C, state_mlstm_n, state_mlstm_m, c, c_ctx, w_ada, b_ada, norm_gain,
              w_in, b_in, a_out_gain, b_q_gain, b_k_gain, b_sink, c_q_gain, c_k_gain, c_lambda,
              c_out_gain, w_out, peer_wq, peer_subkeys, peer_u, peer_v):
    rows = x_sample.shape[1] // GRID_W
    n_lat = rows * GRID_W
    rope_b = axial_rope_tables(n_lat, B_HD)
    rope_c = axial_rope_tables(n_lat, C_DH)
    yp, ys = x_prompt, x_sample
    ctx_layers = []
    for l in range(DEPTH):
        p = {'w_ada': w_ada[l], 'b_ada': b_ada[l], 'norm_gain': norm_gain[l], 'w_in': w_in[l],
             'b_in': b_in[l], 'a_out_gain': a_out_gain[l], 'b_q_gain': b_q_gain[l],
             'b_k_gain': b_k_gain[l], 'b_sink': b_sink[l], 'c_q_gain': c_q_gain[l],
             'c_k_gain': c_k_gain[l], 'c_lambda': c_lambda[l], 'c_out_gain': c_out_gain[l],
             'w_out': w_out[l], 'peer_wq': peer_wq[l], 'peer_subkeys': peer_subkeys[l],
             'peer_u': peer_u[l], 'peer_v': peer_v[l]}
        lam_init = 0.8 - 0.6 * math.exp(-0.3 * l)
        yp, ctx = context_layer(yp, c_ctx, p, lam_init)
        ctx_layers.append(ctx)
        cache_l = (cache_swa_k[:, l], cache_swa_v[:, l], cache_diff_k[:, l], cache_diff_v[:, l],
                   state_mlstm_C[:, l], state_mlstm_n[:, l], state_mlstm_m[:, l])
        ys = latent_layer(ys, c, p, lam_init, cache_l, rope_b, rope_c)
    stack = lambda j: jnp.stack([ctx[j] for ctx in ctx_layers], axis=1)
    new_swa_k, new_swa_v = stack(0), stack(1)
    new_diff_k, new_diff_v = stack(2), stack(3)
    new_C, new_n, new_m = stack(4), stack(5), stack(6)
    return (yp, ys, new_swa_k, new_swa_v, new_diff_k, new_diff_v, new_C, new_n, new_m)


_drawn_inputs = setup_inputs


def setup_inputs(seed=0):
    import zlib

    import numpy as np

    out = dict(_drawn_inputs(seed))
    spreads = {}
    factors = {'cache_swa_k': 3.112,
     'state_mlstm_C': 4.006,
     'state_mlstm_n': 7.943,
     'state_mlstm_m': 6.158,
     'a_out_gain': 8.0,
     'b_q_gain': 8.0,
     'b_k_gain': 2.984,
     'b_sink': 64.0,
     'c_q_gain': 8.0,
     'c_k_gain': 2.779,
     'c_lambda': 8.0,
     'c_out_gain': 6.736,
     'cache_diff_k': 8.0,
     'cache_diff_v': 8.0}
    for name, (base, spread) in spreads.items():
        noise = np.random.default_rng([zlib.crc32(name.encode()), seed]).standard_normal(out[name].shape)
        drawn = base * np.exp(spread * noise) if base else spread * noise
        out[name] = __import__('jax').numpy.asarray(drawn.astype(out[name].dtype))
    for name, factor in factors.items():
        out[name] = (out[name] * factor).astype(out[name].dtype)
    return out
```

```python
import math
from contextlib import ExitStack

import concourse.bass as bass
from concourse import mybir

F32 = mybir.dt.float32
BF16 = mybir.dt.bfloat16
U32 = mybir.dt.uint32
ALU = mybir.AluOpType
ACT = mybir.ActivationFunctionType
AX_X = mybir.AxisListType.X

P = 128
D = 1024
KD = D // P
SEQ, DEC_SEQ, PAST = 128, 512, 128
NT = (SEQ + DEC_SEQ) // P
N = NT * P
DEPTH = 2
EPS = 1e-6
NEG = -1e30
BIG = 3e38

AQ, AK, AV, AO, AG = 0, 256, 512, 768, 1024
BQ, BK, BV = 1040, 1552, 1680
CQ, CK, CV = 1808, 2064, 2320
IN_COLS = 2576
IN_SLICES = 7
IN_W = IN_COLS // IN_SLICES
B_GROUPS, C_GROUPS = 10, 16

MA, MB, MC = 0, 256, 768

ADA_SLICES = 6 * D // 512

C_ID, C_TRIF, C_TRIB, C_ONE, C_MF, C_MB = 0, 128, 256, 384, 512, 640
C_BAND, C_BAND1 = 768, 1280
C_IOTA = 1664
C_RB, C_RC = 1792, 2048
C_SEL = 2176
C_EPS = 2432
N_CONST = 2433

R_BIN, R_GB, R_GC, R_GA, R_GO, R_SINK, R_LAM = 0, 2576, 3216, 3728, 3984, 4240, 4248
N_ROWS = 4376

NK = 128
HEADS, TOPK = 8, 16
HC = 2 * HEADS
HALF = N // 2
GT = 64
U_SLOTS, V_SLOTS = 4, 8
BLOCKS = 8

A_P, A_WR, A_MIX = 0, 12880, 25168
ARENA = 30288
WSLOT = 4096


class Tally:

    def __init__(self, sem, n=0):
        self.sem, self.n, self.terms, self.start = sem, n, [], []

    def at(self, k=0):
        value = self.n + k
        for reg, per in self.terms:
            value = reg * per + value
        return value

    def enter(self, reg, per):
        self.terms.append((reg, per))
        self.start.append(self.n)

    def leave(self, turns):
        _, per = self.terms.pop()
        began = self.start.pop()
        assert self.n - began == per, (self.n - began, per)
        self.n = began + turns * per

    def next(self, eng):
        self.n += 1
        eng.wait_ge(self.sem, self.at())


class BankWriter:

    def __init__(self, banks, filled, drained):
        self.banks, self.filled, self.drained = banks, Tally(filled), drained

    def open(self, pe):
        n = self.filled.n
        if n >= 4 or self.filled.terms:
            pe.wait_ge(self.drained, self.filled.at(-3))
        return self.banks[n % 4]

    def close(self, ins):
        ins.then_inc(self.filled.sem, 1)
        self.filled.n += 1

    def landed(self, pe):
        pe.wait_ge(self.drained, self.filled.at())


class BankReader:

    def __init__(self, banks, filled, drained):
        self.banks, self.filled, self.drained = banks, Tally(filled), drained

    def take(self, eng):
        bank = self.banks[self.filled.n % 4]
        self.filled.next(eng)
        return bank

    def give(self, ins):
        ins.then_inc(self.drained, 1)


def cond_of(t):
    return 0 if t == 0 else 1


def b_units():
    return [(t, g, pp) for t in range(NT) for g in range(2) for pp in range(2)]


def b_local(t):
    return [0] if t == 0 else [s for s in (t - 1, t, t + 1) if 1 <= s < NT]


def b_keys(t):
    return P if t == 0 else P * (1 + len(b_local(t)))


def c_units():
    return [(t, h) for t in range(NT) for h in range(4)]


def c_keys(t):
    return P if t == 0 else DEC_SEQ + PAST


def a_units():
    out = [(0, 0, 0), (0, 1, 0)]
    for s in range(NT - 1):
        out += [(1, 0, 1 + s), (1, 1, NT - 1 - s)]
    return out


def lam_init(layer):
    return 0.8 - 0.6 * math.exp(-0.3 * layer)


def hybrid_step(nc, io):
    with ExitStack() as ctx:
        def sb(name, shape, dt=F32):
            return ctx.enter_context(nc.sbuf_tensor(name, shape, dt))

        def sem(name):
            return ctx.enter_context(nc.semaphore(name))

        X = sb("X", [P, NT, D])
        HT = sb("HT", [P, KD * N])
        GB = sb("GB", [P, 2, 2, D])
        CON = sb("CON", [P, N_CONST])
        ROWS = sb("ROWS", [P, N_ROWS])
        AR = sb("AR", [P, ARENA])
        SM = sb("SM", [P, 1400])
        vbank = [ctx.enter_context(nc.psum_tensor(f"vbank{i}", [P, 512], F32)) for i in range(4)]
        sbank = [ctx.enter_context(nc.psum_tensor(f"sbank{i}", [P, 512], F32)) for i in range(4)]

        small_at = [0]

        def small(n, dt=F32):
            a = small_at[0]
            small_at[0] += n
            assert small_at[0] <= 1400
            return SM[:, a:a + n]

        cond = small(16).rearrange("p (k c) -> p k c", c=2)
        conds = small(16).rearrange("p (k c) -> p k c", c=2)
        ngain = small(16).rearrange("p (w k) -> p w k", w=2)
        mod = small(64).rearrange("p (v k c) -> p v k c", v=4, c=2)
        ssq, root, rinv = small(NT), small(NT), small(NT)
        gss, groot, grinv = (small(NT * 26).rearrange("p (t g) -> p t g", t=NT) for _ in range(3))
        hss, hroot, hrinv = (small(NT * 8).rearrange("p (t g) -> p t g", t=NT) for _ in range(3))
        bmax, bsum, brec = (small(4).rearrange("p (s i) -> p s i", s=2) for _ in range(3))
        cmax, csum, crec = (small(4).rearrange("p (s i) -> p s i", s=2) for _ in range(3))
        lamw = small(64)
        lamv = small(4)
        lf = small(40)
        lft = small(40)
        bci = small(80)
        ci = small(40)
        mstate = small(16).rearrange("p (s d h) -> p s d h", s=2, d=2)
        args = small(40).rearrange("p (s k h) -> p s k h", s=2, k=5)
        mtmp = small(40).rearrange("p (s k h) -> p s k h", s=2, k=5)
        den = small(8).rearrange("p (k h) -> p k h", k=2)

        ident = CON[:, C_ID:C_ID + P]
        ones = CON[:, C_ONE:C_ONE + P]
        eps = CON[:, C_EPS:C_EPS + 1]
        iota = CON[:, C_IOTA:C_IOTA + NK]

        wslot = [AR[:, A_WR + i * WSLOT:A_WR + (i + 1) * WSLOT] for i in range(3)]
        PR = AR[:, A_P:A_P + NT * IN_COLS].rearrange("p (t c) -> p t c", t=NT)
        ada = AR[0:2, A_P:A_P + 6 * D]
        bada = AR[0:2, A_P + 6 * D:A_P + 12 * D]
        MIX = AR[:, A_MIX:A_MIX + NT * D].rearrange("p (t c) -> p t c", t=NT)
        HTk = HT[:, :].rearrange("p (k n) -> p k n", k=KD)
        QKT = AR[:, A_WR:A_WR + 13 * N].rearrange("p (b n) -> p b n", b=13)
        W0 = A_WR + 13 * N
        kcb = HT[:, 0:128]
        kcc = HT[:, 128:384].rearrange("p (b n) -> p b n", b=2)
        vcb = HT[:, 384:512]
        vcc = HT[:, 512:768]
        H0 = 768
        SQ = AR[:, W0:W0 + 1152]
        hsq = HT[:, H0:H0 + 512]
        b_s = HT[:, H0:H0 + 2080].rearrange("p (s i n) -> p s i n", s=2, i=2)
        b_et = HT[:, H0 + 2080:H0 + 2080 + 2048].rearrange("p (s i n) -> p s i n", s=2, i=2)
        c_s = HT[:, H0:H0 + 2560].rearrange("p (s i n) -> p s i n", s=2, i=2)
        c_at = HT[:, H0 + 2560:H0 + 2560 + 1280].rearrange("p (s n) -> p s n", s=2)

        def work(a, n):
            return AR[:, W0 + a:W0 + a + n]
        vaug = work(0, 1300).rearrange("p (t h c) -> p t h c", t=NT, h=4)
        cst = work(1300, 520).rearrange("p (s d j c) -> p s d j c", s=2, d=2, j=2)
        nd = work(1820, 260).rearrange("p (h c) -> p h c", h=4)
        wk = work(2080, 256)
        htmp = work(2336, 256).rearrange("p (h c) -> p h c", h=4)
        dg = work(2592, 512).rearrange("p (h s) -> p h s", h=4)
        cm = HT[:, H0:H0 + 512].rearrange("p (h s) -> p h s", h=4)
        pm = HT[:, H0 + 512:H0 + 1024].rearrange("p (h s) -> p h s", h=4)
        pt = HT[:, H0 + 1024:H0 + 1536].rearrange("p (h s) -> p h s", h=4)
        xtmp = AR[:, A_P:A_P + 1024].rearrange("p (s n) -> p s n", s=2)
        SC = AR[:, A_P:A_P + NT * HC * NK].rearrange("p (t c k) -> p t c k", t=NT, c=HC)
        QT = AR[:, A_P + 10240:A_P + 10240 + 2 * N].rearrange("p (s n) -> p s n", s=2)
        SUBT = ROWS[:, 0:2048].rearrange("p (c k) -> p c k", c=HC)
        val = AR[:, A_MIX:A_MIX + 256].rearrange("p (c k) -> p c k", c=HC)
        idx = AR[:, A_MIX + 256:A_MIX + 512].bitcast(U32).rearrange("p (c k) -> p c k", c=HC)
        cand = AR[:, A_MIX + 512:A_MIX + 2560].rearrange("p (h a b) -> p h a b", h=HEADS, a=TOPK)
        eq = AR[:, A_MIX + 2560:A_MIX + 4608]
        o = 2048
        idxf = ROWS[:, o:o + 256].rearrange("p (h c k) -> p h c k", h=HEADS, c=2)
        tops = ROWS[:, o + 256:o + 384].rearrange("p (h k) -> p h k", h=HEADS)
        posu = ROWS[:, o + 384:o + 512].bitcast(U32).rearrange("p (h k) -> p h k", h=HEADS)
        pab = [ROWS[:, o + 512:o + 640].bitcast(U32), ROWS[:, o + 640:o + 768].bitcast(U32)]
        pabf = [ROWS[:, o + 768:o + 896], ROWS[:, o + 896:o + 1024]]
        sel = [ROWS[:, o + 1024:o + 1152], ROWS[:, o + 1152:o + 1280]]
        gate = ROWS[:, o + 1280:o + 1408].rearrange("p (h k) -> p h k", h=HEADS)
        gsum = ROWS[:, o + 1408:o + 1416]
        grec = ROWS[:, o + 1416:o + 1424]
        pflat = ROWS[:, o + 384:o + 512].bitcast(U32)
        gbf = ROWS[:, o + 1424:o + 1488].bitcast(BF16)
        IGT = [AR[:, A_WR + i * N:A_WR + (i + 1) * N] for i in range(5)]
        OH = AR[:, 16080:16080 + 4096].bitcast(BF16).rearrange("p (s t k n) -> p s t k n", s=4, t=4, k=4)
        GS = [AR[:, a:a + NK * GT].rearrange("p (b t) -> p b t", b=NK) for a in (0, 20176)]
        UR = [AR[:, i * 1024:(i + 1) * 1024].rearrange("p (k e) -> p k e", k=KD) for i in range(U_SLOTS)]
        GR = [AR[:, 4096 + i * N:4096 + (i + 1) * N] for i in range(U_SLOTS)]
        VR = [AR[:, 6656 + i * 1024:6656 + (i + 1) * 1024] for i in range(V_SLOTS)]
        ACC = AR[:, 14848:14848 + 5120].rearrange("p (t c) -> p t c", t=NT)
        HW = AR[:, 19968:19968 + BLOCKS * N].rearrange("p (b n) -> p b n", b=BLOCKS)
        GE = AR[:, 25088:25088 + 2 * N].rearrange("p (s n) -> p s n", s=2)

        vec_filled, vec_drained = sem("vec_filled"), sem("vec_drained")
        sca_filled, sca_drained = sem("sca_filled"), sem("sca_drained")
        phase_done = sem("phase_done")
        setup_in = sem("setup_in")
        vectors_in = sem("vectors_in")
        slice_in = [sem(f"slice_in{i}") for i in range(3)]
        cond_ready = sem("cond_ready")
        ada_rows = sem("ada_rows")
        mod_ready = sem("mod_ready")
        x_ready = sem("x_ready")
        roots_ready = sem("roots_ready")
        xn_ready = sem("xn_ready")
        group_squares = sem("group_squares")
        group_roots = sem("group_roots")
        qk_ready = sem("qk_ready")
        caches_in = sem("caches_in")
        b_scores = sem("b_scores")
        b_exps = sem("b_exps")
        c_scores = sem("c_scores")
        c_exps = sem("c_exps")
        c_weights = sem("c_weights")
        gates_signed = sem("gates_signed")
        softplus_ready = sem("softplus_ready")
        log_f_ready = sem("log_f_ready")
        diag_ready = sem("diag_ready")
        ml_args = sem("ml_args")
        ml_exps = sem("ml_exps")
        ml_products = sem("ml_products")
        state_final = sem("state_final")
        head_squares = sem("head_squares")
        head_roots = sem("head_roots")
        lam_dots = sem("lam_dots")
        lam_exps = sem("lam_exps")
        mix_ready = sem("mix_ready")
        subkeys_in = sem("subkeys_in")
        tops_ready = sem("tops_ready")
        top_exps = sem("top_exps")
        picks_ready = sem("picks_ready")
        onehot_ready = sem("onehot_ready")
        gates_built = sem("gates_built")
        gates_stored = [sem(f"gates_stored{i}") for i in range(2)]
        u_in = [sem(f"u_in{i}") for i in range(U_SLOTS)]
        v_in = [sem(f"v_in{i}") for i in range(V_SLOTS)]
        hidden_ready = sem("hidden_ready")
        x_final = sem("x_final")
        out_done = sem("out_done")

        slice_read = []
        loop_base = {}

        block = ctx.enter_context(nc.Block())

        @block.tensor
        def _(pe):
            V = BankWriter(vbank, vec_filled, vec_drained)
            S = BankWriter(sbank, sca_filled, sca_drained)
            slices = [0, 0, 0]
            n_slice = [0]
            phase = [0]

            def barrier():
                phase[0] += 1
                pe.drain().then_inc(phase_done, 1)
                pe.wait_ge(phase_done, 3 * phase[0])

            def next_slice():
                i = n_slice[0] % 3
                n_slice[0] += 1
                slices[i] += 16
                pe.wait_ge(slice_in[i], slices[i])
                return wslot[i]

            def slice_done(w):
                slice_read.append((w.filled.sem, w.filled.n))

            def transposed_norm():
                for t in range(NT):
                    xn_t.next(pe)
                    for half in range(2):
                        ps = S.open(pe)
                        for j in range(4):
                            k = 4 * half + j
                            ins = pe.transpose(ps[:, j * P:(j + 1) * P], MIX[:, t, k * P:(k + 1) * P], ident)
                        S.close(ins)

            xn_t, qk_t, be_t, cw_t = Tally(xn_ready), Tally(qk_ready), Tally(b_exps), Tally(c_weights)
            ada_t, lf_t, dg_t, mp_t = Tally(ada_rows), Tally(log_f_ready), Tally(diag_ready), Tally(ml_products)
            mix_t, pk_t, oh_t, hid_t = Tally(mix_ready), Tally(picks_ready), Tally(onehot_ready), Tally(hidden_ready, 8)
            u_t = [Tally(s) for s in u_in]
            v_t = [Tally(s) for s in v_in]
            pe.wait_ge(setup_in, 16 * 4)
            pe.wait_ge(cond_ready, 1)

            for layer in range(DEPTH):
                for n in range(ADA_SLICES):
                    w = next_slice().rearrange("p (k n) -> p k n", k=KD)
                    ps = V.open(pe)
                    for k in range(KD):
                        ins = pe.matmul(ps[0:2, :], conds[:, k, :], w[:, k, :], start=(k == 0), stop=(k == KD - 1))
                    V.close(ins)
                    slice_done(V)
                ada_t.next(pe)
                ps = V.open(pe)
                for v, vec in enumerate((0, 1, 3, 4)):
                    for k in range(KD):
                        a = vec * D + k * P
                        ins = pe.transpose(ps[:, (v * KD + k) * 2:(v * KD + k) * 2 + 2], ada[:, a:a + P], ident[0:2, 0:2])
                V.close(ins)
                for vec in (2, 5):
                    for c in range(2):
                        for half in range(2):
                            ps = S.open(pe)
                            a = vec * D + half * 512
                            S.close(pe.matmul(ps[:, :], CON[0:2, C_SEL + c * P:C_SEL + (c + 1) * P], ada[:, a:a + 512],
                                              start=True, stop=True))
                transposed_norm()
                S.landed(pe)
                for n in range(IN_SLICES):
                    w = next_slice()[:, 0:KD * IN_W].rearrange("p (k n) -> p k n", k=KD)
                    for t in range(NT):
                        ps = V.open(pe)
                        for k in range(KD):
                            ins = pe.matmul(ps[:, 0:IN_W], HTk[:, k, t * P:(t + 1) * P], w[:, k, :],
                                            start=(k == 0), stop=(k == KD - 1))
                        V.close(ins)
                    slice_done(V)
                barrier()

                cols = [BQ + P * i for i in range(4)] + [BK, CQ, CQ + P, CK, CK + P, AQ, AQ + P, AK, AK + P]
                for t in range(NT):
                    qk_t.next(pe)
                    for b0 in range(0, 13, 4):
                        ps = S.open(pe)
                        for b in range(b0, min(b0 + 4, 13)):
                            ins = pe.transpose(ps[:, (b - b0) * P:(b - b0 + 1) * P], PR[:, t, cols[b]:cols[b] + P], ident)
                        S.close(ins)
                S.landed(pe)
                pe.wait_ge(caches_in, 96 * (layer + 1))

                units = b_units()

                def scores(u):
                    t, g, pp = units[u]
                    r = slice(64 * g, 64 * g + 64)
                    for i in range(2):
                        ps = V.open(pe)
                        q = QKT[r, 2 * pp + i, t * P:(t + 1) * P]
                        if t == 0:
                            ins = pe.matmul(ps[:, 0:P], q, QKT[r, 4, 0:P], start=True, stop=True)
                        else:
                            loc = b_local(t)
                            pe.matmul(ps[:, 0:P], q, kcb[r, :], start=True, stop=True)
                            ins = pe.matmul(ps[:, P:P + P * len(loc)], q, QKT[r, 4, loc[0] * P:(loc[-1] + 1) * P],
                                            start=True, stop=True)
                        V.close(ins)

                def mixed(u):
                    t, g, pp = units[u]
                    nb = b_keys(t) // P
                    be_t.next(pe)
                    for i in range(2):
                        ps = S.open(pe)
                        for b in range(nb):
                            ins = pe.transpose(ps[:, b * P:(b + 1) * P], b_s[:, u % 2, i, b * P:(b + 1) * P], ident)
                        S.close(ins)
                    S.landed(pe)
                    ps = V.open(pe)
                    for i in range(2):
                        for b in range(nb):
                            if t == 0:
                                v = PR[:, 0, BV + 64 * g:BV + 64 * g + 64]
                            elif b == 0:
                                v = vcb[:, 64 * g:64 * g + 64]
                            else:
                                v = PR[:, b_local(t)[b - 1], BV + 64 * g:BV + 64 * g + 64]
                            ins = pe.matmul(ps[:, 64 * i:64 * i + 64], b_et[:, u % 2, i, b * P:(b + 1) * P], v,
                                            start=(b == 0), stop=(b == nb - 1))
                    V.close(ins)

                scores(0)
                for u in range(len(units)):
                    if u + 1 < len(units):
                        scores(u + 1)
                    mixed(u)
                barrier()

                cu = c_units()

                def c_score(u):
                    t, h = cu[u]

                    def qk(c):
                        g = 2 * h + c
                        r = slice(32 * (g % 4), 32 * (g % 4) + 32)
                        return r, QKT[r, 5 + g // 4, t * P:(t + 1) * P], 7 + g // 4, g // 4
                    if t == 0:
                        for c in range(2):
                            ps = V.open(pe)
                            r, q, kb, _ = qk(c)
                            V.close(pe.matmul(ps[:, 0:P], q, QKT[r, kb, 0:P], start=True, stop=True))
                        return
                    for c in range(2):
                        ps = V.open(pe)
                        r, q, kb, _ = qk(c)
                        V.close(pe.matmul(ps[:, :], q, QKT[r, kb, P:N], start=True, stop=True))
                    for c in range(2):
                        ps = V.open(pe)
                        r, q, _, kc = qk(c)
                        V.close(pe.matmul(ps[:, 0:P], q, kcc[r, kc, :], start=True, stop=True))

                def c_mixed(u):
                    t, h = cu[u]
                    nb = c_keys(t) // P
                    cw_t.next(pe)
                    for b0 in range(0, nb, 4):
                        ps = S.open(pe)
                        for b in range(b0, min(b0 + 4, nb)):
                            ins = pe.transpose(ps[:, (b - b0) * P:(b - b0 + 1) * P],
                                               c_s[:, u % 2, 0, b * P:(b + 1) * P], ident)
                        S.close(ins)
                    S.landed(pe)
                    ps = V.open(pe)
                    for b in range(nb):
                        if b == 4:
                            v = vcc[:, 64 * h:64 * h + 64]
                        else:
                            v = PR[:, 0 if t == 0 else 1 + b, CV + 64 * h:CV + 64 * h + 64]
                        ins = pe.matmul(ps[:, 0:64], c_at[:, u % 2, b * P:(b + 1) * P], v,
                                        start=(b == 0), stop=(b == nb - 1))
                    V.close(ins)

                c_score(0)
                for u in range(len(cu)):
                    if u + 1 < len(cu):
                        c_score(u + 1)
                    c_mixed(u)
                barrier()

                lf_t.next(pe)
                ps = V.open(pe)
                pe.matmul(ps[:, 0:20], CON[:, C_TRIF:C_TRIF + P], lf[:, 0:20], start=True, stop=True)
                pe.matmul(ps[:, 20:40], CON[:, C_TRIB:C_TRIB + P], lf[:, 20:40], start=True, stop=True)
                V.close(pe.matmul(ps[:, 40:80], ones, lf[:, :], start=True, stop=True))
                for seg, d, t in a_units():
                    dg_t.next(pe)
                    ps = V.open(pe)
                    V.close(pe.matmul(ps[:, :], ones, dg[:, :, :].rearrange("p h s -> p (h s)"), start=True, stop=True))
                    for odd in range(2):
                        ps = V.open(pe)
                        r = slice(64 * odd, 64 * odd + 64)
                        for j in range(2):
                            ins = pe.matmul(ps[:, j * P:(j + 1) * P], QKT[r, 9 + j, t * P:(t + 1) * P],
                                            QKT[r, 11 + j, t * P:(t + 1) * P], start=True, stop=True)
                        V.close(ins)
                    mp_t.next(pe)
                    ps = S.open(pe)
                    for h in range(4):
                        ins = pe.transpose(ps[:, h * P:(h + 1) * P], pm[:, h, :], ident)
                    S.close(ins)
                    for odd in range(2):
                        ps = V.open(pe)
                        r = slice(64 * odd, 64 * odd + 64)
                        for j in range(2):
                            ins = pe.matmul(ps[:, j * 65:(j + 1) * 65], QKT[r, 9 + j, t * P:(t + 1) * P],
                                            cst[r, seg, d, j, :], start=True, stop=True)
                        V.close(ins)
                    ps = V.open(pe)
                    for j in range(2):
                        ins = pe.matmul(ps[:, j * 130:(j + 1) * 130], wk[:, j * P:(j + 1) * P],
                                        vaug[:, t, 2 * j:2 * j + 2, :].rearrange("p h c -> p (h c)"),
                                        start=True, stop=True)
                    V.close(ins)
                    S.landed(pe)
                    ps = V.open(pe)
                    for h in range(4):
                        ins = pe.matmul(ps[:, h * 65:(h + 1) * 65], pt[:, h, :], vaug[:, t, h, :], start=True, stop=True)
                    V.close(ins)
                barrier()

                for t in range(NT):
                    if t == 0:
                        mix_t.next(pe)
                    for half in range(2):
                        ps = S.open(pe)
                        for j in range(4):
                            k = 4 * half + j
                            ins = pe.transpose(ps[:, j * P:(j + 1) * P], MIX[:, t, k * P:(k + 1) * P], ident)
                        S.close(ins)
                S.landed(pe)
                for n in range(2):
                    w = next_slice().rearrange("p (k n) -> p k n", k=KD)
                    for t in range(NT):
                        ps = V.open(pe)
                        for k in range(KD):
                            ins = pe.matmul(ps[:, :], HTk[:, k, t * P:(t + 1) * P], w[:, k, :],
                                            start=(k == 0), stop=(k == KD - 1))
                        V.close(ins)
                    slice_done(V)
                transposed_norm()
                S.landed(pe)

                pe.wait_ge(subkeys_in, 16 * (layer + 1))
                w = None

                def query(c, w):
                    for j in range(2):
                        ps = S.open(pe)
                        for k in range(KD):
                            ins = pe.matmul(ps[:, 0:HALF], w[:, c % 4, k, :], HTk[:, k, j * HALF:(j + 1) * HALF],
                                            start=(k == 0), stop=(k == KD - 1))
                        S.close(ins)
                    return S.filled.n

                def key_scores(c, after):
                    pe.wait_ge(sca_drained, after)
                    for t0 in (0, 4):
                        ps = S.open(pe)
                        for t in range(t0, min(t0 + 4, NT)):
                            ins = pe.matmul(ps[:, (t - t0) * P:(t - t0 + 1) * P], QT[:, c % 2, t * P:(t + 1) * P],
                                            SUBT[:, c, :], start=True, stop=True)
                        S.close(ins)

                after = 0
                for c in range(HC + 1):
                    was = after
                    if c < HC:
                        if c % 4 == 0:
                            w = next_slice().rearrange("p (c k n) -> p c k n", c=4, k=KD)
                        after = query(c, w)
                        if c % 4 == 3:
                            slice_done(S)
                    if c >= 1:
                        key_scores(c - 1, was)
                barrier()

                for t in range(NT):
                    pk_t.next(pe)
                    ps = V.open(pe)
                    pe.transpose(ps[:, 0:P], sel[0], ident)
                    pe.transpose(ps[:, P:2 * P], sel[1], ident)
                    V.close(pe.transpose(ps[:, 2 * P:3 * P], gate[:, :, :].rearrange("p h k -> p (h k)"), ident))
                barrier()

                loop_base["gate", layer] = S.filled.n
                with pe.Fori(0, N // (2 * GT)) as i:
                    S.filled.enter(i, 32)
                    oh_t.enter(i, 32)
                    for slot in range(2):
                        with pe.Fori(0, GT // 16) as j:
                            S.filled.enter(j, 4)
                            oh_t.enter(j, 4)
                            for b in range(4):
                                oh_t.next(pe)
                                ps = S.open(pe)
                                for q in range(4):
                                    for part in range(3):
                                        ins = pe.matmul(ps[:, q * P:(q + 1) * P], OH[:, b, q, 3, :], OH[:, b, q, part, :],
                                                        start=(part == 0), stop=(part == 2))
                                S.close(ins)
                            S.filled.leave(GT // 16)
                            oh_t.leave(GT // 16)
                    S.filled.leave(N // (2 * GT))
                    oh_t.leave(N // (2 * GT))
                barrier()

                loop_base["s", layer], loop_base["v", layer] = S.filled.n, V.filled.n
                steps = NK // BLOCKS
                with pe.Fori(0, steps) as i:
                    S.filled.enter(i, 2 * BLOCKS)
                    V.filled.enter(i, 4 * NT)
                    hid_t.enter(i, BLOCKS)
                    for x in u_t:
                        x.enter(i, 32 * BLOCKS // U_SLOTS)
                    for x in v_t:
                        x.enter(i, 16)
                    for b in range(BLOCKS):
                        slot = b % U_SLOTS
                        u_t[slot].n += 32
                        pe.wait_ge(u_in[slot], u_t[slot].at())
                        for j in range(2):
                            ps = S.open(pe)
                            for k in range(KD):
                                ins = pe.matmul(ps[:, 0:HALF], UR[slot][:, k, :], HTk[:, k, j * HALF:(j + 1) * HALF],
                                                start=(k == 0), stop=(k == KD - 1))
                            S.close(ins)
                    for half in range(2):
                        for b in range(4 * half, 4 * half + 4):
                            v_t[b].n += 16
                            pe.wait_ge(v_in[b], v_t[b].at())
                            hid_t.next(pe)
                        for t in range(NT):
                            for ch in range(2):
                                ps = V.open(pe)
                                for b in range(4 * half, 4 * half + 4):
                                    ins = pe.matmul(ps[:, :], HW[:, b, t * P:(t + 1) * P], VR[b][:, ch * 512:(ch + 1) * 512],
                                                    start=(b % 4 == 0), stop=(b % 4 == 3))
                                V.close(ins)
                    S.filled.leave(steps)
                    V.filled.leave(steps)
                    hid_t.leave(steps)
                    for x in u_t + v_t:
                        x.leave(steps)
                barrier()

        @block.vector
        def _(v):
            V = BankReader(vbank, vec_filled, vec_drained)
            phase = [0]
            rt_t, gr_t, sp_t, le_t = Tally(roots_ready), Tally(group_roots), Tally(softplus_ready), Tally(lam_exps)
            ce_t, be_t, me_t, hr_t = Tally(c_exps), Tally(b_exps), Tally(ml_exps), Tally(head_roots)
            te_t, ge_t = Tally(top_exps), Tally(sca_drained)
            u_t = [Tally(s) for s in u_in]
            hid = Tally(hidden_ready, 8)

            def barrier():
                phase[0] += 1
                v.drain().then_inc(phase_done, 1)
                v.wait_ge(phase_done, 3 * phase[0])

            def tt(out, a, b, op):
                return v.tensor_tensor(out, a, b, op)

            def normed():
                rt_t.next(v)
                v.reciprocal(rinv[:, :], root[:, :])
                v.drain()
                for t in range(NT):
                    v.tensor_scalar(MIX[:, t, :], X[:, t, :], rinv[:, t:t + 1], None, ALU.mult).then_inc(xn_ready, 1)

            v.memset(den[:, :, :], 0.0).then_inc(hidden_ready, 8)
            v.wait_ge(setup_in, 16 * 4)

            for layer in range(DEPTH):
                v.wait_ge(vectors_in, 48 * (layer + 1))
                for n in range(ADA_SLICES):
                    ps = V.take(v)
                    V.give(tt(ada[:, n * 512:(n + 1) * 512], ps[0:2, :], bada[:, n * 512:(n + 1) * 512], ALU.add))
                v.drain().then_inc(ada_rows, 1)
                ps = V.take(v)
                for w in range(2):
                    cols = ps[:, w * 32:(w + 1) * 32].rearrange("p (v k c) -> p v k c", v=2, c=2)
                    v.tensor_copy(mod[:, 2 * w, :, :], cols[:, 0])
                    ins = v.scalar_tensor_tensor(mod[:, 2 * w + 1, :, :], cols[:, 1], 1.0,
                                                 ngain[:, w, :].unsqueeze(2).broadcast_to([P, KD, 2]), ALU.add, ALU.mult)
                V.give(ins)
                v.drain().then_inc(mod_ready, 1)
                normed()
                for n in range(IN_SLICES):
                    for t in range(NT):
                        ps = V.take(v)
                        V.give(tt(PR[:, t, n * IN_W:(n + 1) * IN_W], ps[:, 0:IN_W],
                                  ROWS[:, R_BIN + n * IN_W:R_BIN + (n + 1) * IN_W], ALU.add))
                barrier()

                for t in range(NT):
                    tt(SQ[:, 0:640], PR[:, t, BQ:BQ + 640], PR[:, t, BQ:BQ + 640], ALU.mult)
                    tt(SQ[:, 640:1152], PR[:, t, CQ:CQ + 512], PR[:, t, CQ:CQ + 512], ALU.mult)
                    v.drain()
                    v.tensor_reduce(gss[:, t, 0:10], SQ[:, 0:640].rearrange("p (g c) -> p g c", c=64), AX_X, ALU.add)
                    v.tensor_reduce(gss[:, t, 10:26], SQ[:, 640:1152].rearrange("p (g c) -> p g c", c=32), AX_X, ALU.add)
                    v.drain()
                v.drain().then_inc(group_squares, 1)
                lam = ROWS[:, R_LAM:R_LAM + 128].rearrange("p (a b c) -> p a b c", a=2, b=2)
                tt(lamw[:, :].rearrange("p (a c) -> p a c", a=2), lam[:, :, 0, :], lam[:, :, 1, :], ALU.mult)
                v.drain()
                v.tensor_reduce(lamv[:, 0:2], lamw[:, :].rearrange("p (a c) -> p a c", a=2), AX_X, ALU.add)
                v.drain().then_inc(lam_dots, 1)
                le_t.next(v)
                tt(lamv[:, 2:3], lamv[:, 1:2], lamv[:, 0:1], ALU.subtract)
                v.drain()
                v.tensor_scalar(lamv[:, 3:4], lamv[:, 2:3], lam_init(layer), None, ALU.subtract)
                gr_t.next(v)
                v.reciprocal(grinv[:, :, :], groot[:, :, :])
                v.drain()
                for t in range(NT):
                    qb = PR[:, t, BQ:BQ + 640].rearrange("p (g c) -> p g c", c=64)
                    qc = PR[:, t, CQ:CQ + 512].rearrange("p (g c) -> p g c", c=32)
                    tt(qb, qb, grinv[:, t, 0:10].unsqueeze(2).broadcast_to([P, 10, 64]), ALU.mult)
                    tt(qc, qc, grinv[:, t, 10:26].unsqueeze(2).broadcast_to([P, 16, 32]), ALU.mult)
                    v.drain()
                    tt(PR[:, t, BQ:BQ + 640], PR[:, t, BQ:BQ + 640], ROWS[:, R_GB:R_GB + 640], ALU.mult)
                    tt(PR[:, t, CQ:CQ + 512], PR[:, t, CQ:CQ + 512], ROWS[:, R_GC:R_GC + 512], ALU.mult)
                    v.drain()
                    if t > 0:
                        for at, ng, q, tab in ((BQ, B_GROUPS, 16, C_RB), (CQ, C_GROUPS, 8, C_RC)):
                            n = ng * 4 * q
                            x4 = PR[:, t, at:at + n].rearrange("p (g a b q) -> p g a b q", a=2, b=2, q=q)
                            h1, h2 = x4[:, :, :, 0, :], x4[:, :, :, 1, :]

                            def table(k):
                                a = tab + k * 4 * 2 * q + (t - 1) * 2 * q
                                return CON[:, a:a + 2 * q].rearrange("p (a q) -> p a q", a=2).unsqueeze(1)\
                                    .broadcast_to([P, ng, 2, q])
                            tmp = [AR[:, W0 + i * 320:W0 + i * 320 + n // 2].rearrange("p (g a q) -> p g a q", a=2, q=q)
                                   for i in range(4)]
                            tt(tmp[0], h1, table(0), ALU.mult)
                            tt(tmp[1], h2, table(1), ALU.mult)
                            tt(tmp[2], h2, table(0), ALU.mult)
                            tt(tmp[3], h1, table(1), ALU.mult)
                            v.drain()
                            tt(h1, tmp[0], tmp[1], ALU.subtract)
                            tt(h2, tmp[2], tmp[3], ALU.add)
                            v.drain()
                    v.drain().then_inc(qk_ready, 1)

                units = b_units()

                def prep(u):
                    t, g, pp = units[u]
                    nk = b_keys(t)
                    s = b_s[:, u % 2]
                    h = 4 * g + 2 * pp
                    band = CON[:, C_BAND1:C_BAND1 + nk] if t == 1 else CON[:, C_BAND:C_BAND + nk]
                    v.tensor_scalar(s[:, :, nk:nk + 1], ROWS[:, R_SINK + h:R_SINK + h + 2].unsqueeze(2), 8.0, None, ALU.mult)
                    for i in range(2):
                        ps = V.take(v)
                        if t == 0:
                            V.give(v.tensor_copy(s[:, i, 0:nk], ps[:, 0:nk]))
                        else:
                            V.give(tt(s[:, i, 0:nk], ps[:, 0:nk], band, ALU.add))
                    v.drain()
                    v.tensor_reduce(bmax[:, u % 2, :], s[:, :, 0:nk + 1], AX_X, ALU.max)
                    v.drain()
                    v.tensor_scalar(bmax[:, u % 2, :], bmax[:, u % 2, :], -0.125, None, ALU.mult).then_inc(b_scores, 1)

                def finish(u):
                    t, g, pp = units[u]
                    h = 4 * g + 2 * pp
                    be_t.next(v)
                    v.reciprocal(brec[:, u % 2, :], bsum[:, u % 2, :])
                    v.drain()
                    ps = V.take(v)
                    V.give(tt(MIX[:, t, MB + 64 * h:MB + 64 * h + 128].rearrange("p (i c) -> p i c", i=2),
                              ps[:, 0:128].rearrange("p (i c) -> p i c", i=2),
                              brec[:, u % 2, :].unsqueeze(2).broadcast_to([P, 2, 64]), ALU.mult))

                prep(0)
                for u in range(len(units)):
                    if u + 1 < len(units):
                        prep(u + 1)
                    finish(u)
                barrier()

                cu = c_units()

                def c_prep(u):
                    t, h = cu[u]
                    s = c_s[:, u % 2]
                    nk = c_keys(t)
                    for k0 in range(0, nk, 512):
                        n = min(512, nk - k0)
                        for c in range(2):
                            ps = V.take(v)
                            V.give(v.tensor_copy(s[:, c, k0:k0 + n], ps[:, 0:n]))
                    v.drain()
                    v.tensor_reduce(cmax[:, u % 2, :], s[:, :, 0:nk], AX_X, ALU.max)
                    v.drain()
                    v.tensor_scalar(cmax[:, u % 2, :], cmax[:, u % 2, :], -(32 ** -0.5), None, ALU.mult)\
                        .then_inc(c_scores, 1)

                def c_mid(u):
                    t, h = cu[u]
                    s = c_s[:, u % 2]
                    nk = c_keys(t)
                    ce_t.next(v)
                    v.reciprocal(crec[:, u % 2, :], csum[:, u % 2, :])
                    v.drain()
                    tt(crec[:, u % 2, 1:2], crec[:, u % 2, 1:2], lamv[:, 3:4], ALU.mult)
                    v.tensor_scalar(s[:, 0, 0:nk], s[:, 0, 0:nk], crec[:, u % 2, 0:1], None, ALU.mult)
                    v.drain()
                    v.scalar_tensor_tensor(s[:, 0, 0:nk], s[:, 1, 0:nk], crec[:, u % 2, 1:2], s[:, 0, 0:nk],
                                           ALU.mult, ALU.add).then_inc(c_weights, 1)

                def c_finish(u):
                    t, h = cu[u]
                    ps = V.take(v)
                    V.give(v.tensor_copy(MIX[:, t, MC + 64 * h:MC + 64 * h + 64], ps[:, 0:64]))

                c_prep(0)
                for u in range(len(cu)):
                    if u + 1 < len(cu):
                        c_prep(u + 1)
                    c_mid(u)
                    c_finish(u)
                barrier()

                gview = PR[:, :, AG:AG + 16].rearrange("p t (d x h) -> p d x t h", d=2, x=2)

                def dth(ap):
                    return ap.rearrange("p (d t h) -> p d t h", d=2, t=NT)
                for d in range(2):
                    v.tensor_scalar(dth(lft[:, :])[:, d], gview[:, d, 1], -1.0, None, ALU.mult)
                v.drain()
                for d in range(2):
                    tt(dth(lft[:, :])[:, d], dth(lft[:, :])[:, d], gview[:, d, 1], ALU.min)
                v.drain().then_inc(gates_signed, 1)
                for d in range(2):
                    v.tensor_scalar(dth(lf[:, :])[:, d], gview[:, d, 1], 0.0, None, ALU.min)
                v.memset(vaug[:, :, :, 64:65], 1.0)
                for t in range(NT):
                    v.tensor_copy(vaug[:, t, :, 0:64], PR[:, t, AV:AV + 256].rearrange("p (h c) -> p h c", h=4))
                v.memset(cst[:, 0], 0.0)
                v.memset(mstate[:, 0], 0.0)
                sp_t.next(v)
                v.drain()
                tt(lf[:, :], lf[:, :], lft[:, :], ALU.subtract)
                v.drain().then_inc(log_f_ready, 1)
                ps = V.take(v)
                V.give(v.tensor_copy(bci[:, :], ps[:, 0:80]))
                v.drain()
                for d in range(2):
                    tt(dth(ci[:, :])[:, d], gview[:, d, 0], dth(bci[:, 0:40])[:, d], ALU.subtract)
                v.drain()
                bc, bl, cc = dth(bci[:, 0:40]), dth(bci[:, 40:80]), dth(ci[:, :])
                seen = set()
                for seg, d, t in a_units():
                    m = mstate[:, seg, d, :]
                    mask = CON[:, (C_MF, C_MB)[d]:(C_MF, C_MB)[d] + P]
                    ar, mt = args[:, 0], mtmp[:, 0]
                    tt(dg[:, :, :], ident.unsqueeze(1).broadcast_to([P, 4, P]),
                       cc[:, d, t, :].unsqueeze(2).broadcast_to([P, 4, P]), ALU.mult).then_inc(diag_ready, 1)
                    ps = V.take(v)
                    tt(cm[:, :, :], ps[:, :].rearrange("p (h s) -> p h s", h=4),
                       mask.unsqueeze(1).broadcast_to([P, 4, P]), ALU.add)
                    V.give(v.tensor_reduce(mt[:, 0, :], ps[:, :].rearrange("p (h s) -> p h s", h=4), AX_X, ALU.max))
                    v.drain()
                    v.tensor_reduce(mt[:, 1, :], cm[:, :, :], AX_X, ALU.max)
                    tt(mt[:, 2, :], mt[:, 0, :], m, ALU.max)
                    v.drain()
                    tt(mt[:, 3, :], mt[:, 1, :], m, ALU.max)
                    tt(ar[:, 1, :], m, mt[:, 2, :], ALU.subtract)
                    tt(ar[:, 2, :], cc[:, d, t, :], mt[:, 2, :], ALU.subtract)
                    v.drain()
                    tt(ar[:, 0, :], m, mt[:, 3, :], ALU.subtract)
                    tt(mt[:, 4, :], bc[:, d, t, :], mt[:, 3, :], ALU.add)
                    v.tensor_scalar(ar[:, 4, :], mt[:, 3, :], -1.0, None, ALU.mult)
                    v.drain()
                    v.tensor_scalar(ar[:, 3, :], mt[:, 4, :], -1.0, None, ALU.mult)
                    tt(m, bl[:, d, t, :], mt[:, 2, :], ALU.add)
                    v.drain().then_inc(ml_args, 1)
                    me_t.next(v)
                    for odd in range(2):
                        ps = V.take(v)
                        V.give(v.scalar_tensor_tensor(pm[:, odd::2, :], ps[:, 0:256].rearrange("p (j s) -> p j s", j=2),
                                                      0.125, cm[:, odd::2, :], ALU.mult, ALU.mult))
                    v.scalar_tensor_tensor(wk[:, :].rearrange("p (h c) -> p h c", h=4),
                                           PR[:, t, AK:AK + 256].rearrange("p (h c) -> p h c", h=4), 0.125,
                                           ar[:, 2, :].unsqueeze(2).broadcast_to([P, 4, 64]), ALU.mult, ALU.mult)
                    v.drain().then_inc(ml_products, 1)
                    for odd in range(2):
                        ps = V.take(v)
                        V.give(tt(nd[:, odd::2, :], ps[:, 0:130].rearrange("p (j c) -> p j c", j=2),
                                  ar[:, 0, odd::2].unsqueeze(2).broadcast_to([P, 2, 65]), ALU.mult))
                    ps = V.take(v)
                    for h in range(4):
                        r = slice(64 * (h % 2), 64 * (h % 2) + 64)
                        st = cst[r, seg, d, h // 2, :]
                        ins = v.scalar_tensor_tensor(st, st, ar[r, 1, h:h + 1], ps[r, h * 65:(h + 1) * 65],
                                                     ALU.mult, ALU.add)
                    V.give(ins)
                    v.drain()
                    ps = V.take(v)
                    V.give(tt(nd[:, :, :], nd[:, :, :], ps[:, 0:260].rearrange("p (h c) -> p h c", h=4), ALU.add))
                    v.drain()
                    dn = nd[:, :, 64:65]
                    d0, d1 = den[:, 0, :].unsqueeze(2), den[:, 1, :].unsqueeze(2)
                    v.tensor_scalar(d0, dn, -1.0, None, ALU.mult)
                    v.drain()
                    tt(d0, d0, dn, ALU.max)
                    v.drain()
                    tt(d0, d0, ar[:, 3, :].unsqueeze(2), ALU.max)
                    v.drain()
                    v.reciprocal(d1, d0)
                    v.drain()
                    dst = MIX[:, t, MA:MA + 256].rearrange("p (h c) -> p h c", h=4)
                    rec = den[:, 1, :].unsqueeze(2).broadcast_to([P, 4, 64])
                    if t not in seen:
                        seen.add(t)
                        tt(dst, nd[:, :, 0:64], rec, ALU.mult)
                    else:
                        tt(htmp[:, :, :], nd[:, :, 0:64], rec, ALU.mult)
                        v.drain()
                        tt(dst, dst, htmp[:, :, :], ALU.add)
                    v.drain()
                    if (seg, d) == (0, 1):
                        v.drain().then_inc(state_final, 1)
                barrier()

                for t in range(NT):
                    for j, c0 in enumerate((MA, MC)):
                        tt(hsq[:, j * 256:(j + 1) * 256], MIX[:, t, c0:c0 + 256], MIX[:, t, c0:c0 + 256], ALU.mult)
                    v.drain()
                    v.tensor_reduce(hss[:, t, :], hsq.rearrange("p (g c) -> p g c", c=64), AX_X, ALU.add)
                    v.drain()
                v.drain().then_inc(head_squares, 1)
                hr_t.next(v)
                v.reciprocal(hrinv[:, :, :], hroot[:, :, :])
                v.drain()
                v.tensor_scalar(hrinv[:, :, 4:8], hrinv[:, :, 4:8], 1.0 - lam_init(layer), None, ALU.mult)
                v.drain()
                for t in range(NT):
                    for j, c0 in enumerate((MA, MC)):
                        y = MIX[:, t, c0:c0 + 256].rearrange("p (h c) -> p h c", h=4)
                        tt(y, y, hrinv[:, t, 4 * j:4 * j + 4].unsqueeze(2).broadcast_to([P, 4, 64]), ALU.mult)
                    v.drain()
                    tt(MIX[:, t, MA:MA + 256], MIX[:, t, MA:MA + 256], ROWS[:, R_GA:R_GA + 256], ALU.mult)
                    tt(MIX[:, t, MC:MC + 256], MIX[:, t, MC:MC + 256], ROWS[:, R_GO:R_GO + 256], ALU.mult)
                    v.drain()
                    tt(MIX[:, t, MA:MA + 256], MIX[:, t, MA:MA + 256], PR[:, t, AO:AO + 256], ALU.mult)
                v.drain().then_inc(mix_ready, 1)

                job = 0
                for n in range(2):
                    for t in range(NT):
                        ps = V.take(v)
                        tmp = xtmp[:, job % 2, :]
                        V.give(tt(tmp, ps[:, :], GB[:, 0, cond_of(t), n * 512:(n + 1) * 512], ALU.mult))
                        v.drain()
                        tt(X[:, t, n * 512:(n + 1) * 512], X[:, t, n * 512:(n + 1) * 512], tmp, ALU.add)
                        job += 1
                v.drain().then_inc(x_ready, 1)
                normed()
                barrier()

                for t in range(NT):
                    s = SC[:, t]
                    for rnd in range(2):
                        lo, hi = 8 * rnd, 8 * rnd + 8
                        for c in range(HC):
                            v.max(val[:, c, lo:hi], s[:, c, :])
                        v.drain()
                        for c in range(HC):
                            v.max_index(idx[:, c, lo:hi], val[:, c, lo:hi], s[:, c, :])
                        if rnd == 0:
                            v.drain()
                            for c in range(HC):
                                v.match_replace(s[:, c, :], val[:, c, lo:hi], s[:, c, :], -BIG)
                            v.drain()
                    v.drain()
                    v.tensor_copy(idxf[:, :, :, :].rearrange("p h c k -> p (h c) k"), idx[:, :, :])
                    v4 = val[:, :, :].rearrange("p (h c) k -> p h c k", c=2)
                    tt(cand, v4[:, :, 0, :].unsqueeze(3).broadcast_to([P, HEADS, TOPK, TOPK]),
                       v4[:, :, 1, :].unsqueeze(2).broadcast_to([P, HEADS, TOPK, TOPK]), ALU.add)
                    v.drain()
                    for rnd in range(2):
                        lo, hi = 8 * rnd, 8 * rnd + 8
                        for h in range(HEADS):
                            v.max(tops[:, h, lo:hi], cand[:, h].rearrange("p a b -> p (a b)"))
                        v.drain()
                        for h in range(HEADS):
                            v.max_index(posu[:, h, lo:hi], tops[:, h, lo:hi], cand[:, h].rearrange("p a b -> p (a b)"))
                        if rnd == 0:
                            v.drain()
                            for h in range(HEADS):
                                ch = cand[:, h].rearrange("p a b -> p (a b)")
                                v.match_replace(ch, tops[:, h, lo:hi], ch, -BIG)
                            v.drain()
                    v.drain()
                    tt(gate[:, :, :], tops[:, :, :], tops[:, :, 0:1].broadcast_to([P, HEADS, TOPK]), ALU.subtract)
                    v.tensor_scalar(pab[0], pflat, 4, None, ALU.logical_shift_right)
                    v.tensor_scalar(pab[1], pflat, 15, None, ALU.bitwise_and)
                    v.drain().then_inc(tops_ready, 1)
                    for j in range(2):
                        v.tensor_copy(pabf[j], pab[j])
                    v.drain()
                    for j in range(2):
                        eq3 = eq.rearrange("p (n a) -> p n a", a=TOPK)
                        tt(eq3, pabf[j].unsqueeze(2).broadcast_to([P, P, TOPK]),
                           iota[:, 0:TOPK].unsqueeze(1).broadcast_to([P, P, TOPK]), ALU.is_equal)
                        v.drain()
                        eq4 = eq.rearrange("p (h k a) -> p h k a", h=HEADS, a=TOPK)
                        tt(eq4, eq4, idxf[:, :, j, :].unsqueeze(2).broadcast_to([P, HEADS, TOPK, TOPK]), ALU.mult)
                        v.drain()
                        v.tensor_reduce(sel[j], eq3, AX_X, ALU.add)
                        v.drain()
                    te_t.next(v)
                    v.tensor_reduce(gsum, gate[:, :, :], AX_X, ALU.add)
                    v.drain()
                    v.reciprocal(grec, gsum)
                    v.drain()
                    tt(gate[:, :, :], gate[:, :, :], grec.unsqueeze(2).broadcast_to([P, HEADS, TOPK]), ALU.mult)
                    v.drain().then_inc(picks_ready, 1)
                    ps = V.take(v)
                    cols = slice(t * P, (t + 1) * P)
                    for j in range(2):
                        v.tensor_copy(IGT[j][:, cols], ps[:, j * P:(j + 1) * P])
                    v.tensor_copy(gbf, ps[:, 2 * P:3 * P])
                    v.drain()
                    v.tensor_copy(IGT[2][:, cols], gbf)
                    v.drain()
                    tt(IGT[4][:, cols], ps[:, 2 * P:3 * P], IGT[2][:, cols], ALU.subtract)
                    v.drain()
                    v.tensor_copy(gbf, IGT[4][:, cols])
                    v.drain()
                    v.tensor_copy(IGT[3][:, cols], gbf)
                    v.drain()
                    V.give(tt(IGT[4][:, cols], IGT[4][:, cols], IGT[3][:, cols], ALU.subtract))
                barrier()

                used = Tally(sca_filled, loop_base["gate", layer])
                with v.Fori(0, N // (2 * GT)) as i:
                    used.enter(i, 32)
                    for slot in range(2):
                        with v.Fori(0, GT // 16) as j:
                            used.enter(j, 4)
                            for b in range(4):
                                v.wait_ge(sca_filled, used.at(-3))
                                used.n += 1
                                for q in range(4):
                                    tok = i * (2 * GT) + (slot * GT + 4 * b + q) + j * 16

                                    def col(a):
                                        return a[:, bass.ds(tok, 1)]
                                    v.tensor_scalar(OH[:, b, q, 3, :], iota, col(IGT[1]), None, ALU.is_equal)
                                    for part in range(3):
                                        ins = v.tensor_scalar(OH[:, b, q, part, :], iota, col(IGT[0]), col(IGT[2 + part]),
                                                              ALU.is_equal, ALU.mult)
                                ins.then_inc(onehot_ready, 1)
                            used.leave(GT // 16)
                    used.leave(N // (2 * GT))
                barrier()

                v.memset(ACC[:, :, :], 0.0)
                v.drain()
                steps = NK // BLOCKS
                ge_t.n = loop_base["s", layer]
                with v.Fori(0, steps) as i:
                    V.filled.enter(i, 4 * NT)
                    ge_t.enter(i, 2 * BLOCKS)
                    for x in u_t:
                        x.enter(i, 32 * BLOCKS // U_SLOTS)
                    for b in range(BLOCKS):
                        slot = b % U_SLOTS
                        u_t[slot].n += 32
                        v.wait_ge(u_in[slot], u_t[slot].at())
                        ge_t.n += 2
                        v.wait_ge(sca_drained, ge_t.at())
                        tt(HW[:, b, :], GE[:, b % 2, :], GR[slot], ALU.mult).then_inc(hidden_ready, 1)
                    for half in range(2):
                        for t in range(NT):
                            for ch in range(2):
                                ps = V.take(v)
                                a = ACC[:, t, ch * 512:(ch + 1) * 512]
                                V.give(tt(a, a, ps[:, :], ALU.add))
                        v.drain()
                    V.filled.leave(steps)
                    ge_t.leave(steps)
                    for x in u_t:
                        x.leave(steps)
                for t in range(NT):
                    tt(ACC[:, t, :], ACC[:, t, :], GB[:, 1, cond_of(t), :], ALU.mult)
                v.drain()
                for t in range(NT):
                    tt(X[:, t, :], X[:, t, :], ACC[:, t, :], ALU.add)
                v.drain().then_inc(x_final if layer == DEPTH - 1 else x_ready, 1)
                barrier()

        @block.scalar
        def _(a):
            S = BankReader(sbank, sca_filled, sca_drained)
            phase = [0]
            x_t, mod_t, gs_t, ld_t = Tally(x_ready), Tally(mod_ready), Tally(group_squares), Tally(lam_dots)
            bs_t, cs_t, sg_t, ma_t, hs_t = Tally(b_scores), Tally(c_scores), Tally(gates_signed), Tally(ml_args), Tally(head_squares)
            tp_t = Tally(tops_ready)
            stored = [Tally(s, 0) for s in gates_stored]

            def barrier():
                phase[0] += 1
                a.drain().then_inc(phase_done, 1)
                a.wait_ge(phase_done, 3 * phase[0])

            def roots():
                for t in range(NT):
                    a.activation(MIX[:, t, :], X[:, t, :], ACT.Square, accum_out=ssq[:, t:t + 1])
                a.drain()
                a.activation(root[:, :], ssq[:, :], ACT.Sqrt, bias=eps, scale=1.0 / D).then_inc(roots_ready, 1)

            def modulated(which):
                for t in range(NT):
                    for half in range(2):
                        ps = S.take(a)
                        for j in range(4):
                            k = 4 * half + j
                            c = cond_of(t)
                            ins = a.activation(HTk[:, k, t * P:(t + 1) * P], ps[:, j * P:(j + 1) * P], ACT.Identity,
                                               bias=mod[:, 2 * which, k, c:c + 1], scale=mod[:, 2 * which + 1, k, c:c + 1])
                        S.give(ins)

            a.wait_ge(setup_in, 16 * 4)
            a.activation(conds[:, :, :], cond[:, :, :], ACT.Silu).then_inc(cond_ready, 1)
            for layer in range(DEPTH):
                if layer:
                    x_t.next(a)
                roots()
                for w in range(2):
                    for c in range(2):
                        for half in range(2):
                            ps = S.take(a)
                            S.give(a.activation(GB[:, w, c, half * 512:(half + 1) * 512], ps[:, :], ACT.Copy))
                mod_t.next(a)
                modulated(0)
                barrier()

                gs_t.next(a)
                a.activation(groot[:, :, 0:10], gss[:, :, 0:10], ACT.Sqrt, bias=eps, scale=1.0 / 64)
                a.activation(groot[:, :, 10:26], gss[:, :, 10:26], ACT.Sqrt, bias=eps, scale=1.0 / 32).then_inc(group_roots, 1)
                ld_t.next(a)
                a.activation(lamv[:, 0:2], lamv[:, 0:2], ACT.Exp).then_inc(lam_exps, 1)
                for t in range(NT):
                    for b0 in range(0, 13, 4):
                        nb = min(4, 13 - b0)
                        ps = S.take(a)
                        S.give(a.activation(QKT[:, b0:b0 + nb, t * P:(t + 1) * P],
                                            ps[:, 0:nb * P].rearrange("p (b n) -> p b n", b=nb), ACT.Copy))
                units = b_units()

                def exps(u):
                    nk = b_keys(units[u][0])
                    bs_t.next(a)
                    for i in range(2):
                        row = b_s[:, u % 2, i, 0:nk + 1]
                        ins = a.activation(row, row, ACT.Exp, bias=bmax[:, u % 2, i:i + 1], scale=0.125,
                                           accum_out=bsum[:, u % 2, i:i + 1])
                    ins.then_inc(b_exps, 1)

                exps(0)
                for u in range(len(units)):
                    if u + 1 < len(units):
                        exps(u + 1)
                    nk = b_keys(units[u][0])
                    for i in range(2):
                        ps = S.take(a)
                        S.give(a.activation(b_et[:, u % 2, i, 0:nk], ps[:, 0:nk], ACT.Copy))
                barrier()

                cu = c_units()

                def c_exp(u):
                    nk = c_keys(cu[u][0])
                    cs_t.next(a)
                    for i in range(2):
                        row = c_s[:, u % 2, i, 0:nk]
                        ins = a.activation(row, row, ACT.Exp, bias=cmax[:, u % 2, i:i + 1], scale=32 ** -0.5,
                                           accum_out=csum[:, u % 2, i:i + 1])
                    ins.then_inc(c_exps, 1)

                c_exp(0)
                for u in range(len(cu)):
                    if u + 1 < len(cu):
                        c_exp(u + 1)
                    nk = c_keys(cu[u][0])
                    for b0 in range(0, nk, 512):
                        n = min(512, nk - b0)
                        ps = S.take(a)
                        S.give(a.activation(c_at[:, u % 2, b0:b0 + n], ps[:, 0:n], ACT.Copy))
                barrier()

                sg_t.next(a)
                a.activation(lft[:, :], lft[:, :], ACT.Exp)
                a.drain()
                a.activation(lft[:, :], lft[:, :], ACT.Ln, bias=ones[:, 0:1]).then_inc(softplus_ready, 1)
                for seg, d, t in a_units():
                    ma_t.next(a)
                    for h in range(4):
                        a.activation(cm[:, h, :], cm[:, h, :], ACT.Exp, bias=args[:, 0, 4, h:h + 1])
                    a.activation(args[:, 0, 0:4, :], args[:, 0, 0:4, :], ACT.Exp).then_inc(ml_exps, 1)
                    ps = S.take(a)
                    S.give(a.activation(pt[:, :, :], ps[:, :].rearrange("p (h s) -> p h s", h=4), ACT.Copy))
                barrier()

                hs_t.next(a)
                a.activation(PR[:, :, AO:AO + 256], PR[:, :, AO:AO + 256], ACT.Sigmoid)
                a.activation(hroot[:, :, :], hss[:, :, :], ACT.Sqrt, bias=eps, scale=1.0 / 64).then_inc(head_roots, 1)
                for t in range(NT):
                    for half in range(2):
                        ps = S.take(a)
                        S.give(a.activation(HTk[:, 4 * half:4 * half + 4, t * P:(t + 1) * P],
                                            ps[:, :].rearrange("p (k n) -> p k n", k=4), ACT.Copy))
                x_t.next(a)
                roots()
                modulated(1)
                def queries(c):
                    for j in range(2):
                        ps = S.take(a)
                        S.give(a.activation(QT[:, c % 2, j * HALF:(j + 1) * HALF], ps[:, 0:HALF], ACT.Copy))
                for c in range(HC + 1):
                    if c < HC:
                        queries(c)
                    if c >= 1:
                        for t0, n in ((0, 4), (4, 1)):
                            ps = S.take(a)
                            S.give(a.activation(SC[:, t0:t0 + n, c - 1, :], ps[:, 0:n * P].rearrange("p (t k) -> p t k", t=n),
                                                ACT.Copy))
                barrier()
                for t in range(NT):
                    tp_t.next(a)
                    a.activation(gate[:, :, :], gate[:, :, :], ACT.Exp).then_inc(top_exps, 1)
                barrier()

                with a.Fori(0, N // (2 * GT)) as i:
                    S.filled.enter(i, 32)
                    for x in stored:
                        x.enter(i, 16)
                    for slot in range(2):
                        stored[slot].n += 16
                        a.wait_ge(gates_stored[slot], stored[slot].at())
                        with a.Fori(0, GT // 16) as j:
                            S.filled.enter(j, 4)
                            for b in range(4):
                                ps = S.take(a)
                                dst = GS[slot][:, :, bass.ds(j * 16 + 4 * b, 4)].rearrange("p b t -> p t b")
                                S.give(a.activation(dst, ps[:, :].rearrange("p (t b) -> p t b", t=4), ACT.Copy))
                            S.filled.leave(GT // 16)
                        a.drain().then_inc(gates_built, 1)
                    S.filled.leave(N // (2 * GT))
                    for x in stored:
                        x.leave(N // (2 * GT))
                barrier()

                steps = NK // BLOCKS
                hid = Tally(hidden_ready, 8 + layer * NK)
                with a.Fori(0, steps) as i:
                    S.filled.enter(i, 2 * BLOCKS)
                    hid.enter(i, BLOCKS)
                    for b in range(BLOCKS):
                        a.wait_ge(hidden_ready, hid.at(-1))
                        hid.n += 1
                        for j in range(2):
                            ps = S.take(a)
                            S.give(a.activation(GE[:, b % 2, j * HALF:(j + 1) * HALF], ps[:, 0:HALF], ACT.Gelu))
                    S.filled.leave(steps)
                    hid.leave(steps)
                barrier()

        @block.sync
        def _(sp):
            sp.dma_start(CON[:, :], io["consts"]).then_inc(setup_in, 16)
            sp.dma_start(cond[:, :, :], io["cond"]).then_inc(setup_in, 16)
            sp.dma_start(X[:, 0, :], io["x_prompt"]).then_inc(setup_in, 16)
            sp.dma_start(X[:, 1:NT, :], io["x_sample"].rearrange("(t p) c -> p t c", p=P)).then_inc(setup_in, 16)
            for slot in range(2):
                sp.sem_inc(gates_stored[slot], 16)
            n_slice = [0]
            outs = [0]

            def load(src, width):
                n = n_slice[0]
                n_slice[0] += 1
                if n >= 3:
                    sp.wait_ge(*slice_read[n - 3])
                sp.dma_start(wslot[n % 3][:, 0:width], src).then_inc(slice_in[n % 3], 16)

            def store(dst, src):
                sp.dma_start(dst, src).then_inc(out_done, 16)
                outs[0] += 16

            built = Tally(gates_built)
            for layer in range(DEPTH):
                ph = 8 * layer
                if layer:
                    sp.wait_ge(phase_done, 3 * ph)
                sp.dma_start(ROWS[:, :], io["rows"][layer:layer + 1, :].broadcast_to([P, N_ROWS])).then_inc(vectors_in, 16)
                sp.dma_start(bada, io["b_ada"][layer:layer + 1, :].broadcast_to([2, 6 * D])).then_inc(vectors_in, 16)
                sp.dma_start(ngain[:, :, :], io["ngain"][layer]).then_inc(vectors_in, 16)
                for n in range(ADA_SLICES):
                    load(io["w_ada"][layer, n], KD * 512)
                for n in range(IN_SLICES):
                    load(io["w_in"][layer, n], KD * IN_W)
                sp.wait_ge(phase_done, 3 * (ph + 1))
                sp.dma_start(kcb, io["cache_bk"][layer]).then_inc(caches_in, 16)
                sp.dma_start(kcc[:, :, :], io["cache_ck"][layer]).then_inc(caches_in, 16)
                sp.dma_start(vcb, io["cache_bv"][layer]).then_inc(caches_in, 16)
                sp.dma_start(vcc, io["cache_cv"][layer]).then_inc(caches_in, 16)
                sp.dma_start(mstate[:, 1], io["state_m"][layer:layer + 1].broadcast_to([P, 8])).then_inc(caches_in, 16)
                sp.wait_ge(qk_ready, NT * layer + 1)
                store(io["o_bk"][layer], PR[:, 0, BK:BK + 128])
                store(io["o_bv"][layer], PR[:, 0, BV:BV + 128])
                store(io["o_ck"][layer], PR[:, 0, CK:CK + 256])
                store(io["o_cv"][layer], PR[:, 0, CV:CV + 256])
                sp.wait_ge(qk_ready, NT * (layer + 1))
                sp.dma_start(cst[:, 1], io["state_C"][layer]).then_inc(caches_in, 16)
                sp.wait_ge(state_final, layer + 1)
                store(io["o_state"][layer], cst[:, 0])
                store(io["o_m"][layer:layer + 1], mstate[0:1, 0])
                sp.wait_ge(phase_done, 3 * (ph + 4))
                for n in range(2):
                    load(io["w_out"][layer, n], KD * 512)
                sp.wait_ge(mix_ready, layer + 1)
                sp.dma_start(SUBT[:, :, :], io["subkeys"][layer]).then_inc(subkeys_in, 16)
                for n in range(4):
                    load(io["wq"][layer, n], WSLOT)

                with sp.Fori(0, N // (2 * GT)) as i:
                    built.enter(i, 2)
                    for slot in range(2):
                        built.next(sp)
                        dst = io["gates"][:, :, bass.ds(i * (2 * GT) + slot * GT, GT)].rearrange("b p t -> p b t")
                        sp.dma_start(dst, GS[slot]).then_inc(gates_stored[slot], 16)
                    built.leave(N // (2 * GT))
                for slot in range(2):
                    sp.wait_ge(gates_stored[slot], 16 + 16 * (layer + 1) * N // (2 * GT))
                sp.wait_ge(phase_done, 3 * (ph + 7))
                hid = Tally(hidden_ready, 8 + layer * NK)
                act = Tally(sca_filled, loop_base["s", layer])
                out = Tally(vec_filled, loop_base["v", layer])
                with sp.Fori(0, NK // BLOCKS) as i:
                    hid.enter(i, BLOCKS)
                    act.enter(i, 2 * BLOCKS)
                    out.enter(i, 4 * NT)
                    for b in range(BLOCKS):
                        slot = b % U_SLOTS
                        sp.wait_ge(sca_filled, act.at(2 * (b - U_SLOTS) + 2))
                        sp.dma_start(UR[slot], io["u"][layer, bass.ds(i * BLOCKS + b, 1)].rearrange("o p k e -> p (o k) e"))\
                            .then_inc(u_in[slot], 16)
                        sp.wait_ge(hidden_ready, hid.at(b - U_SLOTS + 1))
                        sp.dma_start(GR[slot], io["gates"][bass.ds(i * BLOCKS + b, 1)].rearrange("o p t -> p (o t)"))\
                            .then_inc(u_in[slot], 16)
                        sp.wait_ge(vec_filled, out.at(-4 * NT + (10 if b < 4 else 20)))
                        sp.dma_start(VR[b], io["v"][layer, bass.ds(i * BLOCKS + b, 1)].rearrange("o p c -> p (o c)"))\
                            .then_inc(v_in[b], 16)
                    hid.n += BLOCKS
                    act.n += 2 * BLOCKS
                    out.n += 4 * NT
                    hid.leave(NK // BLOCKS)
                    act.leave(NK // BLOCKS)
                    out.leave(NK // BLOCKS)
            sp.wait_ge(x_final, 1)
            store(io["o_prompt"], X[:, 0, :])
            store(io["o_sample"].rearrange("(t p) c -> p t c", p=P), X[:, 1:NT, :])
            sp.wait_ge(out_done, outs[0])


def _constants():
    import numpy as np
    c = np.zeros((P, N_CONST), np.float32)
    i = np.arange(P)
    lower = i[:, None] >= i[None, :]
    c[:, C_ID:C_ID + P] = np.eye(P)
    c[:, C_TRIF:C_TRIF + P] = lower.T
    c[:, C_TRIB:C_TRIB + P] = lower
    c[:, C_ONE:C_ONE + P] = 1
    c[:, C_MF:C_MF + P] = np.where(lower, 0, NEG)
    c[:, C_MB:C_MB + P] = np.where(lower.T, 0, NEG)
    before, after = np.where(lower.T, 0, NEG), np.where(lower, 0, NEG)
    zero = np.zeros((P, P))
    c[:, C_BAND:C_BAND + 512] = np.concatenate([zero, before, zero, after], 1)
    c[:, C_BAND1:C_BAND1 + 384] = np.concatenate([zero, zero, after], 1)
    c[:, C_IOTA:C_IOTA + NK] = i
    t = np.arange(DEC_SEQ)
    place = np.stack([t // 64, t % 64], 1).astype(np.float32)
    for at, q in ((C_RB, 16), (C_RC, 8)):
        inv = (np.float32(10000.0) ** (-np.arange(q, dtype=np.float32) / np.float32(q))).astype(np.float32)
        ang = place[:, :, None] * inv
        for k, f in enumerate((np.cos, np.sin)):
            tab = f(ang).astype(np.float32).reshape(NT - 1, P, 2 * q).transpose(1, 0, 2).reshape(P, -1)
            c[:, at + k * 8 * q:at + (k + 1) * 8 * q] = tab
    for r in range(2):
        c[r, C_SEL + r * P:C_SEL + (r + 1) * P] = 1
    c[:, C_EPS] = EPS
    return c


def kernel(**inputs):
    import numpy as np
    import concourse.bacc as bacc
    from concourse.bass_utils import run_bass_kernel_spmd

    f = {k: np.asarray(v) for k, v in inputs.items()}
    L = DEPTH
    sizes = (256, 256, 256, 256, 16, 512, 128, 128, 256, 256, 256)
    starts = np.concatenate([[0], np.cumsum(sizes)])
    bq = starts[5] + np.concatenate([np.arange(64) + 64 * h for p in range(4) for h in (p, p + 4)])
    order = np.concatenate([np.arange(starts[5]), bq, np.arange(starts[6], starts[-1])])

    def chunks(w, width):
        n = w.shape[-1] // width
        return w.reshape(L, KD, P, n, width).transpose(0, 3, 2, 1, 4)

    def tiled(g, k):
        return np.tile(g.reshape(L, -1), (1, k))

    arrays = {
        "consts": _constants(),
        "cond": np.stack([f["c_ctx"].reshape(KD, P).T, f["c"].reshape(KD, P).T], -1),
        "x_prompt": f["x_prompt"][0],
        "x_sample": f["x_sample"][0],
        "rows": np.concatenate([f["b_in"][:, order], tiled(f["b_q_gain"], 8), tiled(f["b_k_gain"], 2),
                                tiled(f["c_q_gain"], 4), tiled(f["c_k_gain"], 4), f["a_out_gain"],
                                tiled(f["c_out_gain"], 4), f["b_sink"], f["c_lambda"].reshape(L, -1)], 1),
        "b_ada": f["b_ada"],
        "ngain": f["norm_gain"].reshape(L, 2, KD, P).transpose(0, 3, 1, 2),
        "w_ada": chunks(f["w_ada"], 512).reshape(L, ADA_SLICES, P, -1),
        "w_in": chunks(f["w_in"][:, :, order], IN_W).reshape(L, IN_SLICES, P, -1),
        "w_out": chunks(f["w_out"], 512).reshape(L, 2, P, -1),
        "wq": f["peer_wq"].reshape(L, KD, P, 4, 4, P).transpose(0, 3, 2, 4, 1, 5).reshape(L, 4, P, -1),
        "subkeys": f["peer_subkeys"].transpose(0, 4, 1, 2, 3).reshape(L, P, HC, NK),
        "cache_bk": f["cache_swa_k"][0].transpose(0, 2, 3, 1).reshape(L, P, PAST),
        "cache_bv": f["cache_swa_v"][0].reshape(L, PAST, 128),
        "cache_ck": f["cache_diff_k"][0].reshape(L, PAST, 2, P).transpose(0, 3, 2, 1),
        "cache_cv": f["cache_diff_v"][0].reshape(L, PAST, 256),
        "state_C": np.concatenate([f["state_mlstm_C"][0], f["state_mlstm_n"][0][..., None]], -1)
        .reshape(L, 2, 2, 2, 64, 65).transpose(0, 3, 4, 1, 2, 5).reshape(L, P, 2, 2, 65),
        "state_m": f["state_mlstm_m"][0].reshape(L, 8),
        "u": f["peer_u"].reshape(L, NK, P, KD, P).transpose(0, 1, 4, 3, 2),
        "v": f["peer_v"].reshape(L, NK, P, D),
    }
    outs = {"o_prompt": (SEQ, D), "o_sample": (DEC_SEQ, D), "o_bk": (L, P, 128), "o_bv": (L, P, 128),
            "o_ck": (L, P, 256), "o_cv": (L, P, 256), "o_state": (L, P, 2, 2, 65), "o_m": (L, 8)}
    nc = bacc.Bacc("TRN2", target_bir_lowering=False, num_devices=1)
    io, fed = {}, {}
    for name, a in arrays.items():
        a = np.ascontiguousarray(a)
        fed[f"in_{name}"] = a
        io[name] = nc.dram_tensor(f"in_{name}", a.shape, mybir.dt.from_np(a.dtype), kind="ExternalInput").ap()
    for name, shape in outs.items():
        io[name] = nc.dram_tensor(f"out_{name}", shape, F32, kind="ExternalOutput").ap()
    io["gates"] = nc.dram_tensor("gates", (NK, P, N), F32, kind="Internal").ap()
    hybrid_step(nc, io)
    r = run_bass_kernel_spmd(nc, [fed], core_ids=[0]).results[0]
    g = {name: np.asarray(r[f"out_{name}"]) for name in outs}
    state = g["o_state"].reshape(L, 2, 64, 2, 2, 65).transpose(0, 3, 4, 1, 2, 5).reshape(1, L, 2, 4, 64, 65)
    return (g["o_prompt"][None], g["o_sample"][None],
            g["o_bk"].reshape(1, L, P, 2, 64), g["o_bv"].reshape(1, L, P, 2, 64),
            g["o_ck"].reshape(1, L, P, 4, 64), g["o_cv"].reshape(1, L, P, 4, 64),
            np.ascontiguousarray(state[..., :64]), np.ascontiguousarray(state[..., 64]),
            g["o_m"].reshape(1, L, 2, 4))
```

```python
import math
from contextlib import ExitStack

import concourse.bass as bass
from concourse import mybir

F32 = mybir.dt.float32
F32R = mybir.dt.float32r
BF16 = mybir.dt.bfloat16
U32 = mybir.dt.uint32
ALU = mybir.AluOpType
ACT = mybir.ActivationFunctionType
AX_X = mybir.AxisListType.X

P = 128
D = 1024
KD = D // P
SEQ, DEC_SEQ, PAST = 128, 512, 128
NT = (SEQ + DEC_SEQ) // P
N = NT * P
DEPTH = 2
EPS = 1e-6
NEG = -1e30
BIG = 3e38

AQ, AK, AV, AO, AG = 0, 256, 512, 768, 1024
BQ, BK, BV = 1040, 1552, 1680
CQ, CK, CV = 1808, 2064, 2320
IN_COLS = 2576
IN_SLICES = 7
IN_W = IN_COLS // IN_SLICES
B_GROUPS, C_GROUPS = 10, 16

MA, MB, MC = 0, 256, 768

ADA_SLICES = 6 * D // 512

C_ID, C_TRIF, C_TRIB, C_ONE, C_MF, C_MB = 0, 128, 256, 384, 512, 640
C_BAND, C_BAND1 = 768, 1280
C_IOTA = 1664
C_RB, C_RC = 1792, 2048
C_SEL = 2176
C_EPS = 2432
N_CONST = 2433

R_BIN, R_GB, R_GC, R_GA, R_GO, R_SINK, R_LAM = 0, 2576, 3216, 3728, 3984, 4240, 4248
N_ROWS = 4376

NK = 128
HEADS, TOPK = 8, 16
HC = 2 * HEADS
HALF = N // 2
GT = 64
GROUP = 4
PICK_BLOCKS = 8
TOK = 16

A_ROWS, A_X, A_HT = 0, 4376, 9496
A_P, A_WR, A_MIX = 14616, 27496, 39784
ARENA = 44904
A_HTL = A_P
A_WQ, A_QT, A_SC = 19736, 27928, 29464
A_UR, A_UH, A_UL, A_GE = 19736, 21784, 23832, 25880
A_GS = (28440, 36632)
A_VR, A_TMP, A_GG, A_VH, A_VL = (0, 1024, 3328, 38680), 2048, 4376, 9496, 17688
A_HWH, A_HWL, A_HB = 25880, 31000, 36120
WSLOT = 4096


class Tally:

    def __init__(self, sem, n=0):
        self.sem, self.n, self.terms, self.start = sem, n, [], []

    def at(self, k=0):
        value = self.n + k
        for reg, per in self.terms:
            value = reg * per + value
        return value

    def enter(self, reg, per):
        self.terms.append((reg, per))
        self.start.append(self.n)

    def leave(self, turns):
        _, per = self.terms.pop()
        began = self.start.pop()
        assert self.n - began == per, (self.n - began, per)
        self.n = began + turns * per

    def next(self, eng):
        self.n += 1
        eng.wait_ge(self.sem, self.at())


class BankWriter:

    def __init__(self, banks, filled, drained):
        self.banks, self.filled, self.drained = banks, Tally(filled), drained

    def open(self, pe):
        n = self.filled.n
        if n >= 4 or self.filled.terms:
            pe.wait_ge(self.drained, self.filled.at(-3))
        return self.banks[n % 4]

    def close(self, ins):
        ins.then_inc(self.filled.sem, 1)
        self.filled.n += 1

    def landed(self, pe):
        pe.wait_ge(self.drained, self.filled.at())


class BankReader:

    def __init__(self, banks, filled, drained):
        self.banks, self.filled, self.drained = banks, Tally(filled), drained

    def take(self, eng):
        bank = self.banks[self.filled.n % 4]
        self.filled.next(eng)
        return bank

    def give(self, ins):
        ins.then_inc(self.drained, 1)


def cond_of(t):
    return 0 if t == 0 else 1


def b_units():
    return [(t, g, pp) for t in range(NT) for g in range(2) for pp in range(2)]


def b_local(t):
    return [0] if t == 0 else [s for s in (t - 1, t, t + 1) if 1 <= s < NT]


def b_keys(t):
    return P if t == 0 else P * (1 + len(b_local(t)))


def c_units():
    return [(t, h) for t in range(NT) for h in range(4)]


def c_keys(t):
    return P if t == 0 else DEC_SEQ + PAST


def a_units():
    out = [(0, 0, 0), (0, 1, 0)]
    for s in range(NT - 1):
        out += [(1, 0, 1 + s), (1, 1, NT - 1 - s)]
    return out


def lam_init(layer):
    return 0.8 - 0.6 * math.exp(-0.3 * layer)


def hybrid_step(nc, io):
    with ExitStack() as ctx:
        def sb(name, shape, dt=F32):
            return ctx.enter_context(nc.sbuf_tensor(name, shape, dt))

        def sem(name):
            return ctx.enter_context(nc.semaphore(name))

        base = -(-nc.sbuf_base // 32) * 32
        AR = sb("AR", [P, ARENA])
        assert nc.sbuf_base == base + 4 * ARENA

        def over(name, shape, at, dt=F32):
            return nc.alloc_sbuf_tensor_at(name, [P] + shape, dt, offset=base + 4 * at)

        def rounded(name, shape, at):
            return over(name, shape, at, F32R)

        X = AR[:, A_X:A_X + NT * D].rearrange("p (t c) -> p t c", t=NT)
        HT = AR[:, A_HT:A_HT + KD * N]
        ROWS = AR[:, A_ROWS:A_ROWS + N_ROWS]
        GB = sb("GB", [P, 2, 2, D])
        CON = sb("CON", [P, N_CONST])
        SM = sb("SM", [P, 1400])
        vbank = [ctx.enter_context(nc.psum_tensor(f"vbank{i}", [P, 512], F32)) for i in range(4)]
        sbank = [ctx.enter_context(nc.psum_tensor(f"sbank{i}", [P, 512], F32)) for i in range(4)]

        small_at = [0]

        def small(n, dt=F32):
            a = small_at[0]
            small_at[0] += n
            assert small_at[0] <= 1400
            return SM[:, a:a + n]

        cond = small(16).rearrange("p (k c) -> p k c", c=2)
        conds = small(16).rearrange("p (k c) -> p k c", c=2)
        ngain = small(16).rearrange("p (w k) -> p w k", w=2)
        mod = small(64).rearrange("p (v k c) -> p v k c", v=4, c=2)
        ssq, root, rinv = small(NT), small(NT), small(NT)
        gss, groot, grinv = (small(NT * 26).rearrange("p (t g) -> p t g", t=NT) for _ in range(3))
        hss, hroot, hrinv = (small(NT * 8).rearrange("p (t g) -> p t g", t=NT) for _ in range(3))
        bmax, bsum, brec = (small(4).rearrange("p (s i) -> p s i", s=2) for _ in range(3))
        cmax, csum, crec = (small(4).rearrange("p (s i) -> p s i", s=2) for _ in range(3))
        lamw = small(64)
        lamv = small(4)
        lf = small(40)
        lft = small(40)
        bci = small(80)
        ci = small(40)
        mstate = small(16).rearrange("p (s d h) -> p s d h", s=2, d=2)
        args = small(40).rearrange("p (s k h) -> p s k h", s=2, k=5)
        mtmp = small(40).rearrange("p (s k h) -> p s k h", s=2, k=5)
        den = small(8).rearrange("p (k h) -> p k h", k=2)

        ident = CON[:, C_ID:C_ID + P]
        ones = CON[:, C_ONE:C_ONE + P]
        eps = CON[:, C_EPS:C_EPS + 1]
        iota = CON[:, C_IOTA:C_IOTA + NK]

        wslot = [AR[:, A_WR + i * WSLOT:A_WR + (i + 1) * WSLOT] for i in range(3)]
        PR = AR[:, A_P:A_P + NT * IN_COLS].rearrange("p (t c) -> p t c", t=NT)
        ada = AR[0:2, A_P:A_P + 6 * D]
        bada = AR[0:2, A_P + 6 * D:A_P + 12 * D]
        MIX = AR[:, A_MIX:A_MIX + NT * D].rearrange("p (t c) -> p t c", t=NT)
        HTk = HT.rearrange("p (k n) -> p k n", k=KD)
        QKT = AR[:, A_WR:A_WR + 13 * N].rearrange("p (b n) -> p b n", b=13)
        W0 = A_WR + 13 * N
        kcb = HT[:, 0:128]
        kcc = HT[:, 128:384].rearrange("p (b n) -> p b n", b=2)
        vcb = HT[:, 384:512]
        vcc = HT[:, 512:768]
        H0 = 768
        SQ = AR[:, W0:W0 + 1152]
        hsq = HT[:, H0:H0 + 512]
        b_s = HT[:, H0:H0 + 2080].rearrange("p (s i n) -> p s i n", s=2, i=2)
        b_et = HT[:, H0 + 2080:H0 + 2080 + 2048].rearrange("p (s i n) -> p s i n", s=2, i=2)
        c_s = HT[:, H0:H0 + 2560].rearrange("p (s i n) -> p s i n", s=2, i=2)
        c_at = HT[:, H0 + 2560:H0 + 2560 + 1280].rearrange("p (s n) -> p s n", s=2)

        def work(a, n):
            return AR[:, W0 + a:W0 + a + n]
        vaug = work(0, 1300).rearrange("p (t h c) -> p t h c", t=NT, h=4)
        cst = work(1300, 520).rearrange("p (s d j c) -> p s d j c", s=2, d=2, j=2)
        nd = work(1820, 260).rearrange("p (h c) -> p h c", h=4)
        wk = work(2080, 256)
        htmp = work(2336, 256).rearrange("p (h c) -> p h c", h=4)
        dg = work(2592, 512).rearrange("p (h s) -> p h s", h=4)
        cm = HT[:, H0:H0 + 512].rearrange("p (h s) -> p h s", h=4)
        pm = HT[:, H0 + 512:H0 + 1024].rearrange("p (h s) -> p h s", h=4)
        pt = HT[:, H0 + 1024:H0 + 1536].rearrange("p (h s) -> p h s", h=4)
        xtmp = AR[:, A_P:A_P + 1024].rearrange("p (s n) -> p s n", s=2)
        HTF = AR[:, A_X:A_X + KD * N].rearrange("p (k n) -> p k n", k=KD)
        HTH, HTL = rounded("HTH", [KD, N], A_HT), rounded("HTL", [KD, N], A_HTL)
        wq_slot = [AR[:, A_WQ + i * WSLOT:A_WQ + (i + 1) * WSLOT] for i in range(2)]
        SC = AR[:, A_SC:A_SC + NT * HC * NK].rearrange("p (t c k) -> p t c k", t=NT, c=HC)
        QT = AR[:, A_QT:A_QT + 2 * N].rearrange("p (s n) -> p s n", s=2)
        SUBT = ROWS[:, 0:2048].rearrange("p (c k) -> p c k", c=HC)
        IGT = [ROWS[:, i * N:(i + 1) * N] for i in range(3)]
        o = A_X
        val = AR[:, o:o + 256].rearrange("p (c k) -> p c k", c=HC)
        idx = AR[:, o + 256:o + 512].bitcast(U32).rearrange("p (c k) -> p c k", c=HC)
        cand = AR[:, o + 512:o + 2560].rearrange("p (h a b) -> p h a b", h=HEADS, a=TOPK)
        eq = AR[:, o + 2560:o + 4608]
        idxf = AR[:, o + 4608:o + 4864].rearrange("p (h c k) -> p h c k", h=HEADS, c=2)
        tops = AR[:, o + 4864:o + 4992].rearrange("p (h k) -> p h k", h=HEADS)
        gate = AR[:, o + 4992:o + 5120].rearrange("p (h k) -> p h k", h=HEADS)
        o = 5 * N
        pflat = ROWS[:, o:o + 128].bitcast(U32)
        posu = pflat.rearrange("p (h k) -> p h k", h=HEADS)
        pab = [ROWS[:, o + 128:o + 256].bitcast(U32), ROWS[:, o + 256:o + 384].bitcast(U32)]
        pabf = [ROWS[:, o + 384:o + 512], ROWS[:, o + 512:o + 640]]
        sel = [ROWS[:, o + 640:o + 768], ROWS[:, o + 768:o + 896]]
        gsum = ROWS[:, o + 896:o + 904]
        grec = ROWS[:, o + 904:o + 912]
        UR = [AR[:, A_UR + i * 1024:A_UR + (i + 1) * 1024].rearrange("p (k e) -> p k e", k=KD) for i in range(2)]
        UH, UL = rounded("UH", [2, KD, P], A_UH), rounded("UL", [2, KD, P], A_UL)
        GE = AR[:, A_GE:A_GE + 2 * N].rearrange("p (s n) -> p s n", s=2)
        OH = AR[:, A_X:A_X + 4096].rearrange("p (s t k n) -> p s t k n", s=4, t=4, k=2)
        GS = [AR[:, a:a + NK * GT].rearrange("p (b t) -> p b t", b=NK) for a in A_GS]
        VR = [over(f"VR{i}", [D], a) for i, a in enumerate(A_VR)]
        TMP = [AR[:, A_TMP + i * N:A_TMP + (i + 1) * N] for i in range(2)]
        HB = [AR[:, A_HB + i * N:A_HB + (i + 1) * N] for i in range(GROUP)]
        GG = [AR[:, A_GG + i * GROUP * N:A_GG + (i + 1) * GROUP * N]
              .rearrange("p (h b t) -> p h b t", h=N // GT, b=GROUP) for i in range(2)]
        VH, VL = rounded("VH", [2 * GROUP, D], A_VH), rounded("VL", [2 * GROUP, D], A_VL)
        HWH, HWL = rounded("HWH", [2 * GROUP, N], A_HWH), rounded("HWL", [2 * GROUP, N], A_HWL)
        ACC = AR[:, A_MIX:A_MIX + NT * D].rearrange("p (t c) -> p t c", t=NT)

        vec_filled, vec_drained = sem("vec_filled"), sem("vec_drained")
        sca_filled, sca_drained = sem("sca_filled"), sem("sca_drained")
        phase_done = sem("phase_done")
        setup_in = sem("setup_in")
        vectors_in = sem("vectors_in")
        slice_in = [sem(f"slice_in{i}") for i in range(3)]
        cond_ready = sem("cond_ready")
        ada_rows = sem("ada_rows")
        mod_ready = sem("mod_ready")
        x_ready = sem("x_ready")
        roots_ready = sem("roots_ready")
        xn_ready = sem("xn_ready")
        group_squares = sem("group_squares")
        group_roots = sem("group_roots")
        qk_ready = sem("qk_ready")
        caches_in = sem("caches_in")
        b_scores = sem("b_scores")
        b_exps = sem("b_exps")
        c_scores = sem("c_scores")
        c_exps = sem("c_exps")
        c_weights = sem("c_weights")
        gates_signed = sem("gates_signed")
        softplus_ready = sem("softplus_ready")
        log_f_ready = sem("log_f_ready")
        diag_ready = sem("diag_ready")
        ml_args = sem("ml_args")
        ml_exps = sem("ml_exps")
        ml_products = sem("ml_products")
        state_final = sem("state_final")
        head_squares = sem("head_squares")
        head_roots = sem("head_roots")
        lam_dots = sem("lam_dots")
        lam_exps = sem("lam_exps")
        mix_ready = sem("mix_ready")
        subkeys_in = sem("subkeys_in")
        tops_ready = sem("tops_ready")
        top_exps = sem("top_exps")
        picks_ready = sem("picks_ready")
        onehot_ready = sem("onehot_ready")
        gates_stored = [sem(f"gates_stored{i}") for i in range(2)]
        wq_in = [sem(f"wq_in{i}") for i in range(2)]
        x_spilled = sem("x_spilled")
        x_back = sem("x_back")
        turned_ready = sem("turned_ready")
        split_ready = sem("split_ready")
        u_in = [sem(f"u_in{i}") for i in range(2)]
        u_split = sem("u_split")
        u_high = sem("u_high")
        v_high = sem("v_high")
        hidden_stored = [sem(f"hidden_stored{i}") for i in range(2)]
        v_in = [sem(f"v_in{i}") for i in range(4)]
        v_split = sem("v_split")
        hidden_in = [sem(f"hidden_in{i}") for i in range(GROUP)]
        gates_in = [sem(f"gates_in{i}") for i in range(2)]
        gated_ready = sem("gated_ready")
        high_ready = sem("high_ready")
        low_ready = sem("low_ready")
        x_final = sem("x_final")
        out_done = sem("out_done")

        slice_read = []
        loop_base = {}
        wq_read = []

        block = ctx.enter_context(nc.Block())

        @block.tensor
        def _(pe):
            V = BankWriter(vbank, vec_filled, vec_drained)
            S = BankWriter(sbank, sca_filled, sca_drained)
            slices = [0, 0, 0]
            n_slice = [0]
            phase = [0]

            def barrier():
                phase[0] += 1
                pe.drain().then_inc(phase_done, 1)
                pe.wait_ge(phase_done, 3 * phase[0])

            def next_slice():
                i = n_slice[0] % 3
                n_slice[0] += 1
                slices[i] += 16
                pe.wait_ge(slice_in[i], slices[i])
                return wslot[i]

            def slice_done(w):
                slice_read.append((w.filled.sem, w.filled.n))

            def transposed_norm():
                for t in range(NT):
                    xn_t.next(pe)
                    for half in range(2):
                        ps = S.open(pe)
                        for j in range(4):
                            k = 4 * half + j
                            ins = pe.transpose(ps[:, j * P:(j + 1) * P], MIX[:, t, k * P:(k + 1) * P], ident)
                        S.close(ins)

            xn_t, qk_t, be_t, cw_t = Tally(xn_ready), Tally(qk_ready), Tally(b_exps), Tally(c_weights)
            ada_t, lf_t, dg_t, mp_t = Tally(ada_rows), Tally(log_f_ready), Tally(diag_ready), Tally(ml_products)
            mix_t, pk_t, oh_t, low_t = Tally(mix_ready), Tally(picks_ready), Tally(onehot_ready), Tally(low_ready)
            us_t, vs_t, sp_t = Tally(u_split, 2), Tally(v_split, 4), Tally(split_ready)
            wq_t = [Tally(s) for s in wq_in]

            def hidden_block(b):
                us_t.next(pe)
                for j in range(2):
                    cols = slice(j * HALF, (j + 1) * HALF)
                    ps = S.open(pe)[:, 0:HALF]
                    for k in range(KD):
                        pe.matmul(ps, UH[:, b, k, :], HTH[:, k, cols], start=(k == 0), stop=False)
                        pe.matmul(ps, UH[:, b, k, :], HTL[:, k, cols], start=False, stop=False)
                        ins = pe.matmul(ps, UL[:, b, k, :], HTH[:, k, cols], start=False, stop=(k == KD - 1))
                    S.close(ins)

            def hidden_loop(turns):
                with pe.Fori(0, turns) as j:
                    S.filled.enter(j, 4)
                    us_t.enter(j, 2)
                    for b in range(2):
                        hidden_block(b)
                    S.filled.leave(turns)
                    us_t.leave(turns)

            pe.wait_ge(setup_in, 16 * 4)
            pe.wait_ge(cond_ready, 1)

            for layer in range(DEPTH):
                for n in range(ADA_SLICES):
                    w = next_slice().rearrange("p (k n) -> p k n", k=KD)
                    ps = V.open(pe)
                    for k in range(KD):
                        ins = pe.matmul(ps[0:2, :], conds[:, k, :], w[:, k, :], start=(k == 0), stop=(k == KD - 1))
                    V.close(ins)
                    slice_done(V)
                ada_t.next(pe)
                ps = V.open(pe)
                for v, vec in enumerate((0, 1, 3, 4)):
                    for k in range(KD):
                        a = vec * D + k * P
                        ins = pe.transpose(ps[:, (v * KD + k) * 2:(v * KD + k) * 2 + 2], ada[:, a:a + P], ident[0:2, 0:2])
                V.close(ins)
                for vec in (2, 5):
                    for c in range(2):
                        for half in range(2):
                            ps = S.open(pe)
                            a = vec * D + half * 512
                            S.close(pe.matmul(ps[:, :], CON[0:2, C_SEL + c * P:C_SEL + (c + 1) * P], ada[:, a:a + 512],
                                              start=True, stop=True))
                transposed_norm()
                S.landed(pe)
                for n in range(IN_SLICES):
                    w = next_slice()[:, 0:KD * IN_W].rearrange("p (k n) -> p k n", k=KD)
                    for t in range(NT):
                        ps = V.open(pe)
                        for k in range(KD):
                            ins = pe.matmul(ps[:, 0:IN_W], HTk[:, k, t * P:(t + 1) * P], w[:, k, :],
                                            start=(k == 0), stop=(k == KD - 1))
                        V.close(ins)
                    slice_done(V)
                barrier()

                cols = [BQ + P * i for i in range(4)] + [BK, CQ, CQ + P, CK, CK + P, AQ, AQ + P, AK, AK + P]
                for t in range(NT):
                    qk_t.next(pe)
                    for b0 in range(0, 13, 4):
                        ps = S.open(pe)
                        for b in range(b0, min(b0 + 4, 13)):
                            ins = pe.transpose(ps[:, (b - b0) * P:(b - b0 + 1) * P], PR[:, t, cols[b]:cols[b] + P], ident)
                        S.close(ins)
                S.landed(pe)
                pe.wait_ge(caches_in, 96 * (layer + 1))

                units = b_units()

                def scores(u):
                    t, g, pp = units[u]
                    r = slice(64 * g, 64 * g + 64)
                    for i in range(2):
                        ps = V.open(pe)
                        q = QKT[r, 2 * pp + i, t * P:(t + 1) * P]
                        if t == 0:
                            ins = pe.matmul(ps[:, 0:P], q, QKT[r, 4, 0:P], start=True, stop=True)
                        else:
                            loc = b_local(t)
                            pe.matmul(ps[:, 0:P], q, kcb[r, :], start=True, stop=True)
                            ins = pe.matmul(ps[:, P:P + P * len(loc)], q, QKT[r, 4, loc[0] * P:(loc[-1] + 1) * P],
                                            start=True, stop=True)
                        V.close(ins)

                def mixed(u):
                    t, g, pp = units[u]
                    nb = b_keys(t) // P
                    be_t.next(pe)
                    for i in range(2):
                        ps = S.open(pe)
                        for b in range(nb):
                            ins = pe.transpose(ps[:, b * P:(b + 1) * P], b_s[:, u % 2, i, b * P:(b + 1) * P], ident)
                        S.close(ins)
                    S.landed(pe)
                    ps = V.open(pe)
                    for i in range(2):
                        for b in range(nb):
                            if t == 0:
                                v = PR[:, 0, BV + 64 * g:BV + 64 * g + 64]
                            elif b == 0:
                                v = vcb[:, 64 * g:64 * g + 64]
                            else:
                                v = PR[:, b_local(t)[b - 1], BV + 64 * g:BV + 64 * g + 64]
                            ins = pe.matmul(ps[:, 64 * i:64 * i + 64], b_et[:, u % 2, i, b * P:(b + 1) * P], v,
                                            start=(b == 0), stop=(b == nb - 1))
                    V.close(ins)

                scores(0)
                for u in range(len(units)):
                    if u + 1 < len(units):
                        scores(u + 1)
                    mixed(u)
                barrier()

                cu = c_units()

                def c_score(u):
                    t, h = cu[u]

                    def qk(c):
                        g = 2 * h + c
                        r = slice(32 * (g % 4), 32 * (g % 4) + 32)
                        return r, QKT[r, 5 + g // 4, t * P:(t + 1) * P], 7 + g // 4, g // 4
                    if t == 0:
                        for c in range(2):
                            ps = V.open(pe)
                            r, q, kb, _ = qk(c)
                            V.close(pe.matmul(ps[:, 0:P], q, QKT[r, kb, 0:P], start=True, stop=True))
                        return
                    for c in range(2):
                        ps = V.open(pe)
                        r, q, kb, _ = qk(c)
                        V.close(pe.matmul(ps[:, :], q, QKT[r, kb, P:N], start=True, stop=True))
                    for c in range(2):
                        ps = V.open(pe)
                        r, q, _, kc = qk(c)
                        V.close(pe.matmul(ps[:, 0:P], q, kcc[r, kc, :], start=True, stop=True))

                def c_mixed(u):
                    t, h = cu[u]
                    nb = c_keys(t) // P
                    cw_t.next(pe)
                    for b0 in range(0, nb, 4):
                        ps = S.open(pe)
                        for b in range(b0, min(b0 + 4, nb)):
                            ins = pe.transpose(ps[:, (b - b0) * P:(b - b0 + 1) * P],
                                               c_s[:, u % 2, 0, b * P:(b + 1) * P], ident)
                        S.close(ins)
                    S.landed(pe)
                    ps = V.open(pe)
                    for b in range(nb):
                        if b == 4:
                            v = vcc[:, 64 * h:64 * h + 64]
                        else:
                            v = PR[:, 0 if t == 0 else 1 + b, CV + 64 * h:CV + 64 * h + 64]
                        ins = pe.matmul(ps[:, 0:64], c_at[:, u % 2, b * P:(b + 1) * P], v,
                                        start=(b == 0), stop=(b == nb - 1))
                    V.close(ins)

                c_score(0)
                for u in range(len(cu)):
                    if u + 1 < len(cu):
                        c_score(u + 1)
                    c_mixed(u)
                barrier()

                lf_t.next(pe)
                ps = V.open(pe)
                pe.matmul(ps[:, 0:20], CON[:, C_TRIF:C_TRIF + P], lf[:, 0:20], start=True, stop=True)
                pe.matmul(ps[:, 20:40], CON[:, C_TRIB:C_TRIB + P], lf[:, 20:40], start=True, stop=True)
                V.close(pe.matmul(ps[:, 40:80], ones, lf[:, :], start=True, stop=True))
                for seg, d, t in a_units():
                    dg_t.next(pe)
                    ps = V.open(pe)
                    V.close(pe.matmul(ps[:, :], ones, dg[:, :, :].rearrange("p h s -> p (h s)"), start=True, stop=True))
                    for odd in range(2):
                        ps = V.open(pe)
                        r = slice(64 * odd, 64 * odd + 64)
                        for j in range(2):
                            ins = pe.matmul(ps[:, j * P:(j + 1) * P], QKT[r, 9 + j, t * P:(t + 1) * P],
                                            QKT[r, 11 + j, t * P:(t + 1) * P], start=True, stop=True)
                        V.close(ins)
                    mp_t.next(pe)
                    ps = S.open(pe)
                    for h in range(4):
                        ins = pe.transpose(ps[:, h * P:(h + 1) * P], pm[:, h, :], ident)
                    S.close(ins)
                    for odd in range(2):
                        ps = V.open(pe)
                        r = slice(64 * odd, 64 * odd + 64)
                        for j in range(2):
                            ins = pe.matmul(ps[:, j * 65:(j + 1) * 65], QKT[r, 9 + j, t * P:(t + 1) * P],
                                            cst[r, seg, d, j, :], start=True, stop=True)
                        V.close(ins)
                    ps = V.open(pe)
                    for j in range(2):
                        ins = pe.matmul(ps[:, j * 130:(j + 1) * 130], wk[:, j * P:(j + 1) * P],
                                        vaug[:, t, 2 * j:2 * j + 2, :].rearrange("p h c -> p (h c)"),
                                        start=True, stop=True)
                    V.close(ins)
                    S.landed(pe)
                    ps = V.open(pe)
                    for h in range(4):
                        ins = pe.matmul(ps[:, h * 65:(h + 1) * 65], pt[:, h, :], vaug[:, t, h, :], start=True, stop=True)
                    V.close(ins)
                barrier()

                for t in range(NT):
                    if t == 0:
                        mix_t.next(pe)
                    for half in range(2):
                        ps = S.open(pe)
                        for j in range(4):
                            k = 4 * half + j
                            ins = pe.transpose(ps[:, j * P:(j + 1) * P], MIX[:, t, k * P:(k + 1) * P], ident)
                        S.close(ins)
                S.landed(pe)
                for n in range(2):
                    w = next_slice().rearrange("p (k n) -> p k n", k=KD)
                    for t in range(NT):
                        ps = V.open(pe)
                        for k in range(KD):
                            ins = pe.matmul(ps[:, :], HTk[:, k, t * P:(t + 1) * P], w[:, k, :],
                                            start=(k == 0), stop=(k == KD - 1))
                        V.close(ins)
                    slice_done(V)
                transposed_norm()
                S.landed(pe)
                wq_read.append([])

                pe.wait_ge(subkeys_in, 16 * (layer + 1))
                w = None

                def query(c, w):
                    for j in range(2):
                        ps = S.open(pe)
                        for k in range(KD):
                            ins = pe.matmul(ps[:, 0:HALF], w[:, c % 4, k, :], HTF[:, k, j * HALF:(j + 1) * HALF],
                                            start=(k == 0), stop=(k == KD - 1))
                        S.close(ins)
                    return S.filled.n

                def key_scores(c, after):
                    pe.wait_ge(sca_drained, after)
                    for t0 in (0, 4):
                        ps = S.open(pe)
                        for t in range(t0, min(t0 + 4, NT)):
                            ins = pe.matmul(ps[:, (t - t0) * P:(t - t0 + 1) * P], QT[:, c % 2, t * P:(t + 1) * P],
                                            SUBT[:, c, :], start=True, stop=True)
                        S.close(ins)

                after = 0
                for c in range(HC + 1):
                    was = after
                    if c < HC:
                        if c % 4 == 0:
                            i = c // 4 % 2
                            wq_t[i].n += 16
                            pe.wait_ge(wq_in[i], wq_t[i].n)
                            w = wq_slot[i].rearrange("p (c k n) -> p c k n", c=4, k=KD)
                        after = query(c, w)
                        if c % 4 == 3:
                            wq_read[-1].append(S.filled.n)
                    if c >= 1:
                        key_scores(c - 1, was)
                barrier()

                sp_t.next(pe)
                for t in range(NT):
                    hidden_loop(PICK_BLOCKS // 2)
                    pk_t.next(pe)
                    ps = V.open(pe)
                    pe.transpose(ps[:, 0:P], sel[0], ident)
                    pe.transpose(ps[:, P:2 * P], sel[1], ident)
                    V.close(pe.transpose(ps[:, 2 * P:3 * P], gate.rearrange("p h k -> p (h k)"), ident))
                barrier()

                turns, inner = N // (2 * GT), GT // TOK
                loop_base["gate", layer] = S.filled.n
                with pe.Fori(0, turns) as i:
                    S.filled.enter(i, 16 * inner)
                    us_t.enter(i, 4 * inner)
                    oh_t.enter(i, 8 * inner)
                    for slot in range(2):
                        with pe.Fori(0, inner) as j:
                            S.filled.enter(j, 8)
                            us_t.enter(j, 2)
                            oh_t.enter(j, 4)
                            for b in range(2):
                                hidden_block(b)
                            for b in range(4):
                                oh_t.next(pe)
                                ps = S.open(pe)
                                for q in range(4):
                                    ins = pe.matmul(ps[:, q * P:(q + 1) * P], OH[:, b, q, 1, :], OH[:, b, q, 0, :],
                                                    start=True, stop=True)
                                S.close(ins)
                            for x in (S.filled, us_t, oh_t):
                                x.leave(inner)
                    for x in (S.filled, us_t, oh_t):
                        x.leave(turns)
                hidden_loop((NK - NT * PICK_BLOCKS - 2 * N // TOK) // 2)
                barrier()

                steps = NK // (2 * GROUP)
                loop_base["out", layer] = V.filled.n
                with pe.Fori(0, steps) as i:
                    V.filled.enter(i, 4 * NT)
                    vs_t.enter(i, 2 * GROUP)
                    low_t.enter(i, 2 * GROUP)
                    for g in range(2):
                        for _ in range(GROUP):
                            vs_t.next(pe)
                            low_t.next(pe)
                        for t in range(NT):
                            for ch in range(2):
                                ps = V.open(pe)
                                for b in range(GROUP * g, GROUP * (g + 1)):
                                    rows, cols = slice(t * P, (t + 1) * P), slice(ch * 512, (ch + 1) * 512)
                                    first, last = b == GROUP * g, b == GROUP * (g + 1) - 1
                                    pe.matmul(ps[:, :], HWH[:, b, rows], VH[:, b, cols], start=first, stop=False)
                                    pe.matmul(ps[:, :], HWH[:, b, rows], VL[:, b, cols], start=False, stop=False)
                                    ins = pe.matmul(ps[:, :], HWL[:, b, rows], VH[:, b, cols], start=False, stop=last)
                                V.close(ins)
                    for x in (V.filled, vs_t, low_t):
                        x.leave(steps)
                barrier()

        @block.vector
        def _(v):
            V = BankReader(vbank, vec_filled, vec_drained)
            phase = [0]
            rt_t, gr_t, sp_t, le_t = Tally(roots_ready), Tally(group_roots), Tally(softplus_ready), Tally(lam_exps)
            ce_t, be_t, me_t, hr_t = Tally(c_exps), Tally(b_exps), Tally(ml_exps), Tally(head_roots)
            te_t = Tally(top_exps)
            hi_t, in_t, gi_t = Tally(high_ready), [Tally(s) for s in hidden_in], [Tally(s) for s in gates_in]
            ht_t, vx_t = Tally(turned_ready), Tally(x_back)

            def barrier():
                phase[0] += 1
                v.drain().then_inc(phase_done, 1)
                v.wait_ge(phase_done, 3 * phase[0])

            def tt(out, a, b, op):
                return v.tensor_tensor(out, a, b, op)

            def normed():
                rt_t.next(v)
                v.reciprocal(rinv[:, :], root[:, :])
                v.drain()
                for t in range(NT):
                    v.tensor_scalar(MIX[:, t, :], X[:, t, :], rinv[:, t:t + 1], None, ALU.mult).then_inc(xn_ready, 1)

            v.wait_ge(setup_in, 16 * 4)

            for layer in range(DEPTH):
                v.wait_ge(vectors_in, 48 * (layer + 1))
                for n in range(ADA_SLICES):
                    ps = V.take(v)
                    V.give(tt(ada[:, n * 512:(n + 1) * 512], ps[0:2, :], bada[:, n * 512:(n + 1) * 512], ALU.add))
                v.drain().then_inc(ada_rows, 1)
                ps = V.take(v)
                for w in range(2):
                    cols = ps[:, w * 32:(w + 1) * 32].rearrange("p (v k c) -> p v k c", v=2, c=2)
                    v.tensor_copy(mod[:, 2 * w, :, :], cols[:, 0])
                    ins = v.scalar_tensor_tensor(mod[:, 2 * w + 1, :, :], cols[:, 1], 1.0,
                                                 ngain[:, w, :].unsqueeze(2).broadcast_to([P, KD, 2]), ALU.add, ALU.mult)
                V.give(ins)
                v.drain().then_inc(mod_ready, 1)
                normed()
                for n in range(IN_SLICES):
                    for t in range(NT):
                        ps = V.take(v)
                        V.give(tt(PR[:, t, n * IN_W:(n + 1) * IN_W], ps[:, 0:IN_W],
                                  ROWS[:, R_BIN + n * IN_W:R_BIN + (n + 1) * IN_W], ALU.add))
                barrier()

                for t in range(NT):
                    tt(SQ[:, 0:640], PR[:, t, BQ:BQ + 640], PR[:, t, BQ:BQ + 640], ALU.mult)
                    tt(SQ[:, 640:1152], PR[:, t, CQ:CQ + 512], PR[:, t, CQ:CQ + 512], ALU.mult)
                    v.drain()
                    v.tensor_reduce(gss[:, t, 0:10], SQ[:, 0:640].rearrange("p (g c) -> p g c", c=64), AX_X, ALU.add)
                    v.tensor_reduce(gss[:, t, 10:26], SQ[:, 640:1152].rearrange("p (g c) -> p g c", c=32), AX_X, ALU.add)
                    v.drain()
                v.drain().then_inc(group_squares, 1)
                lam = ROWS[:, R_LAM:R_LAM + 128].rearrange("p (a b c) -> p a b c", a=2, b=2)
                tt(lamw[:, :].rearrange("p (a c) -> p a c", a=2), lam[:, :, 0, :], lam[:, :, 1, :], ALU.mult)
                v.drain()
                v.tensor_reduce(lamv[:, 0:2], lamw[:, :].rearrange("p (a c) -> p a c", a=2), AX_X, ALU.add)
                v.drain().then_inc(lam_dots, 1)
                le_t.next(v)
                tt(lamv[:, 2:3], lamv[:, 1:2], lamv[:, 0:1], ALU.subtract)
                v.drain()
                v.tensor_scalar(lamv[:, 3:4], lamv[:, 2:3], lam_init(layer), None, ALU.subtract)
                gr_t.next(v)
                v.reciprocal(grinv[:, :, :], groot[:, :, :])
                v.drain()
                for t in range(NT):
                    qb = PR[:, t, BQ:BQ + 640].rearrange("p (g c) -> p g c", c=64)
                    qc = PR[:, t, CQ:CQ + 512].rearrange("p (g c) -> p g c", c=32)
                    tt(qb, qb, grinv[:, t, 0:10].unsqueeze(2).broadcast_to([P, 10, 64]), ALU.mult)
                    tt(qc, qc, grinv[:, t, 10:26].unsqueeze(2).broadcast_to([P, 16, 32]), ALU.mult)
                    v.drain()
                    tt(PR[:, t, BQ:BQ + 640], PR[:, t, BQ:BQ + 640], ROWS[:, R_GB:R_GB + 640], ALU.mult)
                    tt(PR[:, t, CQ:CQ + 512], PR[:, t, CQ:CQ + 512], ROWS[:, R_GC:R_GC + 512], ALU.mult)
                    v.drain()
                    if t > 0:
                        for at, ng, q, tab in ((BQ, B_GROUPS, 16, C_RB), (CQ, C_GROUPS, 8, C_RC)):
                            n = ng * 4 * q
                            x4 = PR[:, t, at:at + n].rearrange("p (g a b q) -> p g a b q", a=2, b=2, q=q)
                            h1, h2 = x4[:, :, :, 0, :], x4[:, :, :, 1, :]

                            def table(k):
                                a = tab + k * 4 * 2 * q + (t - 1) * 2 * q
                                return CON[:, a:a + 2 * q].rearrange("p (a q) -> p a q", a=2).unsqueeze(1)\
                                    .broadcast_to([P, ng, 2, q])
                            tmp = [AR[:, W0 + i * 320:W0 + i * 320 + n // 2].rearrange("p (g a q) -> p g a q", a=2, q=q)
                                   for i in range(4)]
                            tt(tmp[0], h1, table(0), ALU.mult)
                            tt(tmp[1], h2, table(1), ALU.mult)
                            tt(tmp[2], h2, table(0), ALU.mult)
                            tt(tmp[3], h1, table(1), ALU.mult)
                            v.drain()
                            tt(h1, tmp[0], tmp[1], ALU.subtract)
                            tt(h2, tmp[2], tmp[3], ALU.add)
                            v.drain()
                    v.drain().then_inc(qk_ready, 1)

                units = b_units()

                def prep(u):
                    t, g, pp = units[u]
                    nk = b_keys(t)
                    s = b_s[:, u % 2]
                    h = 4 * g + 2 * pp
                    band = CON[:, C_BAND1:C_BAND1 + nk] if t == 1 else CON[:, C_BAND:C_BAND + nk]
                    v.tensor_scalar(s[:, :, nk:nk + 1], ROWS[:, R_SINK + h:R_SINK + h + 2].unsqueeze(2), 8.0, None, ALU.mult)
                    for i in range(2):
                        ps = V.take(v)
                        if t == 0:
                            V.give(v.tensor_copy(s[:, i, 0:nk], ps[:, 0:nk]))
                        else:
                            V.give(tt(s[:, i, 0:nk], ps[:, 0:nk], band, ALU.add))
                    v.drain()
                    v.tensor_reduce(bmax[:, u % 2, :], s[:, :, 0:nk + 1], AX_X, ALU.max)
                    v.drain()
                    v.tensor_scalar(bmax[:, u % 2, :], bmax[:, u % 2, :], -0.125, None, ALU.mult).then_inc(b_scores, 1)

                def finish(u):
                    t, g, pp = units[u]
                    h = 4 * g + 2 * pp
                    be_t.next(v)
                    v.reciprocal(brec[:, u % 2, :], bsum[:, u % 2, :])
                    v.drain()
                    ps = V.take(v)
                    V.give(tt(MIX[:, t, MB + 64 * h:MB + 64 * h + 128].rearrange("p (i c) -> p i c", i=2),
                              ps[:, 0:128].rearrange("p (i c) -> p i c", i=2),
                              brec[:, u % 2, :].unsqueeze(2).broadcast_to([P, 2, 64]), ALU.mult))

                prep(0)
                for u in range(len(units)):
                    if u + 1 < len(units):
                        prep(u + 1)
                    finish(u)
                barrier()

                cu = c_units()

                def c_prep(u):
                    t, h = cu[u]
                    s = c_s[:, u % 2]
                    nk = c_keys(t)
                    for k0 in range(0, nk, 512):
                        n = min(512, nk - k0)
                        for c in range(2):
                            ps = V.take(v)
                            V.give(v.tensor_copy(s[:, c, k0:k0 + n], ps[:, 0:n]))
                    v.drain()
                    v.tensor_reduce(cmax[:, u % 2, :], s[:, :, 0:nk], AX_X, ALU.max)
                    v.drain()
                    v.tensor_scalar(cmax[:, u % 2, :], cmax[:, u % 2, :], -(32 ** -0.5), None, ALU.mult)\
                        .then_inc(c_scores, 1)

                def c_mid(u):
                    t, h = cu[u]
                    s = c_s[:, u % 2]
                    nk = c_keys(t)
                    ce_t.next(v)
                    v.reciprocal(crec[:, u % 2, :], csum[:, u % 2, :])
                    v.drain()
                    tt(crec[:, u % 2, 1:2], crec[:, u % 2, 1:2], lamv[:, 3:4], ALU.mult)
                    v.tensor_scalar(s[:, 0, 0:nk], s[:, 0, 0:nk], crec[:, u % 2, 0:1], None, ALU.mult)
                    v.drain()
                    v.scalar_tensor_tensor(s[:, 0, 0:nk], s[:, 1, 0:nk], crec[:, u % 2, 1:2], s[:, 0, 0:nk],
                                           ALU.mult, ALU.add).then_inc(c_weights, 1)

                def c_finish(u):
                    t, h = cu[u]
                    ps = V.take(v)
                    V.give(v.tensor_copy(MIX[:, t, MC + 64 * h:MC + 64 * h + 64], ps[:, 0:64]))

                c_prep(0)
                for u in range(len(cu)):
                    if u + 1 < len(cu):
                        c_prep(u + 1)
                    c_mid(u)
                    c_finish(u)
                barrier()

                gview = PR[:, :, AG:AG + 16].rearrange("p t (d x h) -> p d x t h", d=2, x=2)

                def dth(ap):
                    return ap.rearrange("p (d t h) -> p d t h", d=2, t=NT)
                for d in range(2):
                    v.tensor_scalar(dth(lft[:, :])[:, d], gview[:, d, 1], -1.0, None, ALU.mult)
                v.drain()
                for d in range(2):
                    tt(dth(lft[:, :])[:, d], dth(lft[:, :])[:, d], gview[:, d, 1], ALU.min)
                v.drain().then_inc(gates_signed, 1)
                for d in range(2):
                    v.tensor_scalar(dth(lf[:, :])[:, d], gview[:, d, 1], 0.0, None, ALU.min)
                v.memset(vaug[:, :, :, 64:65], 1.0)
                for t in range(NT):
                    v.tensor_copy(vaug[:, t, :, 0:64], PR[:, t, AV:AV + 256].rearrange("p (h c) -> p h c", h=4))
                v.memset(cst[:, 0], 0.0)
                v.memset(mstate[:, 0], 0.0)
                sp_t.next(v)
                v.drain()
                tt(lf[:, :], lf[:, :], lft[:, :], ALU.subtract)
                v.drain().then_inc(log_f_ready, 1)
                ps = V.take(v)
                V.give(v.tensor_copy(bci[:, :], ps[:, 0:80]))
                v.drain()
                for d in range(2):
                    tt(dth(ci[:, :])[:, d], gview[:, d, 0], dth(bci[:, 0:40])[:, d], ALU.subtract)
                v.drain()
                bc, bl, cc = dth(bci[:, 0:40]), dth(bci[:, 40:80]), dth(ci[:, :])
                seen = set()
                for seg, d, t in a_units():
                    m = mstate[:, seg, d, :]
                    mask = CON[:, (C_MF, C_MB)[d]:(C_MF, C_MB)[d] + P]
                    ar, mt = args[:, 0], mtmp[:, 0]
                    tt(dg[:, :, :], ident.unsqueeze(1).broadcast_to([P, 4, P]),
                       cc[:, d, t, :].unsqueeze(2).broadcast_to([P, 4, P]), ALU.mult).then_inc(diag_ready, 1)
                    ps = V.take(v)
                    tt(cm[:, :, :], ps[:, :].rearrange("p (h s) -> p h s", h=4),
                       mask.unsqueeze(1).broadcast_to([P, 4, P]), ALU.add)
                    V.give(v.tensor_reduce(mt[:, 0, :], ps[:, :].rearrange("p (h s) -> p h s", h=4), AX_X, ALU.max))
                    v.drain()
                    v.tensor_reduce(mt[:, 1, :], cm[:, :, :], AX_X, ALU.max)
                    tt(mt[:, 2, :], mt[:, 0, :], m, ALU.max)
                    v.drain()
                    tt(mt[:, 3, :], mt[:, 1, :], m, ALU.max)
                    tt(ar[:, 1, :], m, mt[:, 2, :], ALU.subtract)
                    tt(ar[:, 2, :], cc[:, d, t, :], mt[:, 2, :], ALU.subtract)
                    v.drain()
                    tt(ar[:, 0, :], m, mt[:, 3, :], ALU.subtract)
                    tt(mt[:, 4, :], bc[:, d, t, :], mt[:, 3, :], ALU.add)
                    v.tensor_scalar(ar[:, 4, :], mt[:, 3, :], -1.0, None, ALU.mult)
                    v.drain()
                    v.tensor_scalar(ar[:, 3, :], mt[:, 4, :], -1.0, None, ALU.mult)
                    tt(m, bl[:, d, t, :], mt[:, 2, :], ALU.add)
                    v.drain().then_inc(ml_args, 1)
                    me_t.next(v)
                    for odd in range(2):
                        ps = V.take(v)
                        V.give(v.scalar_tensor_tensor(pm[:, odd::2, :], ps[:, 0:256].rearrange("p (j s) -> p j s", j=2),
                                                      0.125, cm[:, odd::2, :], ALU.mult, ALU.mult))
                    v.scalar_tensor_tensor(wk[:, :].rearrange("p (h c) -> p h c", h=4),
                                           PR[:, t, AK:AK + 256].rearrange("p (h c) -> p h c", h=4), 0.125,
                                           ar[:, 2, :].unsqueeze(2).broadcast_to([P, 4, 64]), ALU.mult, ALU.mult)
                    v.drain().then_inc(ml_products, 1)
                    for odd in range(2):
                        ps = V.take(v)
                        V.give(tt(nd[:, odd::2, :], ps[:, 0:130].rearrange("p (j c) -> p j c", j=2),
                                  ar[:, 0, odd::2].unsqueeze(2).broadcast_to([P, 2, 65]), ALU.mult))
                    ps = V.take(v)
                    for h in range(4):
                        r = slice(64 * (h % 2), 64 * (h % 2) + 64)
                        st = cst[r, seg, d, h // 2, :]
                        ins = v.scalar_tensor_tensor(st, st, ar[r, 1, h:h + 1], ps[r, h * 65:(h + 1) * 65],
                                                     ALU.mult, ALU.add)
                    V.give(ins)
                    v.drain()
                    ps = V.take(v)
                    V.give(tt(nd[:, :, :], nd[:, :, :], ps[:, 0:260].rearrange("p (h c) -> p h c", h=4), ALU.add))
                    v.drain()
                    dn = nd[:, :, 64:65]
                    d0, d1 = den[:, 0, :].unsqueeze(2), den[:, 1, :].unsqueeze(2)
                    v.tensor_scalar(d0, dn, -1.0, None, ALU.mult)
                    v.drain()
                    tt(d0, d0, dn, ALU.max)
                    v.drain()
                    tt(d0, d0, ar[:, 3, :].unsqueeze(2), ALU.max)
                    v.drain()
                    v.reciprocal(d1, d0)
                    v.drain()
                    dst = MIX[:, t, MA:MA + 256].rearrange("p (h c) -> p h c", h=4)
                    rec = den[:, 1, :].unsqueeze(2).broadcast_to([P, 4, 64])
                    if t not in seen:
                        seen.add(t)
                        tt(dst, nd[:, :, 0:64], rec, ALU.mult)
                    else:
                        tt(htmp[:, :, :], nd[:, :, 0:64], rec, ALU.mult)
                        v.drain()
                        tt(dst, dst, htmp[:, :, :], ALU.add)
                    v.drain()
                    if (seg, d) == (0, 1):
                        v.drain().then_inc(state_final, 1)
                barrier()

                for t in range(NT):
                    for j, c0 in enumerate((MA, MC)):
                        tt(hsq[:, j * 256:(j + 1) * 256], MIX[:, t, c0:c0 + 256], MIX[:, t, c0:c0 + 256], ALU.mult)
                    v.drain()
                    v.tensor_reduce(hss[:, t, :], hsq.rearrange("p (g c) -> p g c", c=64), AX_X, ALU.add)
                    v.drain()
                v.drain().then_inc(head_squares, 1)
                hr_t.next(v)
                v.reciprocal(hrinv[:, :, :], hroot[:, :, :])
                v.drain()
                v.tensor_scalar(hrinv[:, :, 4:8], hrinv[:, :, 4:8], 1.0 - lam_init(layer), None, ALU.mult)
                v.drain()
                for t in range(NT):
                    for j, c0 in enumerate((MA, MC)):
                        y = MIX[:, t, c0:c0 + 256].rearrange("p (h c) -> p h c", h=4)
                        tt(y, y, hrinv[:, t, 4 * j:4 * j + 4].unsqueeze(2).broadcast_to([P, 4, 64]), ALU.mult)
                    v.drain()
                    tt(MIX[:, t, MA:MA + 256], MIX[:, t, MA:MA + 256], ROWS[:, R_GA:R_GA + 256], ALU.mult)
                    tt(MIX[:, t, MC:MC + 256], MIX[:, t, MC:MC + 256], ROWS[:, R_GO:R_GO + 256], ALU.mult)
                    v.drain()
                    tt(MIX[:, t, MA:MA + 256], MIX[:, t, MA:MA + 256], PR[:, t, AO:AO + 256], ALU.mult)
                v.drain().then_inc(mix_ready, 1)

                job = 0
                for n in range(2):
                    for t in range(NT):
                        ps = V.take(v)
                        tmp = xtmp[:, job % 2, :]
                        V.give(tt(tmp, ps[:, :], GB[:, 0, cond_of(t), n * 512:(n + 1) * 512], ALU.mult))
                        v.drain()
                        tt(X[:, t, n * 512:(n + 1) * 512], X[:, t, n * 512:(n + 1) * 512], tmp, ALU.add)
                        job += 1
                v.drain().then_inc(x_ready, 1)
                normed()
                ht_t.next(v)
                tt(HTL[:, :, :], HTF, HTH[:, :, :].bitcast(F32), ALU.subtract).then_inc(split_ready, 1)
                barrier()

                for t in range(NT):
                    s = SC[:, t]
                    for rnd in range(2):
                        lo, hi = 8 * rnd, 8 * rnd + 8
                        for c in range(HC):
                            v.max(val[:, c, lo:hi], s[:, c, :])
                        v.drain()
                        for c in range(HC):
                            v.max_index(idx[:, c, lo:hi], val[:, c, lo:hi], s[:, c, :])
                        if rnd == 0:
                            v.drain()
                            for c in range(HC):
                                v.match_replace(s[:, c, :], val[:, c, lo:hi], s[:, c, :], -BIG)
                            v.drain()
                    v.drain()
                    v.tensor_copy(idxf[:, :, :, :].rearrange("p h c k -> p (h c) k"), idx[:, :, :])
                    v4 = val[:, :, :].rearrange("p (h c) k -> p h c k", c=2)
                    tt(cand, v4[:, :, 0, :].unsqueeze(3).broadcast_to([P, HEADS, TOPK, TOPK]),
                       v4[:, :, 1, :].unsqueeze(2).broadcast_to([P, HEADS, TOPK, TOPK]), ALU.add)
                    v.drain()
                    for rnd in range(2):
                        lo, hi = 8 * rnd, 8 * rnd + 8
                        for h in range(HEADS):
                            v.max(tops[:, h, lo:hi], cand[:, h].rearrange("p a b -> p (a b)"))
                        v.drain()
                        for h in range(HEADS):
                            v.max_index(posu[:, h, lo:hi], tops[:, h, lo:hi], cand[:, h].rearrange("p a b -> p (a b)"))
                        if rnd == 0:
                            v.drain()
                            for h in range(HEADS):
                                ch = cand[:, h].rearrange("p a b -> p (a b)")
                                v.match_replace(ch, tops[:, h, lo:hi], ch, -BIG)
                            v.drain()
                    v.drain()
                    tt(gate[:, :, :], tops[:, :, :], tops[:, :, 0:1].broadcast_to([P, HEADS, TOPK]), ALU.subtract)
                    v.tensor_scalar(pab[0], pflat, 4, None, ALU.logical_shift_right)
                    v.tensor_scalar(pab[1], pflat, 15, None, ALU.bitwise_and)
                    v.drain().then_inc(tops_ready, 1)
                    for j in range(2):
                        v.tensor_copy(pabf[j], pab[j])
                    v.drain()
                    for j in range(2):
                        eq3 = eq.rearrange("p (n a) -> p n a", a=TOPK)
                        tt(eq3, pabf[j].unsqueeze(2).broadcast_to([P, P, TOPK]),
                           iota[:, 0:TOPK].unsqueeze(1).broadcast_to([P, P, TOPK]), ALU.is_equal)
                        v.drain()
                        eq4 = eq.rearrange("p (h k a) -> p h k a", h=HEADS, a=TOPK)
                        tt(eq4, eq4, idxf[:, :, j, :].unsqueeze(2).broadcast_to([P, HEADS, TOPK, TOPK]), ALU.mult)
                        v.drain()
                        v.tensor_reduce(sel[j], eq3, AX_X, ALU.add)
                        v.drain()
                    te_t.next(v)
                    v.tensor_reduce(gsum, gate[:, :, :], AX_X, ALU.add)
                    v.drain()
                    v.reciprocal(grec, gsum)
                    v.drain()
                    tt(gate[:, :, :], gate[:, :, :], grec.unsqueeze(2).broadcast_to([P, HEADS, TOPK]), ALU.mult)
                    v.drain().then_inc(picks_ready, 1)
                    ps = V.take(v)
                    cols = slice(t * P, (t + 1) * P)
                    for j in range(3):
                        ins = v.tensor_copy(IGT[j][:, cols], ps[:, j * P:(j + 1) * P])
                    V.give(ins)
                barrier()

                used = Tally(sca_filled, loop_base["gate", layer])
                with v.Fori(0, N // (2 * GT)) as i:
                    used.enter(i, 64)
                    for slot in range(2):
                        with v.Fori(0, GT // TOK) as j:
                            used.enter(j, 8)
                            for b in range(4):
                                v.wait_ge(sca_filled, used.at(b + 1 - 4))
                                for q in range(4):
                                    tok = i * (2 * GT) + (slot * GT + 4 * b + q) + j * 16

                                    def col(a):
                                        return a[:, bass.ds(tok, 1)]
                                    v.tensor_scalar(OH[:, b, q, 1, :], iota, col(IGT[1]), None, ALU.is_equal)
                                    ins = v.tensor_scalar(OH[:, b, q, 0, :], iota, col(IGT[0]), col(IGT[2]),
                                                          ALU.is_equal, ALU.mult)
                                ins.then_inc(onehot_ready, 1)
                            used.n += 8
                            used.leave(GT // TOK)
                    used.leave(N // (2 * GT))
                barrier()

                v.memset(ACC, 0.0)
                v.drain()
                steps = NK // (2 * GROUP)

                def product(b):
                    in_t[b % GROUP].n += 16
                    v.drain()
                    if b % GROUP == 0:
                        gi_t[b // GROUP].n += 16
                        v.wait_ge(gates_in[b // GROUP], gi_t[b // GROUP].at())
                    v.wait_ge(hidden_in[b % GROUP], in_t[b % GROUP].at())
                    tt(TMP[b % 2].rearrange("p (h t) -> p h t", t=GT), HB[b % GROUP].rearrange("p (h t) -> p h t", t=GT),
                       GG[b // GROUP][:, :, b % GROUP, :], ALU.mult).then_inc(gated_ready, 1)

                def low(b):
                    hi_t.next(v)
                    tt(HWL[:, b, :], TMP[b % 2], HWH[:, b, :].bitcast(F32), ALU.subtract).then_inc(low_ready, 1)

                def hidden_group(g):
                    product(GROUP * g)
                    for b in range(GROUP * g, GROUP * (g + 1)):
                        if b + 1 < GROUP * (g + 1):
                            product(b + 1)
                        low(b)

                def add_outputs():
                    for t in range(NT):
                        for ch in range(2):
                            ps = V.take(v)
                            a = ACC[:, t, ch * 512:(ch + 1) * 512]
                            V.give(tt(a, a, ps[:, :], ALU.add))
                    v.drain()

                for g in range(2):
                    hidden_group(g)
                with v.Fori(0, steps - 1) as i:
                    V.filled.enter(i, 4 * NT)
                    hi_t.enter(i, 2 * GROUP)
                    for x in in_t:
                        x.enter(i, 32)
                    for x in gi_t:
                        x.enter(i, 16)
                    for g in range(2):
                        add_outputs()
                        hidden_group(g)
                    for x in [V.filled, hi_t] + in_t + gi_t:
                        x.leave(steps - 1)
                for g in range(2):
                    add_outputs()
                for t in range(NT):
                    tt(ACC[:, t, :], ACC[:, t, :], GB[:, 1, cond_of(t), :], ALU.mult)
                v.drain()
                vx_t.n += 16
                v.wait_ge(x_back, vx_t.n)
                for t in range(NT):
                    tt(X[:, t, :], X[:, t, :], ACC[:, t, :], ALU.add)
                v.drain().then_inc(x_final if layer == DEPTH - 1 else x_ready, 1)
                barrier()

        @block.scalar
        def _(a):
            S = BankReader(sbank, sca_filled, sca_drained)
            phase = [0]
            x_t, mod_t, gs_t, ld_t = Tally(x_ready), Tally(mod_ready), Tally(group_squares), Tally(lam_dots)
            bs_t, cs_t, sg_t, ma_t, hs_t = Tally(b_scores), Tally(c_scores), Tally(gates_signed), Tally(ml_args), Tally(head_squares)
            tp_t, xn_t, gd_t = Tally(tops_ready), Tally(xn_ready), Tally(gated_ready, GROUP)
            stored = [Tally(s) for s in gates_stored]
            kept = [Tally(s) for s in hidden_stored]
            ur, vr = [Tally(s) for s in u_in], [Tally(s) for s in v_in]

            def barrier():
                phase[0] += 1
                a.drain().then_inc(phase_done, 1)
                a.wait_ge(phase_done, 3 * phase[0])

            def roots():
                for t in range(NT):
                    a.activation(MIX[:, t, :], X[:, t, :], ACT.Square, accum_out=ssq[:, t:t + 1])
                a.drain()
                a.activation(root[:, :], ssq[:, :], ACT.Sqrt, bias=eps, scale=1.0 / D).then_inc(roots_ready, 1)

            def modulated(dest, which):
                for t in range(NT):
                    for half in range(2):
                        ps = S.take(a)
                        for j in range(4):
                            k = 4 * half + j
                            c = cond_of(t)
                            ins = a.activation(dest[:, k, t * P:(t + 1) * P], ps[:, j * P:(j + 1) * P], ACT.Identity,
                                               bias=mod[:, 2 * which, k, c:c + 1], scale=mod[:, 2 * which + 1, k, c:c + 1])
                        S.give(ins)

            def high_u(b):
                ur[b].n += 16
                a.wait_ge(u_in[b], ur[b].at())
                a.activation(UH[:, b, :, :], UR[b], ACT.Copy).then_inc(u_high, 1)

            def hidden_block(block, b, more=True):
                if more:
                    high_u(1 - b)
                kept[b].n += 16
                a.wait_ge(hidden_stored[b], kept[b].at())
                for j in range(2):
                    ps = S.take(a)
                    S.give(a.activation(GE[:, b, j * HALF:(j + 1) * HALF], ps[:, 0:HALF], ACT.Gelu))
                a.wait_ge(sca_drained, S.filled.at())
                a.dma_start(io["hidden"][bass.ds(block, 1)].rearrange("o p t -> p (o t)"), GE[:, b, :])\
                    .then_inc(hidden_stored[b], 16)

            def hidden_loop(first, turns):
                with a.Fori(0, turns) as j:
                    S.filled.enter(j, 4)
                    for x in kept + ur:
                        x.enter(j, 16)
                    for b in range(2):
                        hidden_block(j * 2 + (first + b), b)
                    for x in [S.filled] + kept + ur:
                        x.leave(turns)

            a.wait_ge(setup_in, 16 * 4)
            a.activation(conds[:, :, :], cond[:, :, :], ACT.Silu).then_inc(cond_ready, 1)
            for layer in range(DEPTH):
                if layer:
                    x_t.next(a)
                roots()
                for w in range(2):
                    for c in range(2):
                        for half in range(2):
                            ps = S.take(a)
                            S.give(a.activation(GB[:, w, c, half * 512:(half + 1) * 512], ps[:, :], ACT.Copy))
                mod_t.next(a)
                modulated(HTk, 0)
                barrier()

                gs_t.next(a)
                a.activation(groot[:, :, 0:10], gss[:, :, 0:10], ACT.Sqrt, bias=eps, scale=1.0 / 64)
                a.activation(groot[:, :, 10:26], gss[:, :, 10:26], ACT.Sqrt, bias=eps, scale=1.0 / 32).then_inc(group_roots, 1)
                ld_t.next(a)
                a.activation(lamv[:, 0:2], lamv[:, 0:2], ACT.Exp).then_inc(lam_exps, 1)
                for t in range(NT):
                    for b0 in range(0, 13, 4):
                        nb = min(4, 13 - b0)
                        ps = S.take(a)
                        S.give(a.activation(QKT[:, b0:b0 + nb, t * P:(t + 1) * P],
                                            ps[:, 0:nb * P].rearrange("p (b n) -> p b n", b=nb), ACT.Copy))
                units = b_units()

                def exps(u):
                    nk = b_keys(units[u][0])
                    bs_t.next(a)
                    for i in range(2):
                        row = b_s[:, u % 2, i, 0:nk + 1]
                        ins = a.activation(row, row, ACT.Exp, bias=bmax[:, u % 2, i:i + 1], scale=0.125,
                                           accum_out=bsum[:, u % 2, i:i + 1])
                    ins.then_inc(b_exps, 1)

                exps(0)
                for u in range(len(units)):
                    if u + 1 < len(units):
                        exps(u + 1)
                    nk = b_keys(units[u][0])
                    for i in range(2):
                        ps = S.take(a)
                        S.give(a.activation(b_et[:, u % 2, i, 0:nk], ps[:, 0:nk], ACT.Copy))
                barrier()

                cu = c_units()

                def c_exp(u):
                    nk = c_keys(cu[u][0])
                    cs_t.next(a)
                    for i in range(2):
                        row = c_s[:, u % 2, i, 0:nk]
                        ins = a.activation(row, row, ACT.Exp, bias=cmax[:, u % 2, i:i + 1], scale=32 ** -0.5,
                                           accum_out=csum[:, u % 2, i:i + 1])
                    ins.then_inc(c_exps, 1)

                c_exp(0)
                for u in range(len(cu)):
                    if u + 1 < len(cu):
                        c_exp(u + 1)
                    nk = c_keys(cu[u][0])
                    for b0 in range(0, nk, 512):
                        n = min(512, nk - b0)
                        ps = S.take(a)
                        S.give(a.activation(c_at[:, u % 2, b0:b0 + n], ps[:, 0:n], ACT.Copy))
                barrier()

                sg_t.next(a)
                a.activation(lft[:, :], lft[:, :], ACT.Exp)
                a.drain()
                a.activation(lft[:, :], lft[:, :], ACT.Ln, bias=ones[:, 0:1]).then_inc(softplus_ready, 1)
                for seg, d, t in a_units():
                    ma_t.next(a)
                    for h in range(4):
                        a.activation(cm[:, h, :], cm[:, h, :], ACT.Exp, bias=args[:, 0, 4, h:h + 1])
                    a.activation(args[:, 0, 0:4, :], args[:, 0, 0:4, :], ACT.Exp).then_inc(ml_exps, 1)
                    ps = S.take(a)
                    S.give(a.activation(pt[:, :, :], ps[:, :].rearrange("p (h s) -> p h s", h=4), ACT.Copy))
                barrier()

                hs_t.next(a)
                a.activation(PR[:, :, AO:AO + 256], PR[:, :, AO:AO + 256], ACT.Sigmoid)
                a.activation(hroot[:, :, :], hss[:, :, :], ACT.Sqrt, bias=eps, scale=1.0 / 64).then_inc(head_roots, 1)
                for t in range(NT):
                    for half in range(2):
                        ps = S.take(a)
                        S.give(a.activation(HTk[:, 4 * half:4 * half + 4, t * P:(t + 1) * P],
                                            ps[:, :].rearrange("p (k n) -> p k n", k=4), ACT.Copy))
                x_t.next(a)
                roots()
                a.wait_ge(x_spilled, 16 * (layer + 1))
                a.wait_ge(xn_ready, NT * (2 * layer + 2))
                modulated(HTF, 1)
                a.drain()
                a.activation(HTH[:, :, :], HTF, ACT.Copy).then_inc(turned_ready, 1)
                def queries(c):
                    for j in range(2):
                        ps = S.take(a)
                        S.give(a.activation(QT[:, c % 2, j * HALF:(j + 1) * HALF], ps[:, 0:HALF], ACT.Copy))
                for c in range(HC + 1):
                    if c < HC:
                        queries(c)
                    if c >= 1:
                        for t0, n in ((0, 4), (4, 1)):
                            ps = S.take(a)
                            S.give(a.activation(SC[:, t0:t0 + n, c - 1, :], ps[:, 0:n * P].rearrange("p (t k) -> p t k", t=n),
                                                ACT.Copy))
                barrier()
                high_u(0)
                for t in range(NT):
                    hidden_loop(t * PICK_BLOCKS, PICK_BLOCKS // 2)
                    tp_t.next(a)
                    a.activation(gate, gate, ACT.Exp).then_inc(top_exps, 1)
                barrier()

                turns, inner = N // (2 * GT), GT // TOK
                with a.Fori(0, turns) as i:
                    S.filled.enter(i, 16 * inner)
                    for x in kept + ur:
                        x.enter(i, 2 * inner * 16)
                    for x in stored:
                        x.enter(i, 16)
                    for slot in range(2):
                        stored[slot].n += 16
                        with a.Fori(0, inner) as j:
                            S.filled.enter(j, 8)
                            for x in kept + ur:
                                x.enter(j, 16)
                            for b in range(2):
                                hidden_block(i * (4 * inner) + (NT * PICK_BLOCKS + slot * 2 * inner + b) + j * 2, b)
                            a.wait_ge(gates_stored[slot], stored[slot].at())
                            for b in range(4):
                                ps = S.take(a)
                                dst = GS[slot][:, :, bass.ds(j * TOK + 4 * b, 4)].rearrange("p b t -> p t b")
                                S.give(a.activation(dst, ps[:, :].rearrange("p (t b) -> p t b", t=4), ACT.Copy))
                            for x in [S.filled] + kept + ur:
                                x.leave(inner)
                        a.wait_ge(sca_drained, S.filled.at())
                        dst = io["gates"][bass.ds(i * 2 + slot, 1)].rearrange("o p b t -> p (o b) t")
                        a.dma_start(dst, GS[slot]).then_inc(gates_stored[slot], 16)
                    for x in [S.filled] + kept + stored + ur:
                        x.leave(turns)
                done = NT * PICK_BLOCKS + 2 * N // TOK
                hidden_loop(done, (NK - done) // 2 - 1)
                for b in range(2):
                    hidden_block(NK - 2 + b, b, more=(b == 0))
                for x in stored + kept:
                    a.wait_ge(x.sem, x.n + 16)
                barrier()

                steps = NK // (2 * GROUP)
                with a.Fori(0, steps) as i:
                    gd_t.enter(i, 2 * GROUP)
                    for x in vr:
                        x.enter(i, 32)
                    for b in range(2 * GROUP):
                        gd_t.next(a)
                        a.activation(HWH[:, b, :], TMP[b % 2], ACT.Copy).then_inc(high_ready, 1)
                        vr[b % 4].n += 16
                        a.wait_ge(v_in[b % 4], vr[b % 4].at())
                        a.activation(VH[:, b, :], VR[b % 4][:, :], ACT.Copy).then_inc(v_high, 1)
                    for x in [gd_t] + vr:
                        x.leave(steps)
                barrier()

        @block.gpsimd
        def _(g):
            uh, vh = Tally(u_high), Tally(v_high)
            g.sem_inc(u_split, 2)
            g.sem_inc(v_split, 4)
            for layer in range(DEPTH):
                with g.Fori(0, NK // 2) as i:
                    uh.enter(i, 2)
                    for b in range(2):
                        uh.next(g)
                        g.tensor_tensor(UL[:, b, :, :], UR[b], UH[:, b, :, :].bitcast(F32), ALU.subtract)\
                            .then_inc(u_split, 1)
                    uh.leave(NK // 2)
                with g.Fori(0, NK // (2 * GROUP)) as i:
                    vh.enter(i, 2 * GROUP)
                    for b in range(2 * GROUP):
                        vh.next(g)
                        g.tensor_tensor(VL[:, b, :], VR[b % 4][:, :], VH[:, b, :].bitcast(F32), ALU.subtract)\
                            .then_inc(v_split, 1)
                    vh.leave(NK // (2 * GROUP))

        @block.sync
        def _(sp):
            sp.dma_start(CON[:, :], io["consts"]).then_inc(setup_in, 16)
            sp.dma_start(cond[:, :, :], io["cond"]).then_inc(setup_in, 16)
            sp.dma_start(X[:, 0, :], io["x_prompt"]).then_inc(setup_in, 16)
            sp.dma_start(X[:, 1:NT, :], io["x_sample"].rearrange("(t p) c -> p t c", p=P)).then_inc(setup_in, 16)
            for slot in range(2):
                sp.sem_inc(gates_stored[slot], 16)
                sp.sem_inc(hidden_stored[slot], 16)
            sp.sem_inc(gated_ready, GROUP)
            n_slice = [0]
            outs = [0]

            def load(src, width):
                n = n_slice[0]
                n_slice[0] += 1
                if n >= 3:
                    sp.wait_ge(*slice_read[n - 3])
                sp.dma_start(wslot[n % 3][:, 0:width], src).then_inc(slice_in[n % 3], 16)

            def store(dst, src):
                sp.dma_start(dst, src).then_inc(out_done, 16)
                outs[0] += 16

            us = Tally(u_split)
            for layer in range(DEPTH):
                ph = 8 * layer
                if layer:
                    sp.wait_ge(phase_done, 3 * ph)
                sp.dma_start(ROWS[:, :], io["rows"][layer:layer + 1, :].broadcast_to([P, N_ROWS])).then_inc(vectors_in, 16)
                sp.dma_start(bada, io["b_ada"][layer:layer + 1, :].broadcast_to([2, 6 * D])).then_inc(vectors_in, 16)
                sp.dma_start(ngain[:, :, :], io["ngain"][layer]).then_inc(vectors_in, 16)
                for n in range(ADA_SLICES):
                    load(io["w_ada"][layer, n], KD * 512)
                for n in range(IN_SLICES):
                    load(io["w_in"][layer, n], KD * IN_W)
                sp.wait_ge(phase_done, 3 * (ph + 1))
                sp.dma_start(kcb, io["cache_bk"][layer]).then_inc(caches_in, 16)
                sp.dma_start(kcc[:, :, :], io["cache_ck"][layer]).then_inc(caches_in, 16)
                sp.dma_start(vcb, io["cache_bv"][layer]).then_inc(caches_in, 16)
                sp.dma_start(vcc, io["cache_cv"][layer]).then_inc(caches_in, 16)
                sp.dma_start(mstate[:, 1], io["state_m"][layer:layer + 1].broadcast_to([P, 8])).then_inc(caches_in, 16)
                sp.wait_ge(qk_ready, NT * layer + 1)
                store(io["o_bk"][layer], PR[:, 0, BK:BK + 128])
                store(io["o_bv"][layer], PR[:, 0, BV:BV + 128])
                store(io["o_ck"][layer], PR[:, 0, CK:CK + 256])
                store(io["o_cv"][layer], PR[:, 0, CV:CV + 256])
                sp.wait_ge(qk_ready, NT * (layer + 1))
                sp.dma_start(cst[:, 1], io["state_C"][layer]).then_inc(caches_in, 16)
                sp.wait_ge(state_final, layer + 1)
                store(io["o_state"][layer], cst[:, 0])
                store(io["o_m"][layer:layer + 1], mstate[0:1, 0])
                sp.wait_ge(phase_done, 3 * (ph + 4))
                for n in range(2):
                    load(io["w_out"][layer, n], KD * 512)
                sp.wait_ge(mix_ready, layer + 1)
                sp.dma_start(SUBT[:, :, :], io["subkeys"][layer]).then_inc(subkeys_in, 16)
                for n in range(2):
                    sp.dma_start(wq_slot[n], io["wq"][layer, n]).then_inc(wq_in[n], 16)
                sp.wait_ge(x_ready, 2 * layer + 1)
                sp.dma_start(io["x"], X).then_inc(x_spilled, 16)
                for n in range(2, 4):
                    sp.wait_ge(sca_filled, wq_read[layer][n - 2])
                    sp.dma_start(wq_slot[n % 2], io["wq"][layer, n]).then_inc(wq_in[n % 2], 16)

                sp.wait_ge(phase_done, 3 * (ph + 5))
                us.n = 2 + layer * NK
                with sp.Fori(0, NK // 2) as i:
                    us.enter(i, 2)
                    for b in range(2):
                        sp.wait_ge(u_split, us.at(b - 1))
                        sp.dma_start(UR[b], io["u"][layer, bass.ds(i * 2 + b, 1)].rearrange("o p k e -> p (o k) e"))\
                            .then_inc(u_in[b], 16)
                    us.n += 2
                    us.leave(NK // 2)
                sp.wait_ge(phase_done, 3 * (ph + 7))
                used = Tally(gated_ready, GROUP + layer * NK)
                vs = Tally(v_split, 4 + layer * NK)
                with sp.Fori(0, NK // (2 * GROUP)) as i:
                    used.enter(i, 2 * GROUP)
                    vs.enter(i, 2 * GROUP)
                    for b in range(2 * GROUP):
                        block_at = bass.ds(i * (2 * GROUP) + b, 1)
                        sp.wait_ge(gated_ready, used.at(b - GROUP + 1))
                        if b % GROUP == 0:
                            src = io["gates"][:, :, bass.ds(i * (2 * GROUP) + b, GROUP), :].rearrange("h p b t -> p h (b t)")
                            sp.dma_start(GG[b // GROUP].rearrange("p h b t -> p h (b t)"), src)\
                                .then_inc(gates_in[b // GROUP], 16)
                        sp.dma_start(HB[b % GROUP], io["hidden"][block_at].rearrange("o p t -> p (o t)"))\
                            .then_inc(hidden_in[b % GROUP], 16)
                        sp.wait_ge(v_split, vs.at(b - 3))
                        sp.dma_start(VR[b % 4][:, :], io["v"][layer, block_at].rearrange("o p c -> p (o c)"))\
                            .then_inc(v_in[b % 4], 16)
                    used.n += 2 * GROUP
                    vs.n += 2 * GROUP
                    used.leave(NK // (2 * GROUP))
                    vs.leave(NK // (2 * GROUP))
                sp.wait_ge(gated_ready, GROUP + (layer + 1) * NK)
                sp.dma_start(X, io["x"]).then_inc(x_back, 16)
            sp.wait_ge(x_final, 1)
            store(io["o_prompt"], X[:, 0, :])
            store(io["o_sample"].rearrange("(t p) c -> p t c", p=P), X[:, 1:NT, :])
            sp.wait_ge(out_done, outs[0])


def _constants():
    import numpy as np
    c = np.zeros((P, N_CONST), np.float32)
    i = np.arange(P)
    lower = i[:, None] >= i[None, :]
    c[:, C_ID:C_ID + P] = np.eye(P)
    c[:, C_TRIF:C_TRIF + P] = lower.T
    c[:, C_TRIB:C_TRIB + P] = lower
    c[:, C_ONE:C_ONE + P] = 1
    c[:, C_MF:C_MF + P] = np.where(lower, 0, NEG)
    c[:, C_MB:C_MB + P] = np.where(lower.T, 0, NEG)
    before, after = np.where(lower.T, 0, NEG), np.where(lower, 0, NEG)
    zero = np.zeros((P, P))
    c[:, C_BAND:C_BAND + 512] = np.concatenate([zero, before, zero, after], 1)
    c[:, C_BAND1:C_BAND1 + 384] = np.concatenate([zero, zero, after], 1)
    c[:, C_IOTA:C_IOTA + NK] = i
    t = np.arange(DEC_SEQ)
    place = np.stack([t // 64, t % 64], 1).astype(np.float32)
    for at, q in ((C_RB, 16), (C_RC, 8)):
        inv = (np.float32(10000.0) ** (-np.arange(q, dtype=np.float32) / np.float32(q))).astype(np.float32)
        ang = place[:, :, None] * inv
        for k, f in enumerate((np.cos, np.sin)):
            tab = f(ang).astype(np.float32).reshape(NT - 1, P, 2 * q).transpose(1, 0, 2).reshape(P, -1)
            c[:, at + k * 8 * q:at + (k + 1) * 8 * q] = tab
    for r in range(2):
        c[r, C_SEL + r * P:C_SEL + (r + 1) * P] = 1
    c[:, C_EPS] = EPS
    return c


def kernel(**inputs):
    import numpy as np
    import concourse.bacc as bacc
    from concourse.bass_utils import run_bass_kernel_spmd

    f = {k: np.asarray(v) for k, v in inputs.items()}
    L = DEPTH
    sizes = (256, 256, 256, 256, 16, 512, 128, 128, 256, 256, 256)
    starts = np.concatenate([[0], np.cumsum(sizes)])
    bq = starts[5] + np.concatenate([np.arange(64) + 64 * h for p in range(4) for h in (p, p + 4)])
    order = np.concatenate([np.arange(starts[5]), bq, np.arange(starts[6], starts[-1])])

    def chunks(w, width):
        n = w.shape[-1] // width
        return w.reshape(L, KD, P, n, width).transpose(0, 3, 2, 1, 4)

    def tiled(g, k):
        return np.tile(g.reshape(L, -1), (1, k))

    arrays = {
        "consts": _constants(),
        "cond": np.stack([f["c_ctx"].reshape(KD, P).T, f["c"].reshape(KD, P).T], -1),
        "x_prompt": f["x_prompt"][0],
        "x_sample": f["x_sample"][0],
        "rows": np.concatenate([f["b_in"][:, order], tiled(f["b_q_gain"], 8), tiled(f["b_k_gain"], 2),
                                tiled(f["c_q_gain"], 4), tiled(f["c_k_gain"], 4), f["a_out_gain"],
                                tiled(f["c_out_gain"], 4), f["b_sink"], f["c_lambda"].reshape(L, -1)], 1),
        "b_ada": f["b_ada"],
        "ngain": f["norm_gain"].reshape(L, 2, KD, P).transpose(0, 3, 1, 2),
        "w_ada": chunks(f["w_ada"], 512).reshape(L, ADA_SLICES, P, -1),
        "w_in": chunks(f["w_in"][:, :, order], IN_W).reshape(L, IN_SLICES, P, -1),
        "w_out": chunks(f["w_out"], 512).reshape(L, 2, P, -1),
        "wq": f["peer_wq"].reshape(L, KD, P, 4, 4, P).transpose(0, 3, 2, 4, 1, 5).reshape(L, 4, P, -1),
        "subkeys": f["peer_subkeys"].transpose(0, 4, 1, 2, 3).reshape(L, P, HC, NK),
        "cache_bk": f["cache_swa_k"][0].transpose(0, 2, 3, 1).reshape(L, P, PAST),
        "cache_bv": f["cache_swa_v"][0].reshape(L, PAST, 128),
        "cache_ck": f["cache_diff_k"][0].reshape(L, PAST, 2, P).transpose(0, 3, 2, 1),
        "cache_cv": f["cache_diff_v"][0].reshape(L, PAST, 256),
        "state_C": np.concatenate([f["state_mlstm_C"][0], f["state_mlstm_n"][0][..., None]], -1)
        .reshape(L, 2, 2, 2, 64, 65).transpose(0, 3, 4, 1, 2, 5).reshape(L, P, 2, 2, 65),
        "state_m": f["state_mlstm_m"][0].reshape(L, 8),
        "u": f["peer_u"].reshape(L, NK, P, KD, P).transpose(0, 1, 4, 3, 2),
        "v": f["peer_v"].reshape(L, NK, P, D),
    }
    outs = {"o_prompt": (SEQ, D), "o_sample": (DEC_SEQ, D), "o_bk": (L, P, 128), "o_bv": (L, P, 128),
            "o_ck": (L, P, 256), "o_cv": (L, P, 256), "o_state": (L, P, 2, 2, 65), "o_m": (L, 8)}
    nc = bacc.Bacc("TRN2", target_bir_lowering=False, num_devices=1)
    io, fed = {}, {}
    for name, a in arrays.items():
        a = np.ascontiguousarray(a)
        fed[f"in_{name}"] = a
        io[name] = nc.dram_tensor(f"in_{name}", a.shape, mybir.dt.from_np(a.dtype), kind="ExternalInput").ap()
    for name, shape in outs.items():
        io[name] = nc.dram_tensor(f"out_{name}", shape, F32, kind="ExternalOutput").ap()
    io["hidden"] = nc.dram_tensor("hidden", (NK, P, N), F32, kind="Internal").ap()
    io["x"] = nc.dram_tensor("x_kept", (P, NT, D), F32, kind="Internal").ap()
    io["gates"] = nc.dram_tensor("gates", (N // GT, P, NK, GT), F32, kind="Internal").ap()
    hybrid_step(nc, io)
    r = run_bass_kernel_spmd(nc, [fed], core_ids=[0]).results[0]
    g = {name: np.asarray(r[f"out_{name}"]) for name in outs}
    state = g["o_state"].reshape(L, 2, 64, 2, 2, 65).transpose(0, 3, 4, 1, 2, 5).reshape(1, L, 2, 4, 64, 65)
    return (g["o_prompt"][None], g["o_sample"][None],
            g["o_bk"].reshape(1, L, P, 2, 64), g["o_bv"].reshape(1, L, P, 2, 64),
            g["o_ck"].reshape(1, L, P, 4, 64), g["o_cv"].reshape(1, L, P, 4, 64),
            np.ascontiguousarray(state[..., :64]), np.ascontiguousarray(state[..., 64]),
            g["o_m"].reshape(1, L, 2, 4))
```

```python
import math
from contextlib import ExitStack

import concourse.bass as bass
from concourse import mybir

F32 = mybir.dt.float32
F32R = mybir.dt.float32r
U32 = mybir.dt.uint32
ALU = mybir.AluOpType
ACT = mybir.ActivationFunctionType
AX_X = mybir.AxisListType.X

P = 128
D = 1024
KD = D // P
SEQ, DEC_SEQ, PAST = 128, 512, 128
NT = (SEQ + DEC_SEQ) // P
N = NT * P
DEPTH = 2
EPS = 1e-6
NEG = -1e30
BIG = 3e38

AQ, AK, AV, AO, AG = 0, 256, 512, 768, 1024
BQ, BK, BV = 1040, 1552, 1680
CQ, CK, CV = 1808, 2064, 2320
IN_COLS = 2576
IN_SLICES = 7
IN_W = IN_COLS // IN_SLICES
B_GROUPS, C_GROUPS = 10, 16

MA, MB, MC = 0, 256, 768

ADA_SLICES = 6 * D // 512

C_ID, C_TRIF, C_TRIB, C_ONE, C_MF, C_MB = 0, 128, 256, 384, 512, 640
C_BAND, C_BAND1 = 768, 1280
C_IOTA = 1664
C_RB, C_RC = 1792, 2048
C_SEL = 2176
C_EPS = 2432
N_CONST = 2433

R_BIN, R_GB, R_GC, R_GA, R_GO, R_SINK, R_LAM = 0, 2576, 3216, 3728, 3984, 4240, 4248
N_ROWS = 4376

NK = 128
HEADS, TOPK = 8, 16
HC = 2 * HEADS
HALF = N // 2
GT = 64
GROUP = 4
PICK_BLOCKS = (10, 10, 10, 8, 8)
TOK = 16

A_ROWS, A_X, A_HT = 0, 4376, 9496
A_P, A_WR, A_MIX = 14616, 27496, 39784
ARENA = 44904
A_HTL = A_P
A_WQ, A_QT, A_SC = 19736, 27928, 29464
A_UR, A_UH, A_UL, A_GE = 19736, 21784, 23832, 25880
A_GS = (28440, 36632)
A_VR, A_TMP, A_GG, A_VH, A_VL = (0, 1024, 3328, 38680), 2048, 4376, 9496, 17688
A_HWH, A_HWL, A_HB = 25880, 31000, 36120
WSLOT = 4096


class Tally:

    def __init__(self, sem, n=0, by=1):
        self.sem, self.n, self.by, self.terms, self.start = sem, n, by, [], []

    def at(self, k=0):
        value = self.n + k
        for reg, per in self.terms:
            value = reg * per + value
        return value

    def enter(self, reg, per):
        self.terms.append((reg, per))
        self.start.append(self.n)

    def leave(self, turns):
        _, per = self.terms.pop()
        began = self.start.pop()
        assert self.n - began == per, (self.n - began, per)
        self.n = began + turns * per

    def next(self, eng):
        self.n += self.by
        eng.wait_ge(self.sem, self.at())


class BankWriter:

    def __init__(self, banks, filled, drained):
        self.banks, self.filled, self.drained = banks, Tally(filled), drained

    def open(self, pe):
        n = self.filled.n
        if n >= 4 or self.filled.terms:
            pe.wait_ge(self.drained, self.filled.at(-3))
        return self.banks[n % 4]

    def close(self, ins):
        ins.then_inc(self.filled.sem, 1)
        self.filled.n += 1

    def landed(self, pe):
        pe.wait_ge(self.drained, self.filled.at())


class BankReader:

    def __init__(self, banks, filled, drained):
        self.banks, self.filled, self.drained = banks, Tally(filled), drained

    def take(self, eng):
        bank = self.banks[self.filled.n % 4]
        self.filled.next(eng)
        return bank

    def give(self, ins):
        ins.then_inc(self.drained, 1)


def cond_of(t):
    return 0 if t == 0 else 1


def b_units():
    return [(t, g, pp) for t in range(NT) for g in range(2) for pp in range(2)]


def b_local(t):
    return [0] if t == 0 else [s for s in (t - 1, t, t + 1) if 1 <= s < NT]


def b_keys(t):
    return P if t == 0 else P * (1 + len(b_local(t)))


def c_units():
    return [(t, h) for t in range(NT) for h in range(4)]


def c_keys(t):
    return P if t == 0 else DEC_SEQ + PAST


def a_units():
    out = [(0, 0, 0), (0, 1, 0)]
    for s in range(NT - 1):
        out += [(1, 0, 1 + s), (1, 1, NT - 1 - s)]
    return out


def lam_init(layer):
    return 0.8 - 0.6 * math.exp(-0.3 * layer)


def hybrid_step(nc, io):
    with ExitStack() as ctx:
        def sb(name, shape, dt=F32):
            return ctx.enter_context(nc.sbuf_tensor(name, shape, dt))

        def sem(name):
            return ctx.enter_context(nc.semaphore(name))

        base = -(-nc.sbuf_base // 32) * 32
        AR = sb("AR", [P, ARENA])
        assert nc.sbuf_base == base + 4 * ARENA

        def over(name, shape, at, dt=F32):
            return nc.alloc_sbuf_tensor_at(name, [P] + shape, dt, offset=base + 4 * at)

        def rounded(name, shape, at):
            return over(name, shape, at, F32R)

        X = AR[:, A_X:A_X + NT * D].rearrange("p (t c) -> p t c", t=NT)
        HT = AR[:, A_HT:A_HT + KD * N]
        ROWS = AR[:, A_ROWS:A_ROWS + N_ROWS]
        GB = sb("GB", [P, 2, 2, D])
        CON = sb("CON", [P, N_CONST])
        SM = sb("SM", [P, 1400])
        vbank = [ctx.enter_context(nc.psum_tensor(f"vbank{i}", [P, 512], F32)) for i in range(4)]
        sbank = [ctx.enter_context(nc.psum_tensor(f"sbank{i}", [P, 512], F32)) for i in range(4)]

        small_at = [0]

        def small(n, dt=F32):
            a = small_at[0]
            small_at[0] += n
            assert small_at[0] <= 1400
            return SM[:, a:a + n]

        cond = small(16).rearrange("p (k c) -> p k c", c=2)
        conds = small(16).rearrange("p (k c) -> p k c", c=2)
        ngain = small(16).rearrange("p (w k) -> p w k", w=2)
        mod = small(64).rearrange("p (v k c) -> p v k c", v=4, c=2)
        ssq, root, rinv = small(NT), small(NT), small(NT)
        gss, groot, grinv = (small(NT * 26).rearrange("p (t g) -> p t g", t=NT) for _ in range(3))
        hss, hroot, hrinv = (small(NT * 8).rearrange("p (t g) -> p t g", t=NT) for _ in range(3))
        bmax, bsum, brec = (small(8).rearrange("p (s i) -> p s i", s=4) for _ in range(3))
        cmax, csum, crec = (small(4).rearrange("p (s i) -> p s i", s=2) for _ in range(3))
        lamw = small(64)
        lamv = small(4)
        lf = small(40)
        lft = small(40)
        bci = small(80)
        ci = small(40)
        mstate = small(16).rearrange("p (s d h) -> p s d h", s=2, d=2)
        args, mtmp = small(5 * 40), small(5 * 40)
        den = small(8).rearrange("p (k h) -> p k h", k=2)

        ident = CON[:, C_ID:C_ID + P]
        ones = CON[:, C_ONE:C_ONE + P]
        eps = CON[:, C_EPS:C_EPS + 1]
        iota = CON[:, C_IOTA:C_IOTA + NK]

        wslot = [AR[:, A_WR + i * WSLOT:A_WR + (i + 1) * WSLOT] for i in range(3)]
        PR = AR[:, A_P:A_P + NT * IN_COLS].rearrange("p (t c) -> p t c", t=NT)
        ada = AR[0:2, A_P:A_P + 6 * D]
        bada = AR[0:2, A_P + 6 * D:A_P + 12 * D]
        MIX = AR[:, A_MIX:A_MIX + NT * D].rearrange("p (t c) -> p t c", t=NT)
        n = KD * IN_W
        WIR = [AR[:, A_WR + i * n:A_WR + (i + 1) * n].rearrange("p (k n) -> p k n", k=KD) for i in range(2)]
        WIL = [rounded(f"WIL{i}", [KD, IN_W], A_WR + i * n) for i in range(2)]
        WIH = [rounded(f"WIH{i}", [KD, IN_W], A_WR + (2 + i) * n) for i in range(2)]
        assert 4 * n <= 3 * WSLOT
        ITH, ITL = rounded("ITH", [KD, N], A_MIX), rounded("ITL", [KD, N], A_HT)
        HTk = HT.rearrange("p (k n) -> p k n", k=KD)
        QKT = AR[:, A_WR:A_WR + 13 * N].rearrange("p (b n) -> p b n", b=13)
        W0 = A_WR + 13 * N
        kcb = HT[:, 0:128]
        kcc = HT[:, 128:384].rearrange("p (b n) -> p b n", b=2)
        vcb = HT[:, 384:512]
        vcc = HT[:, 512:768]
        H0 = 768
        SQ = AR[:, W0:W0 + 1152]
        hsq = HT[:, H0:H0 + 512]
        b_s = HT[:, H0:H0 + 2080].rearrange("p (s i n) -> p s i n", s=2, i=2)
        b_et = HT[:, H0 + 2080:H0 + 2080 + 2048].rearrange("p (s i n) -> p s i n", s=2, i=2)
        c_s = HT[:, H0:H0 + 2560].rearrange("p (s i n) -> p s i n", s=2, i=2)
        c_at = HT[:, H0 + 2560:H0 + 2560 + 1280].rearrange("p (s n) -> p s n", s=2)

        def work(a, n):
            return AR[:, W0 + a:W0 + a + n]
        vaug = work(0, 1300).rearrange("p (t h c) -> p t h c", t=NT, h=4)
        cst = work(1300, 520).rearrange("p (s d j c) -> p s d j c", s=2, d=2, j=2)
        q0 = A_WR
        dg, pm, pt = (AR[:, q0 + i * 1024:q0 + (i + 1) * 1024].rearrange("p (s h n) -> p s h n", s=2, h=4)
                      for i in range(3))
        wk = AR[:, q0 + 3072:q0 + 3584].rearrange("p (s n) -> p s n", s=2)
        nd = AR[:, q0 + 3584:q0 + 4104].rearrange("p (s h c) -> p s h c", s=2, h=4)
        htmp = AR[:, q0 + 4104:q0 + 4360].rearrange("p (h c) -> p h c", h=4)
        cm = HT.rearrange("p (d t h s) -> p d t h s", d=2, t=NT, h=4)
        xtmp = AR[:, A_P:A_P + 1024].rearrange("p (s n) -> p s n", s=2)
        HTF = AR[:, A_X:A_X + KD * N].rearrange("p (k n) -> p k n", k=KD)
        HTH, HTL = rounded("HTH", [KD, N], A_HT), rounded("HTL", [KD, N], A_HTL)
        wq_slot = [AR[:, A_WQ + i * WSLOT:A_WQ + (i + 1) * WSLOT] for i in range(2)]
        WQH = [rounded(name, [4, KD, P], at) for name, at in (("WQHX", A_X), ("WQHM", A_MIX))]
        WQL = [rounded(f"WQL{i}", [4, KD, P], A_WQ + i * WSLOT) for i in range(2)]
        SC = AR[:, A_SC:A_SC + NT * HC * NK].rearrange("p (t c k) -> p t c k", t=NT, c=HC)
        QT = AR[:, A_QT:A_QT + 2 * N].rearrange("p (s n) -> p s n", s=2)
        SUBT = ROWS[:, 0:2048].rearrange("p (c k) -> p c k", c=HC)
        IGT = [ROWS[:, i * N:(i + 1) * N] for i in range(3)]
        o = A_X
        val = AR[:, o:o + 256].rearrange("p (c k) -> p c k", c=HC)
        idx = AR[:, o + 256:o + 512].bitcast(U32).rearrange("p (c k) -> p c k", c=HC)
        cand = AR[:, o + 512:o + 2560].rearrange("p (h a b) -> p h a b", h=HEADS, a=TOPK)
        eq = AR[:, o + 2560:o + 4608]
        idxf = AR[:, o + 4608:o + 4864].rearrange("p (h c k) -> p h c k", h=HEADS, c=2)
        tops = AR[:, o + 4864:o + 4992].rearrange("p (h k) -> p h k", h=HEADS)
        gate = AR[:, o + 4992:o + 5120].rearrange("p (h k) -> p h k", h=HEADS)
        o = 5 * N
        pflat = ROWS[:, o:o + 128].bitcast(U32)
        posu = pflat.rearrange("p (h k) -> p h k", h=HEADS)
        pab = [ROWS[:, o + 128:o + 256].bitcast(U32), ROWS[:, o + 256:o + 384].bitcast(U32)]
        pabf = [ROWS[:, o + 384:o + 512], ROWS[:, o + 512:o + 640]]
        sel = [ROWS[:, o + 640:o + 768], ROWS[:, o + 768:o + 896]]
        gsum = ROWS[:, o + 896:o + 904]
        grec = ROWS[:, o + 904:o + 912]
        UR = [AR[:, A_UR + i * 1024:A_UR + (i + 1) * 1024].rearrange("p (k e) -> p k e", k=KD) for i in range(2)]
        UH, UL = rounded("UH", [2, KD, P], A_UH), rounded("UL", [2, KD, P], A_UL)
        GE = AR[:, A_GE:A_GE + 2 * N].rearrange("p (s n) -> p s n", s=2)
        OH = AR[:, A_X:A_X + 4096].rearrange("p (s t k n) -> p s t k n", s=4, t=4, k=2)
        GS = [AR[:, a:a + NK * GT].rearrange("p (b t) -> p b t", b=NK) for a in A_GS]
        VR = [over(f"VR{i}", [D], a) for i, a in enumerate(A_VR)]
        TMP = [AR[:, A_TMP + i * N:A_TMP + (i + 1) * N] for i in range(2)]
        HB = [AR[:, A_HB + i * N:A_HB + (i + 1) * N] for i in range(GROUP)]
        GG = [AR[:, A_GG + i * GROUP * N:A_GG + (i + 1) * GROUP * N]
              .rearrange("p (h b t) -> p h b t", h=N // GT, b=GROUP) for i in range(2)]
        VH, VL = rounded("VH", [2 * GROUP, D], A_VH), rounded("VL", [2 * GROUP, D], A_VL)
        HWH, HWL = rounded("HWH", [2 * GROUP, N], A_HWH), rounded("HWL", [2 * GROUP, N], A_HWL)
        ACC = AR[:, A_MIX:A_MIX + NT * D].rearrange("p (t c) -> p t c", t=NT)

        vec_filled, vec_drained = sem("vec_filled"), sem("vec_drained")
        sca_filled, sca_drained = sem("sca_filled"), sem("sca_drained")
        phase_done = sem("phase_done")
        setup_in = sem("setup_in")
        vectors_in = sem("vectors_in")
        slice_in = [sem(f"slice_in{i}") for i in range(3)]
        cond_in = sem("cond_in")
        cond_ready = sem("cond_ready")
        ada_rows = sem("ada_rows")
        mod_ready = sem("mod_ready")
        x_ready = sem("x_ready")
        roots_ready = sem("roots_ready")
        xn_ready = sem("xn_ready")
        group_squares = sem("group_squares")
        group_roots = sem("group_roots")
        qk_ready = sem("qk_ready")
        caches_in = sem("caches_in")
        b_scores = sem("b_scores")
        b_exps = sem("b_exps")
        c_scores = sem("c_scores")
        c_exps = sem("c_exps")
        c_weights = sem("c_weights")
        gates_signed = sem("gates_signed")
        softplus_ready = sem("softplus_ready")
        log_f_ready = sem("log_f_ready")
        diag_ready = sem("diag_ready")
        ml_args = sem("ml_args")
        ml_exps = sem("ml_exps")
        ml_products = sem("ml_products")
        state_ready = sem("state_ready")
        state_final = sem("state_final")
        head_squares = sem("head_squares")
        head_roots = sem("head_roots")
        lam_dots = sem("lam_dots")
        lam_exps = sem("lam_exps")
        mix_ready = sem("mix_ready")
        subkeys_in = sem("subkeys_in")
        tops_ready = sem("tops_ready")
        top_exps = sem("top_exps")
        picks_ready = sem("picks_ready")
        onehot_ready = sem("onehot_ready")
        gates_stored = [sem(f"gates_stored{i}") for i in range(2)]
        wq_in = [sem(f"wq_in{i}") for i in range(2)]
        wi_in = [sem(f"wi_in{i}") for i in range(2)]
        wi_high = sem("wi_high")
        wi_split = sem("wi_split")
        it_high = sem("it_high")
        it_half = sem("it_half")
        it_split = sem("it_split")
        wq_high = sem("wq_high")
        wq_split = sem("wq_split")
        x_spilled = sem("x_spilled")
        x_back = sem("x_back")
        half_ready = sem("half_ready")
        turned_ready = sem("turned_ready")
        split_ready = sem("split_ready")
        u_in = [sem(f"u_in{i}") for i in range(2)]
        u_split = sem("u_split")
        u_high = sem("u_high")
        v_high = sem("v_high")
        hidden_stored = [sem(f"hidden_stored{i}") for i in range(2)]
        v_in = [sem(f"v_in{i}") for i in range(4)]
        v_split = sem("v_split")
        hidden_in = [sem(f"hidden_in{i}") for i in range(GROUP)]
        gates_in = [sem(f"gates_in{i}") for i in range(2)]
        gated_ready = sem("gated_ready")
        high_ready = sem("high_ready")
        low_ready = sem("low_ready")
        x_final = sem("x_final")
        out_done = sem("out_done")

        slice_read = []
        out_filled = []
        loop_base = {}
        wi_read = []
        wq_read = []

        block = ctx.enter_context(nc.Block())

        @block.tensor
        def _(pe):
            V = BankWriter(vbank, vec_filled, vec_drained)
            S = BankWriter(sbank, sca_filled, sca_drained)
            slices = [0, 0, 0]
            n_slice = [0]
            phase = [0]

            def barrier():
                phase[0] += 1
                pe.drain().then_inc(phase_done, 1)
                pe.wait_ge(phase_done, 3 * phase[0])

            def next_slice():
                i = n_slice[0] % 3
                n_slice[0] += 1
                slices[i] += 16
                pe.wait_ge(slice_in[i], slices[i])
                return wslot[i]

            def slice_done(w):
                slice_read.append((w.filled.sem, w.filled.n))

            def transposed_norm():
                for t in range(NT):
                    xn_t.next(pe)
                    for half, W in enumerate((S, V)):
                        ps = W.open(pe)
                        for j in range(4):
                            k = 4 * half + j
                            ins = pe.transpose(ps[:, j * P:(j + 1) * P], MIX[:, t, k * P:(k + 1) * P], ident)
                        W.close(ins)
                for W in (S, V):
                    W.landed(pe)

            xn_t, qk_t, be_t, cw_t = Tally(xn_ready), Tally(qk_ready), Tally(b_exps), Tally(c_weights)
            ada_t, lf_t, dg_t, mp_t = Tally(ada_rows), Tally(log_f_ready), Tally(diag_ready), Tally(ml_products)
            st_t, ws_t = Tally(state_ready), Tally(wq_split)
            wi_t, ws_i, it_t = [Tally(x, by=16) for x in wi_in], Tally(wi_split), Tally(it_split)
            mix_t, pk_t, oh_t, low_t = Tally(mix_ready), Tally(picks_ready), Tally(onehot_ready), Tally(low_ready)
            us_t, vs_t, sp_t = Tally(u_split, 2), Tally(v_split, 4), Tally(split_ready)
            wq_t = [Tally(s) for s in wq_in]

            def hidden_block(b):
                us_t.next(pe)
                for j in range(2):
                    cols = slice(j * HALF, (j + 1) * HALF)
                    ps = S.open(pe)[:, 0:HALF]
                    for k in range(KD):
                        pe.matmul(ps, UH[:, b, k, :], HTH[:, k, cols], start=(k == 0), stop=False)
                        pe.matmul(ps, UH[:, b, k, :], HTL[:, k, cols], start=False, stop=False)
                        ins = pe.matmul(ps, UL[:, b, k, :], HTH[:, k, cols], start=False, stop=(k == KD - 1))
                    S.close(ins)

            def hidden_loop(turns):
                with pe.Fori(0, turns) as j:
                    S.filled.enter(j, 4)
                    us_t.enter(j, 2)
                    for b in range(2):
                        hidden_block(b)
                    S.filled.leave(turns)
                    us_t.leave(turns)

            pe.wait_ge(cond_ready, 1)

            for layer in range(DEPTH):
                for n in range(ADA_SLICES):
                    w = next_slice().rearrange("p (k n) -> p k n", k=KD)
                    ps = V.open(pe)
                    for k in range(KD):
                        ins = pe.matmul(ps[0:2, :], conds[:, k, :], w[:, k, :], start=(k == 0), stop=(k == KD - 1))
                    V.close(ins)
                    slice_done(V)
                ada_t.next(pe)
                if layer == 0:
                    pe.wait_ge(setup_in, 16 * 3)
                ps = V.open(pe)
                for v, vec in enumerate((0, 1, 3, 4)):
                    for k in range(KD):
                        a = vec * D + k * P
                        ins = pe.transpose(ps[:, (v * KD + k) * 2:(v * KD + k) * 2 + 2], ada[:, a:a + P], ident[0:2, 0:2])
                V.close(ins)
                for vec in (2, 5):
                    for c in range(2):
                        for half in range(2):
                            ps = S.open(pe)
                            a = vec * D + half * 512
                            S.close(pe.matmul(ps[:, :], CON[0:2, C_SEL + c * P:C_SEL + (c + 1) * P], ada[:, a:a + 512],
                                              start=True, stop=True))
                transposed_norm()
                wi_read.append([])
                for n in range(IN_SLICES):
                    w, hi, lo = WIR[n % 2], WIH[n % 2], WIL[n % 2]
                    wi_t[n % 2].next(pe)
                    if n >= 1:
                        ws_i.next(pe)
                    for t in range(NT):
                        if n == 1:
                            it_t.next(pe)
                        ps = V.open(pe)[:, 0:IN_W]
                        rows = slice(t * P, (t + 1) * P)
                        for k in range(KD):
                            first, last = k == 0, k == KD - 1
                            if n == 0:
                                ins = pe.matmul(ps, HTk[:, k, rows], w[:, k, :], start=first, stop=last)
                            else:
                                pe.matmul(ps, ITH[:, k, rows], hi[:, k, :], start=first, stop=False)
                                pe.matmul(ps, ITH[:, k, rows], lo[:, k, :], start=False, stop=False)
                                ins = pe.matmul(ps, ITL[:, k, rows], hi[:, k, :], start=False, stop=last)
                        V.close(ins)
                    wi_read[-1].append(V.filled.n)
                barrier()

                cols = [BQ + P * i for i in range(4)] + [BK, CQ, CQ + P, CK, CK + P, AQ, AQ + P, AK, AK + P]
                for t in range(NT):
                    qk_t.next(pe)
                    for b0 in range(0, 13, 4):
                        ps = S.open(pe)
                        for b in range(b0, min(b0 + 4, 13)):
                            ins = pe.transpose(ps[:, (b - b0) * P:(b - b0 + 1) * P], PR[:, t, cols[b]:cols[b] + P], ident)
                        S.close(ins)
                S.landed(pe)
                pe.wait_ge(caches_in, 96 * (layer + 1))

                units = b_units()

                def scores(u):
                    t, g, pp = units[u]
                    r = slice(64 * g, 64 * g + 64)
                    for i in range(2):
                        ps = V.open(pe)
                        q = QKT[r, 2 * pp + i, t * P:(t + 1) * P]
                        if t == 0:
                            ins = pe.matmul(ps[:, 0:P], q, QKT[r, 4, 0:P], start=True, stop=True)
                        else:
                            loc = b_local(t)
                            pe.matmul(ps[:, 0:P], q, kcb[r, :], start=True, stop=True)
                            ins = pe.matmul(ps[:, P:P + P * len(loc)], q, QKT[r, 4, loc[0] * P:(loc[-1] + 1) * P],
                                            start=True, stop=True)
                        V.close(ins)

                turned = {}

                def turn(u):
                    be_t.next(pe)
                    for i in range(2):
                        ps = S.open(pe)
                        for b in range(b_keys(units[u][0]) // P):
                            ins = pe.transpose(ps[:, b * P:(b + 1) * P], b_s[:, u % 2, i, b * P:(b + 1) * P], ident)
                        S.close(ins)
                    turned[u] = S.filled.n

                def mixed(u):
                    t, g, pp = units[u]
                    nb = b_keys(t) // P
                    pe.wait_ge(sca_drained, turned[u])
                    ps = V.open(pe)
                    for i in range(2):
                        for b in range(nb):
                            if t == 0:
                                v = PR[:, 0, BV + 64 * g:BV + 64 * g + 64]
                            elif b == 0:
                                v = vcb[:, 64 * g:64 * g + 64]
                            else:
                                v = PR[:, b_local(t)[b - 1], BV + 64 * g:BV + 64 * g + 64]
                            ins = pe.matmul(ps[:, 64 * i:64 * i + 64], b_et[:, u % 2, i, b * P:(b + 1) * P], v,
                                            start=(b == 0), stop=(b == nb - 1))
                    V.close(ins)

                scores(0)
                scores(1)
                for u in range(len(units)):
                    turn(u)
                    if u >= 1:
                        mixed(u - 1)
                    if u + 2 < len(units):
                        scores(u + 2)
                mixed(len(units) - 1)
                barrier()

                cu = c_units()

                def c_score(u):
                    t, h = cu[u]

                    def qk(c):
                        g = 2 * h + c
                        r = slice(32 * (g % 4), 32 * (g % 4) + 32)
                        return r, QKT[r, 5 + g // 4, t * P:(t + 1) * P], 7 + g // 4, g // 4
                    if t == 0:
                        for c in range(2):
                            ps = V.open(pe)
                            r, q, kb, _ = qk(c)
                            V.close(pe.matmul(ps[:, 0:P], q, QKT[r, kb, 0:P], start=True, stop=True))
                        return
                    for c in range(2):
                        ps = V.open(pe)
                        r, q, kb, _ = qk(c)
                        V.close(pe.matmul(ps[:, :], q, QKT[r, kb, P:N], start=True, stop=True))
                    for c in range(2):
                        ps = V.open(pe)
                        r, q, _, kc = qk(c)
                        V.close(pe.matmul(ps[:, 0:P], q, kcc[r, kc, :], start=True, stop=True))

                c_turned = {}

                def c_turn(u):
                    nb = c_keys(cu[u][0]) // P
                    cw_t.next(pe)
                    for b0 in range(0, nb, 4):
                        ps = S.open(pe)
                        for b in range(b0, min(b0 + 4, nb)):
                            ins = pe.transpose(ps[:, (b - b0) * P:(b - b0 + 1) * P],
                                               c_s[:, u % 2, 0, b * P:(b + 1) * P], ident)
                        S.close(ins)
                    c_turned[u] = S.filled.n

                def c_mixed(u):
                    t, h = cu[u]
                    nb = c_keys(t) // P
                    pe.wait_ge(sca_drained, c_turned[u])
                    ps = V.open(pe)
                    for b in range(nb):
                        if b == 4:
                            v = vcc[:, 64 * h:64 * h + 64]
                        else:
                            v = PR[:, 0 if t == 0 else 1 + b, CV + 64 * h:CV + 64 * h + 64]
                        ins = pe.matmul(ps[:, 0:64], c_at[:, u % 2, b * P:(b + 1) * P], v,
                                        start=(b == 0), stop=(b == nb - 1))
                    V.close(ins)

                c_score(0)
                c_score(1)
                for u in range(len(cu)):
                    c_turn(u)
                    if u >= 1:
                        c_mixed(u - 1)
                    if u + 2 < len(cu):
                        c_score(u + 2)
                c_mixed(len(cu) - 1)
                barrier()

                lf_t.next(pe)
                ps = V.open(pe)
                pe.matmul(ps[:, 0:20], CON[:, C_TRIF:C_TRIF + P], lf[:, 0:20], start=True, stop=True)
                pe.matmul(ps[:, 20:40], CON[:, C_TRIB:C_TRIB + P], lf[:, 20:40], start=True, stop=True)
                V.close(pe.matmul(ps[:, 40:80], ones, lf[:, :], start=True, stop=True))
                au = a_units()
                for u in range(len(au)):
                    dg_t.next(pe)
                    ps = V.open(pe)
                    V.close(pe.matmul(ps[:, :], ones, dg[:, u % 2].rearrange("p h s -> p (h s)"), start=True, stop=True))

                def by_rows(u, n, rhs):
                    t = au[u][2]
                    for odd in range(2):
                        ps = V.open(pe)
                        r = slice(64 * odd, 64 * odd + 64)
                        for j in range(2):
                            ins = pe.matmul(ps[:, j * n:(j + 1) * n], QKT[r, 9 + j, t * P:(t + 1) * P], rhs(r, j),
                                            start=True, stop=True)
                        V.close(ins)

                def key_products(u):
                    t = au[u][2]
                    by_rows(u, P, lambda r, j: QKT[r, 11 + j, t * P:(t + 1) * P])

                a_turned = {}

                def values(u):
                    t = au[u][2]
                    pe.wait_ge(sca_drained, a_turned[u])
                    ps = V.open(pe)
                    for h in range(4):
                        ins = pe.matmul(ps[:, h * 65:(h + 1) * 65], pt[:, u % 2, h, :], vaug[:, t, h, :],
                                        start=True, stop=True)
                    V.close(ins)

                key_products(0)
                key_products(1)
                for u, (seg, d, t) in enumerate(au):
                    mp_t.next(pe)
                    ps = S.open(pe)
                    for h in range(4):
                        ins = pe.transpose(ps[:, h * P:(h + 1) * P], pm[:, u % 2, h, :], ident)
                    S.close(ins)
                    a_turned[u] = S.filled.n
                    if u >= 1:
                        values(u - 1)
                    if u >= 2:
                        st_t.next(pe)
                    by_rows(u, 65, lambda r, j: cst[r, seg, d, j, :])
                    ps = V.open(pe)
                    for j in range(2):
                        ins = pe.matmul(ps[:, j * 130:(j + 1) * 130], wk[:, u % 2, j * P:(j + 1) * P],
                                        vaug[:, t, 2 * j:2 * j + 2, :].rearrange("p h c -> p (h c)"),
                                        start=True, stop=True)
                    V.close(ins)
                    if u + 2 < len(au):
                        key_products(u + 2)
                values(len(au) - 1)
                st_t.n += 2
                barrier()

                for t in range(NT):
                    if t == 0:
                        mix_t.next(pe)
                    for half in range(2):
                        ps = S.open(pe)
                        for j in range(4):
                            k = 4 * half + j
                            ins = pe.transpose(ps[:, j * P:(j + 1) * P], MIX[:, t, k * P:(k + 1) * P], ident)
                        S.close(ins)
                S.landed(pe)
                n_slice[0] += 1
                slice_read.append(slice_read[-1])
                for n in range(2):
                    w = next_slice().rearrange("p (k n) -> p k n", k=KD)
                    for t in range(NT):
                        ps = V.open(pe)
                        for k in range(KD):
                            ins = pe.matmul(ps[:, :], HTk[:, k, t * P:(t + 1) * P], w[:, k, :],
                                            start=(k == 0), stop=(k == KD - 1))
                        V.close(ins)
                    slice_done(V)
                transposed_norm()
                wq_read.append([])

                pe.wait_ge(subkeys_in, 16 * (layer + 1))
                w = None

                def query(c, w):
                    hi, lo = WQH[c // 4 % 2][:, c % 4], WQL[c // 4 % 2][:, c % 4]
                    for j in range(2):
                        ps = S.open(pe)[:, 0:HALF]
                        cols = slice(j * HALF, (j + 1) * HALF)
                        for k in range(KD):
                            first, last = k == 0, k == KD - 1
                            if c < 4:
                                ins = pe.matmul(ps, w[:, c % 4, k, :], HTF[:, k, cols], start=first, stop=last)
                            else:
                                pe.matmul(ps, hi[:, k, :], HTH[:, k, cols], start=first, stop=False)
                                pe.matmul(ps, hi[:, k, :], HTL[:, k, cols], start=False, stop=False)
                                ins = pe.matmul(ps, lo[:, k, :], HTH[:, k, cols], start=False, stop=last)
                        S.close(ins)
                    return S.filled.n

                def key_scores(c, after):
                    pe.wait_ge(sca_drained, after)
                    for t0 in (0, 4):
                        ps = S.open(pe)
                        for t in range(t0, min(t0 + 4, NT)):
                            ins = pe.matmul(ps[:, (t - t0) * P:(t - t0 + 1) * P], QT[:, c % 2, t * P:(t + 1) * P],
                                            SUBT[:, c, :], start=True, stop=True)
                        S.close(ins)

                after = 0
                for c in range(HC + 1):
                    was = after
                    if c < HC:
                        if c % 4 == 0:
                            i = c // 4 % 2
                            wq_t[i].n += 16
                            pe.wait_ge(wq_in[i], wq_t[i].n)
                            w = wq_slot[i].rearrange("p (c k n) -> p c k n", c=4, k=KD)
                            if c == 4:
                                sp_t.next(pe)
                            if c >= 4:
                                ws_t.next(pe)
                        after = query(c, w)
                        if c % 4 == 3:
                            wq_read[-1].append(S.filled.n)
                    if c >= 1:
                        key_scores(c - 1, was)
                barrier()

                for t in range(NT):
                    hidden_loop(PICK_BLOCKS[t] // 2)
                    pk_t.next(pe)
                    ps = V.open(pe)
                    pe.transpose(ps[:, 0:P], sel[0], ident)
                    pe.transpose(ps[:, P:2 * P], sel[1], ident)
                    V.close(pe.transpose(ps[:, 2 * P:3 * P], gate.rearrange("p h k -> p (h k)"), ident))
                barrier()

                turns, inner = N // (2 * GT), GT // TOK
                loop_base["gate", layer] = S.filled.n
                with pe.Fori(0, turns) as i:
                    S.filled.enter(i, 16 * inner)
                    us_t.enter(i, 4 * inner)
                    oh_t.enter(i, 8 * inner)
                    for slot in range(2):
                        with pe.Fori(0, inner) as j:
                            S.filled.enter(j, 8)
                            us_t.enter(j, 2)
                            oh_t.enter(j, 4)
                            for b in range(2):
                                hidden_block(b)
                            for b in range(4):
                                oh_t.next(pe)
                                ps = S.open(pe)
                                for q in range(4):
                                    ins = pe.matmul(ps[:, q * P:(q + 1) * P], OH[:, b, q, 1, :], OH[:, b, q, 0, :],
                                                    start=True, stop=True)
                                S.close(ins)
                            for x in (S.filled, us_t, oh_t):
                                x.leave(inner)
                    for x in (S.filled, us_t, oh_t):
                        x.leave(turns)
                hidden_loop((NK - sum(PICK_BLOCKS) - 2 * N // TOK) // 2)
                barrier()

                steps = NK // (2 * GROUP)
                loop_base["out", layer] = V.filled.n
                with pe.Fori(0, steps) as i:
                    V.filled.enter(i, 4 * NT)
                    vs_t.enter(i, 2 * GROUP)
                    low_t.enter(i, 2 * GROUP)
                    for g in range(2):
                        for _ in range(GROUP):
                            vs_t.next(pe)
                            low_t.next(pe)
                        for t in range(NT):
                            for ch in range(2):
                                ps = V.open(pe)
                                for b in range(GROUP * g, GROUP * (g + 1)):
                                    rows, cols = slice(t * P, (t + 1) * P), slice(ch * 512, (ch + 1) * 512)
                                    first, last = b == GROUP * g, b == GROUP * (g + 1) - 1
                                    pe.matmul(ps[:, :], HWH[:, b, rows], VH[:, b, cols], start=first, stop=False)
                                    pe.matmul(ps[:, :], HWH[:, b, rows], VL[:, b, cols], start=False, stop=False)
                                    ins = pe.matmul(ps[:, :], HWL[:, b, rows], VH[:, b, cols], start=False, stop=last)
                                V.close(ins)
                    for x in (V.filled, vs_t, low_t):
                        x.leave(steps)
                out_filled.append(V.filled.n)
                phase[0] += 1
                pe.drain().then_inc(phase_done, 1)

        @block.vector
        def _(v):
            V = BankReader(vbank, vec_filled, vec_drained)
            phase = [0]
            rt_t, gr_t, sp_t, le_t = Tally(roots_ready), Tally(group_roots), Tally(softplus_ready), Tally(lam_exps)
            ce_t, be_t, me_t, hr_t = Tally(c_exps), Tally(b_exps), Tally(ml_exps), Tally(head_roots)
            te_t = Tally(top_exps)
            hi_t, in_t, gi_t = Tally(high_ready), [Tally(s) for s in hidden_in], [Tally(s) for s in gates_in]
            ht_t, vx_t, wh_t = Tally(turned_ready), Tally(x_back), Tally(wq_high)
            ih_t, wi_h = Tally(it_high), Tally(wi_high)

            def barrier():
                phase[0] += 1
                v.drain().then_inc(phase_done, 1)
                v.wait_ge(phase_done, 3 * phase[0])

            def tt(out, a, b, op):
                return v.tensor_tensor(out, a, b, op)

            def normed():
                rt_t.next(v)
                v.reciprocal(rinv[:, :], root[:, :])
                v.drain()
                for t in range(NT):
                    v.tensor_scalar(MIX[:, t, :], X[:, t, :], rinv[:, t:t + 1], None, ALU.mult).then_inc(xn_ready, 1)

            def modulated(dest, which):
                for t in range(NT):
                    ps = V.take(v)
                    c = cond_of(t)
                    for j in range(4):
                        k = 4 + j
                        ins = v.tensor_scalar(dest[:, k, t * P:(t + 1) * P], ps[:, j * P:(j + 1) * P],
                                              mod[:, 2 * which + 1, k, c:c + 1], mod[:, 2 * which, k, c:c + 1],
                                              ALU.mult, ALU.add)
                    V.give(ins)

            v.wait_ge(setup_in, 16 * 3)

            for layer in range(DEPTH):
                v.wait_ge(vectors_in, 48 * (layer + 1))
                for n in range(ADA_SLICES):
                    ps = V.take(v)
                    V.give(tt(ada[:, n * 512:(n + 1) * 512], ps[0:2, :], bada[:, n * 512:(n + 1) * 512], ALU.add))
                v.drain().then_inc(ada_rows, 1)
                ps = V.take(v)
                for w in range(2):
                    cols = ps[:, w * 32:(w + 1) * 32].rearrange("p (v k c) -> p v k c", v=2, c=2)
                    v.tensor_copy(mod[:, 2 * w, :, :], cols[:, 0])
                    ins = v.scalar_tensor_tensor(mod[:, 2 * w + 1, :, :], cols[:, 1], 1.0,
                                                 ngain[:, w, :].unsqueeze(2).broadcast_to([P, KD, 2]), ALU.add, ALU.mult)
                V.give(ins)
                v.drain().then_inc(mod_ready, 1)
                normed()
                modulated(HTk, 0)
                v.drain().then_inc(it_half, 1)
                for n in range(IN_SLICES):
                    for t in range(NT):
                        ps = V.take(v)
                        V.give(tt(PR[:, t, n * IN_W:(n + 1) * IN_W], ps[:, 0:IN_W],
                                  ROWS[:, R_BIN + n * IN_W:R_BIN + (n + 1) * IN_W], ALU.add))
                        if n == 0:
                            if t == 0:
                                ih_t.next(v)
                            rows = slice(t * P, (t + 1) * P)
                            tt(ITL[:, :, rows], HTk[:, :, rows], ITH[:, :, rows].bitcast(F32), ALU.subtract)\
                                .then_inc(it_split, 1)
                        if (n, t) == (0, 1) or (1 <= n < IN_SLICES - 1 and t == 2):
                            wi_h.next(v)
                            i = (n + 1) % 2
                            tt(WIL[i][:, :, :], WIR[i], WIH[i][:, :, :].bitcast(F32), ALU.subtract).then_inc(wi_split, 1)
                barrier()

                for t in range(NT):
                    tt(SQ[:, 0:640], PR[:, t, BQ:BQ + 640], PR[:, t, BQ:BQ + 640], ALU.mult)
                    tt(SQ[:, 640:1152], PR[:, t, CQ:CQ + 512], PR[:, t, CQ:CQ + 512], ALU.mult)
                    v.drain()
                    v.tensor_reduce(gss[:, t, 0:10], SQ[:, 0:640].rearrange("p (g c) -> p g c", c=64), AX_X, ALU.add)
                    v.tensor_reduce(gss[:, t, 10:26], SQ[:, 640:1152].rearrange("p (g c) -> p g c", c=32), AX_X, ALU.add)
                    v.drain()
                v.drain().then_inc(group_squares, 1)
                lam = ROWS[:, R_LAM:R_LAM + 128].rearrange("p (a b c) -> p a b c", a=2, b=2)
                tt(lamw[:, :].rearrange("p (a c) -> p a c", a=2), lam[:, :, 0, :], lam[:, :, 1, :], ALU.mult)
                v.drain()
                v.tensor_reduce(lamv[:, 0:2], lamw[:, :].rearrange("p (a c) -> p a c", a=2), AX_X, ALU.add)
                v.drain().then_inc(lam_dots, 1)
                le_t.next(v)
                tt(lamv[:, 2:3], lamv[:, 1:2], lamv[:, 0:1], ALU.subtract)
                v.drain()
                v.tensor_scalar(lamv[:, 3:4], lamv[:, 2:3], lam_init(layer), None, ALU.subtract)
                gr_t.next(v)
                v.reciprocal(grinv[:, :, :], groot[:, :, :])
                v.drain()
                for t in range(NT):
                    qb = PR[:, t, BQ:BQ + 640].rearrange("p (g c) -> p g c", c=64)
                    qc = PR[:, t, CQ:CQ + 512].rearrange("p (g c) -> p g c", c=32)
                    tt(qb, qb, grinv[:, t, 0:10].unsqueeze(2).broadcast_to([P, 10, 64]), ALU.mult)
                    tt(qc, qc, grinv[:, t, 10:26].unsqueeze(2).broadcast_to([P, 16, 32]), ALU.mult)
                    v.drain()
                    tt(PR[:, t, BQ:BQ + 640], PR[:, t, BQ:BQ + 640], ROWS[:, R_GB:R_GB + 640], ALU.mult)
                    tt(PR[:, t, CQ:CQ + 512], PR[:, t, CQ:CQ + 512], ROWS[:, R_GC:R_GC + 512], ALU.mult)
                    v.drain()
                    if t > 0:
                        for at, ng, q, tab in ((BQ, B_GROUPS, 16, C_RB), (CQ, C_GROUPS, 8, C_RC)):
                            n = ng * 4 * q
                            x4 = PR[:, t, at:at + n].rearrange("p (g a b q) -> p g a b q", a=2, b=2, q=q)
                            h1, h2 = x4[:, :, :, 0, :], x4[:, :, :, 1, :]

                            def table(k):
                                a = tab + k * 4 * 2 * q + (t - 1) * 2 * q
                                return CON[:, a:a + 2 * q].rearrange("p (a q) -> p a q", a=2).unsqueeze(1)\
                                    .broadcast_to([P, ng, 2, q])
                            tmp = [AR[:, W0 + i * 320:W0 + i * 320 + n // 2].rearrange("p (g a q) -> p g a q", a=2, q=q)
                                   for i in range(4)]
                            tt(tmp[0], h1, table(0), ALU.mult)
                            tt(tmp[1], h2, table(1), ALU.mult)
                            tt(tmp[2], h2, table(0), ALU.mult)
                            tt(tmp[3], h1, table(1), ALU.mult)
                            v.drain()
                            tt(h1, tmp[0], tmp[1], ALU.subtract)
                            tt(h2, tmp[2], tmp[3], ALU.add)
                            v.drain()
                    v.drain().then_inc(qk_ready, 1)

                units = b_units()

                def prep(u):
                    t, g, pp = units[u]
                    nk = b_keys(t)
                    s = b_s[:, u % 2]
                    h = 4 * g + 2 * pp
                    band = CON[:, C_BAND1:C_BAND1 + nk] if t == 1 else CON[:, C_BAND:C_BAND + nk]
                    for i in range(2):
                        ps = V.take(v)
                        if t == 0:
                            V.give(v.tensor_copy(s[:, i, 0:nk], ps[:, 0:nk]))
                        else:
                            V.give(tt(s[:, i, 0:nk], ps[:, 0:nk], band, ALU.add))
                    v.tensor_scalar(s[:, :, nk:nk + 1], ROWS[:, R_SINK + h:R_SINK + h + 2].unsqueeze(2), 8.0, None, ALU.mult)
                    v.drain()
                    v.tensor_reduce(bmax[:, u % 4, :], s[:, :, 0:nk + 1], AX_X, ALU.max)
                    v.drain()
                    v.tensor_scalar(bmax[:, u % 4, :], bmax[:, u % 4, :], -0.125, None, ALU.mult).then_inc(b_scores, 1)

                def finish(u):
                    t, g, pp = units[u]
                    h = 4 * g + 2 * pp
                    be_t.next(v)
                    v.reciprocal(brec[:, u % 4, :], bsum[:, u % 4, :])
                    v.drain()
                    ps = V.take(v)
                    V.give(tt(MIX[:, t, MB + 64 * h:MB + 64 * h + 128].rearrange("p (i c) -> p i c", i=2),
                              ps[:, 0:128].rearrange("p (i c) -> p i c", i=2),
                              brec[:, u % 4, :].unsqueeze(2).broadcast_to([P, 2, 64]), ALU.mult))

                prep(0)
                prep(1)
                for u in range(len(units)):
                    if u >= 1:
                        finish(u - 1)
                    if u + 2 < len(units):
                        prep(u + 2)
                finish(len(units) - 1)
                barrier()

                cu = c_units()

                def c_prep(u):
                    t, h = cu[u]
                    s = c_s[:, u % 2]
                    nk = c_keys(t)
                    for k0 in range(0, nk, 512):
                        n = min(512, nk - k0)
                        for c in range(2):
                            ps = V.take(v)
                            V.give(v.tensor_copy(s[:, c, k0:k0 + n], ps[:, 0:n]))
                    v.drain()
                    v.tensor_reduce(cmax[:, u % 2, :], s[:, :, 0:nk], AX_X, ALU.max)
                    v.drain()
                    v.tensor_scalar(cmax[:, u % 2, :], cmax[:, u % 2, :], -(32 ** -0.5), None, ALU.mult)\
                        .then_inc(c_scores, 1)

                def c_mid(u):
                    t, h = cu[u]
                    s = c_s[:, u % 2]
                    nk = c_keys(t)
                    ce_t.next(v)
                    v.reciprocal(crec[:, u % 2, :], csum[:, u % 2, :])
                    v.drain()
                    tt(crec[:, u % 2, 1:2], crec[:, u % 2, 1:2], lamv[:, 3:4], ALU.mult)
                    v.tensor_scalar(s[:, 0, 0:nk], s[:, 0, 0:nk], crec[:, u % 2, 0:1], None, ALU.mult)
                    v.drain()
                    v.scalar_tensor_tensor(s[:, 0, 0:nk], s[:, 1, 0:nk], crec[:, u % 2, 1:2], s[:, 0, 0:nk],
                                           ALU.mult, ALU.add).then_inc(c_weights, 1)

                def c_finish(u):
                    t, h = cu[u]
                    ps = V.take(v)
                    V.give(v.tensor_copy(MIX[:, t, MC + 64 * h:MC + 64 * h + 64], ps[:, 0:64]))

                c_prep(0)
                c_prep(1)
                c_mid(0)
                for u in range(len(cu)):
                    if u + 1 < len(cu):
                        c_mid(u + 1)
                    if u >= 1:
                        c_finish(u - 1)
                    if u + 2 < len(cu):
                        c_prep(u + 2)
                c_finish(len(cu) - 1)
                barrier()

                gview = PR[:, :, AG:AG + 16].rearrange("p t (d x h) -> p d x t h", d=2, x=2)

                def dth(ap):
                    return ap.rearrange("p (d t h) -> p d t h", d=2, t=NT)
                for d in range(2):
                    v.tensor_scalar(dth(lft[:, :])[:, d], gview[:, d, 1], -1.0, None, ALU.mult)
                v.drain()
                for d in range(2):
                    tt(dth(lft[:, :])[:, d], dth(lft[:, :])[:, d], gview[:, d, 1], ALU.min)
                v.drain().then_inc(gates_signed, 1)
                for d in range(2):
                    v.tensor_scalar(dth(lf[:, :])[:, d], gview[:, d, 1], 0.0, None, ALU.min)
                v.memset(vaug[:, :, :, 64:65], 1.0)
                for t in range(NT):
                    v.tensor_copy(vaug[:, t, :, 0:64], PR[:, t, AV:AV + 256].rearrange("p (h c) -> p h c", h=4))
                v.memset(cst[:, 0], 0.0)
                v.memset(mstate[:, 0], 0.0)
                sp_t.next(v)
                v.drain()
                tt(lf[:, :], lf[:, :], lft[:, :], ALU.subtract)
                v.drain().then_inc(log_f_ready, 1)
                ps = V.take(v)
                V.give(v.tensor_copy(bci[:, :], ps[:, 0:80]))
                v.drain()
                for d in range(2):
                    tt(dth(ci[:, :])[:, d], gview[:, d, 0], dth(bci[:, 0:40])[:, d], ALU.subtract)
                v.drain()
                bc, bl, cc = dth(bci[:, 0:40]), dth(bci[:, 40:80]), dth(ci[:, :])
                au = a_units()
                seen = set()
                k5 = args[:, :].rearrange("p (k n) -> p k n", k=5)
                m5 = mtmp[:, :].rearrange("p (k n) -> p k n", k=5)
                top, row, before, upto, rowto = (m5[:, k] for k in range(5))
                topv, rowv, beforev, uptov = dth(top), dth(row), dth(before), dth(upto)

                def diag(u):
                    seg, d, t = au[u]
                    tt(dg[:, u % 2], ident.unsqueeze(1).broadcast_to([P, 4, P]),
                       cc[:, d, t, :].unsqueeze(2).broadcast_to([P, 4, P]), ALU.mult).then_inc(diag_ready, 1)

                diag(0)
                diag(1)
                for u, (seg, d, t) in enumerate(au):
                    mask = CON[:, (C_MF, C_MB)[d]:(C_MF, C_MB)[d] + P]
                    ps = V.take(v)
                    tt(cm[:, d, t], ps[:, :].rearrange("p (h s) -> p h s", h=4),
                       mask.unsqueeze(1).broadcast_to([P, 4, P]), ALU.add)
                    V.give(v.tensor_reduce(topv[:, d, t, :], ps[:, :].rearrange("p (h s) -> p h s", h=4), AX_X, ALU.max))
                    if u + 2 < len(au):
                        diag(u + 2)
                    v.drain()
                    v.tensor_reduce(rowv[:, d, t, :], cm[:, d, t], AX_X, ALU.max)
                for step in range(NT):
                    pair = au[2 * step:2 * step + 2]
                    for seg, d, t in pair:
                        v.tensor_copy(beforev[:, d, t, :], mstate[:, seg, d, :])
                        tt(uptov[:, d, t, :], topv[:, d, t, :], mstate[:, seg, d, :], ALU.max)
                    v.drain()
                    for seg, d, t in pair:
                        tt(mstate[:, seg, d, :], bl[:, d, t, :], uptov[:, d, t, :], ALU.add)
                    v.drain()
                tt(rowto, row, before, ALU.max)
                tt(k5[:, 1], before, upto, ALU.subtract)
                tt(k5[:, 2], ci[:, :], upto, ALU.subtract)
                v.drain()
                tt(k5[:, 0], before, rowto, ALU.subtract)
                tt(lft[:, :], bci[:, 0:40], rowto, ALU.add)
                v.tensor_scalar(k5[:, 4], rowto, -1.0, None, ALU.mult)
                v.drain()
                v.tensor_scalar(k5[:, 3], lft[:, :], -1.0, None, ALU.mult)
                v.drain().then_inc(ml_args, 1)
                ar = [dth(k5[:, k]) for k in range(4)]
                me_t.next(v)

                def products(u):
                    seg, d, t = au[u]
                    me_t.next(v)
                    for odd in range(2):
                        ps = V.take(v)
                        V.give(v.scalar_tensor_tensor(pm[:, u % 2, odd::2, :],
                                                      ps[:, 0:256].rearrange("p (j s) -> p j s", j=2),
                                                      0.125, cm[:, d, t, odd::2, :], ALU.mult, ALU.mult))
                    v.scalar_tensor_tensor(wk[:, u % 2, :].rearrange("p (h c) -> p h c", h=4),
                                           PR[:, t, AK:AK + 256].rearrange("p (h c) -> p h c", h=4), 0.125,
                                           ar[2][:, d, t, :].unsqueeze(2).broadcast_to([P, 4, 64]), ALU.mult, ALU.mult)
                    v.drain().then_inc(ml_products, 1)

                def finish_unit(u):
                    seg, d, t = au[u]
                    y = nd[:, u % 2]
                    ps = V.take(v)
                    V.give(tt(y, y, ps[:, 0:260].rearrange("p (h c) -> p h c", h=4), ALU.add))
                    v.drain()
                    dn = y[:, :, 64:65]
                    d0, d1 = den[:, 0, :].unsqueeze(2), den[:, 1, :].unsqueeze(2)
                    v.scalar_tensor_tensor(d0, dn, -1.0, dn, ALU.mult, ALU.max)
                    v.drain()
                    tt(d0, d0, ar[3][:, d, t, :].unsqueeze(2), ALU.max)
                    v.drain()
                    v.reciprocal(d1, d0)
                    v.drain()
                    dst = MIX[:, t, MA:MA + 256].rearrange("p (h c) -> p h c", h=4)
                    rec = den[:, 1, :].unsqueeze(2).broadcast_to([P, 4, 64])
                    if t not in seen:
                        seen.add(t)
                        tt(dst, y[:, :, 0:64], rec, ALU.mult)
                    else:
                        tt(htmp[:, :, :], y[:, :, 0:64], rec, ALU.mult)
                        v.drain()
                        tt(dst, dst, htmp[:, :, :], ALU.add)
                    v.drain()

                products(0)
                products(1)
                for u, (seg, d, t) in enumerate(au):
                    if u >= 1:
                        finish_unit(u - 1)
                    for odd in range(2):
                        ps = V.take(v)
                        V.give(tt(nd[:, u % 2, odd::2, :], ps[:, 0:130].rearrange("p (j c) -> p j c", j=2),
                                  ar[0][:, d, t, odd::2].unsqueeze(2).broadcast_to([P, 2, 65]), ALU.mult))
                    ps = V.take(v)
                    for h in range(4):
                        r = slice(64 * (h % 2), 64 * (h % 2) + 64)
                        st = cst[r, seg, d, h // 2, :]
                        ins = v.scalar_tensor_tensor(st, st, ar[1][r, d, t, h:h + 1], ps[r, h * 65:(h + 1) * 65],
                                                     ALU.mult, ALU.add)
                    V.give(ins)
                    v.drain().then_inc(state_ready, 1)
                    if (seg, d) == (0, 1):
                        v.drain().then_inc(state_final, 1)
                    if u + 2 < len(au):
                        products(u + 2)
                finish_unit(len(au) - 1)
                barrier()

                for t in range(NT):
                    for j, c0 in enumerate((MA, MC)):
                        tt(hsq[:, j * 256:(j + 1) * 256], MIX[:, t, c0:c0 + 256], MIX[:, t, c0:c0 + 256], ALU.mult)
                    v.drain()
                    v.tensor_reduce(hss[:, t, :], hsq.rearrange("p (g c) -> p g c", c=64), AX_X, ALU.add)
                    v.drain()
                v.drain().then_inc(head_squares, 1)
                hr_t.next(v)
                v.reciprocal(hrinv[:, :, :], hroot[:, :, :])
                v.drain()
                v.tensor_scalar(hrinv[:, :, 4:8], hrinv[:, :, 4:8], 1.0 - lam_init(layer), None, ALU.mult)
                v.drain()
                for t in range(NT):
                    for j, c0 in enumerate((MA, MC)):
                        y = MIX[:, t, c0:c0 + 256].rearrange("p (h c) -> p h c", h=4)
                        tt(y, y, hrinv[:, t, 4 * j:4 * j + 4].unsqueeze(2).broadcast_to([P, 4, 64]), ALU.mult)
                    v.drain()
                    tt(MIX[:, t, MA:MA + 256], MIX[:, t, MA:MA + 256], ROWS[:, R_GA:R_GA + 256], ALU.mult)
                    tt(MIX[:, t, MC:MC + 256], MIX[:, t, MC:MC + 256], ROWS[:, R_GO:R_GO + 256], ALU.mult)
                    v.drain()
                    tt(MIX[:, t, MA:MA + 256], MIX[:, t, MA:MA + 256], PR[:, t, AO:AO + 256], ALU.mult)
                v.drain().then_inc(mix_ready, 1)

                job = 0
                for n in range(2):
                    for t in range(NT):
                        ps = V.take(v)
                        tmp = xtmp[:, job % 2, :]
                        V.give(tt(tmp, ps[:, :], GB[:, 0, cond_of(t), n * 512:(n + 1) * 512], ALU.mult))
                        v.drain()
                        tt(X[:, t, n * 512:(n + 1) * 512], X[:, t, n * 512:(n + 1) * 512], tmp, ALU.add)
                        job += 1
                v.drain().then_inc(x_ready, 1)
                normed()
                v.drain()
                v.wait_ge(x_spilled, 16 * (layer + 1))
                modulated(HTF, 1)
                v.drain().then_inc(half_ready, 1)
                ht_t.next(v)
                tt(HTL[:, :, :], HTF, HTH[:, :, :].bitcast(F32), ALU.subtract).then_inc(split_ready, 1)
                for n in range(1, 4):
                    wh_t.next(v)
                    tt(WQL[n % 2][:, :, :, :], wq_slot[n % 2].rearrange("p (c k n) -> p c k n", c=4, k=KD),
                       WQH[n % 2][:, :, :, :].bitcast(F32), ALU.subtract).then_inc(wq_split, 1)
                barrier()

                for t in range(NT):
                    s = SC[:, t]
                    for rnd in range(2):
                        lo, hi = 8 * rnd, 8 * rnd + 8
                        for c in range(HC):
                            v.max(val[:, c, lo:hi], s[:, c, :])
                        v.drain()
                        for c in range(HC):
                            v.max_index(idx[:, c, lo:hi], val[:, c, lo:hi], s[:, c, :])
                        if rnd == 0:
                            v.drain()
                            for c in range(HC):
                                v.match_replace(s[:, c, :], val[:, c, lo:hi], s[:, c, :], -BIG)
                            v.drain()
                    v.drain()
                    v.tensor_copy(idxf[:, :, :, :].rearrange("p h c k -> p (h c) k"), idx[:, :, :])
                    v4 = val[:, :, :].rearrange("p (h c) k -> p h c k", c=2)
                    tt(cand, v4[:, :, 0, :].unsqueeze(3).broadcast_to([P, HEADS, TOPK, TOPK]),
                       v4[:, :, 1, :].unsqueeze(2).broadcast_to([P, HEADS, TOPK, TOPK]), ALU.add)
                    v.drain()
                    for rnd in range(2):
                        lo, hi = 8 * rnd, 8 * rnd + 8
                        for h in range(HEADS):
                            v.max(tops[:, h, lo:hi], cand[:, h].rearrange("p a b -> p (a b)"))
                        v.drain()
                        for h in range(HEADS):
                            v.max_index(posu[:, h, lo:hi], tops[:, h, lo:hi], cand[:, h].rearrange("p a b -> p (a b)"))
                        if rnd == 0:
                            v.drain()
                            for h in range(HEADS):
                                ch = cand[:, h].rearrange("p a b -> p (a b)")
                                v.match_replace(ch, tops[:, h, lo:hi], ch, -BIG)
                            v.drain()
                    v.drain()
                    tt(gate[:, :, :], tops[:, :, :], tops[:, :, 0:1].broadcast_to([P, HEADS, TOPK]), ALU.subtract)
                    v.tensor_scalar(pab[0], pflat, 4, None, ALU.logical_shift_right)
                    v.tensor_scalar(pab[1], pflat, 15, None, ALU.bitwise_and)
                    v.drain().then_inc(tops_ready, 1)
                    for j in range(2):
                        v.tensor_copy(pabf[j], pab[j])
                    v.drain()
                    for j in range(2):
                        eq3 = eq.rearrange("p (n a) -> p n a", a=TOPK)
                        tt(eq3, pabf[j].unsqueeze(2).broadcast_to([P, P, TOPK]),
                           iota[:, 0:TOPK].unsqueeze(1).broadcast_to([P, P, TOPK]), ALU.is_equal)
                        v.drain()
                        eq4 = eq.rearrange("p (h k a) -> p h k a", h=HEADS, a=TOPK)
                        tt(eq4, eq4, idxf[:, :, j, :].unsqueeze(2).broadcast_to([P, HEADS, TOPK, TOPK]), ALU.mult)
                        v.drain()
                        v.tensor_reduce(sel[j], eq3, AX_X, ALU.add)
                        v.drain()
                    te_t.next(v)
                    v.tensor_reduce(gsum, gate[:, :, :], AX_X, ALU.add)
                    v.drain()
                    v.reciprocal(grec, gsum)
                    v.drain()
                    tt(gate[:, :, :], gate[:, :, :], grec.unsqueeze(2).broadcast_to([P, HEADS, TOPK]), ALU.mult)
                    v.drain().then_inc(picks_ready, 1)
                    ps = V.take(v)
                    cols = slice(t * P, (t + 1) * P)
                    for j in range(3):
                        ins = v.tensor_copy(IGT[j][:, cols], ps[:, j * P:(j + 1) * P])
                    V.give(ins)
                barrier()

                used = Tally(sca_filled, loop_base["gate", layer])
                with v.Fori(0, N // (2 * GT)) as i:
                    used.enter(i, 64)
                    for slot in range(2):
                        with v.Fori(0, GT // TOK) as j:
                            used.enter(j, 8)
                            for b in range(4):
                                v.wait_ge(sca_filled, used.at(b + 1 - 4))
                                for q in range(4):
                                    tok = i * (2 * GT) + (slot * GT + 4 * b + q) + j * 16

                                    def col(a):
                                        return a[:, bass.ds(tok, 1)]
                                    v.tensor_scalar(OH[:, b, q, 1, :], iota, col(IGT[1]), None, ALU.is_equal)
                                    ins = v.tensor_scalar(OH[:, b, q, 0, :], iota, col(IGT[0]), col(IGT[2]),
                                                          ALU.is_equal, ALU.mult)
                                ins.then_inc(onehot_ready, 1)
                            used.n += 8
                            used.leave(GT // TOK)
                    used.leave(N // (2 * GT))
                barrier()

                v.memset(ACC, 0.0)
                v.drain()
                steps = NK // (2 * GROUP)

                def product(b):
                    in_t[b % GROUP].n += 16
                    v.drain()
                    if b % GROUP == 0:
                        gi_t[b // GROUP].n += 16
                        v.wait_ge(gates_in[b // GROUP], gi_t[b // GROUP].at())
                    v.wait_ge(hidden_in[b % GROUP], in_t[b % GROUP].at())
                    tt(TMP[b % 2].rearrange("p (h t) -> p h t", t=GT), HB[b % GROUP].rearrange("p (h t) -> p h t", t=GT),
                       GG[b // GROUP][:, :, b % GROUP, :], ALU.mult).then_inc(gated_ready, 1)

                def low(b):
                    hi_t.next(v)
                    tt(HWL[:, b, :], TMP[b % 2], HWH[:, b, :].bitcast(F32), ALU.subtract).then_inc(low_ready, 1)

                def hidden_group(g):
                    product(GROUP * g)
                    for b in range(GROUP * g, GROUP * (g + 1)):
                        if b + 1 < GROUP * (g + 1):
                            product(b + 1)
                        low(b)

                def add_outputs():
                    for t in range(NT):
                        for ch in range(2):
                            ps = V.take(v)
                            a = ACC[:, t, ch * 512:(ch + 1) * 512]
                            V.give(tt(a, a, ps[:, :], ALU.add))
                    v.drain()

                for g in range(2):
                    hidden_group(g)
                with v.Fori(0, steps - 1) as i:
                    V.filled.enter(i, 4 * NT)
                    hi_t.enter(i, 2 * GROUP)
                    for x in in_t:
                        x.enter(i, 32)
                    for x in gi_t:
                        x.enter(i, 16)
                    for g in range(2):
                        add_outputs()
                        hidden_group(g)
                    for x in [V.filled, hi_t] + in_t + gi_t:
                        x.leave(steps - 1)
                for g in range(2):
                    add_outputs()
                for t in range(NT):
                    tt(ACC[:, t, :], ACC[:, t, :], GB[:, 1, cond_of(t), :], ALU.mult)
                v.drain()
                vx_t.n += 16
                v.wait_ge(x_back, vx_t.n)
                for t in range(NT):
                    tt(X[:, t, :], X[:, t, :], ACC[:, t, :], ALU.add)
                v.drain().then_inc(x_final if layer == DEPTH - 1 else x_ready, 1)
                barrier()

        @block.scalar
        def _(a):
            S = BankReader(sbank, sca_filled, sca_drained)
            phase = [0]
            x_t, mod_t, gs_t, ld_t = Tally(x_ready), Tally(mod_ready), Tally(group_squares), Tally(lam_dots)
            bs_t, cs_t, sg_t, ma_t, hs_t = Tally(b_scores), Tally(c_scores), Tally(gates_signed), Tally(ml_args), Tally(head_squares)
            tp_t, xn_t, gd_t = Tally(tops_ready), Tally(xn_ready), Tally(gated_ready, GROUP)
            stored = [Tally(s) for s in gates_stored]
            kept = [Tally(s) for s in hidden_stored]
            ur, vr = [Tally(s) for s in u_in], [Tally(s) for s in v_in]
            it_t, wi_t = Tally(it_half), [Tally(s) for s in wi_in]

            def barrier():
                phase[0] += 1
                a.drain().then_inc(phase_done, 1)
                a.wait_ge(phase_done, 3 * phase[0])

            def roots():
                for t in range(NT):
                    a.activation(MIX[:, t, :], X[:, t, :], ACT.Square, accum_out=ssq[:, t:t + 1])
                a.drain()
                a.activation(root[:, :], ssq[:, :], ACT.Sqrt, bias=eps, scale=1.0 / D).then_inc(roots_ready, 1)

            def modulated(dest, which):
                for t in range(NT):
                    ps = S.take(a)
                    c = cond_of(t)
                    for k in range(4):
                        ins = a.activation(dest[:, k, t * P:(t + 1) * P], ps[:, k * P:(k + 1) * P], ACT.Identity,
                                           bias=mod[:, 2 * which, k, c:c + 1], scale=mod[:, 2 * which + 1, k, c:c + 1])
                    S.give(ins)

            def high_u(b):
                ur[b].n += 16
                a.wait_ge(u_in[b], ur[b].at())
                a.activation(UH[:, b, :, :], UR[b], ACT.Copy).then_inc(u_high, 1)

            def hidden_block(block, b, more=True):
                if more:
                    high_u(1 - b)
                kept[b].n += 16
                a.wait_ge(hidden_stored[b], kept[b].at())
                for j in range(2):
                    ps = S.take(a)
                    S.give(a.activation(GE[:, b, j * HALF:(j + 1) * HALF], ps[:, 0:HALF], ACT.Gelu))
                a.wait_ge(sca_drained, S.filled.at())
                a.dma_start(io["hidden"][bass.ds(block, 1)].rearrange("o p t -> p (o t)"), GE[:, b, :])\
                    .then_inc(hidden_stored[b], 16)

            def hidden_loop(first, turns):
                with a.Fori(0, turns) as j:
                    S.filled.enter(j, 4)
                    for x in kept + ur:
                        x.enter(j, 16)
                    for b in range(2):
                        hidden_block(j * 2 + (first + b), b)
                    for x in [S.filled] + kept + ur:
                        x.leave(turns)

            a.wait_ge(cond_in, 16)
            a.activation(conds[:, :, :], cond[:, :, :], ACT.Silu).then_inc(cond_ready, 1)
            a.wait_ge(setup_in, 16 * 3)
            for layer in range(DEPTH):
                if layer:
                    x_t.next(a)
                roots()
                for w in range(2):
                    for c in range(2):
                        for half in range(2):
                            ps = S.take(a)
                            S.give(a.activation(GB[:, w, c, half * 512:(half + 1) * 512], ps[:, :], ACT.Copy))
                mod_t.next(a)
                modulated(HTk, 0)
                a.drain()
                it_t.next(a)
                a.activation(ITH[:, :, :], HTk, ACT.Copy).then_inc(it_high, 1)
                for n in range(IN_SLICES):
                    wi_t[n % 2].n += 16
                    if n >= 1:
                        if n >= 3:
                            a.wait_ge(vec_filled, wi_read[layer][n - 2])
                        a.wait_ge(wi_in[n % 2], wi_t[n % 2].n)
                        a.activation(WIH[n % 2][:, :, :], WIR[n % 2], ACT.Copy).then_inc(wi_high, 1)
                barrier()

                gs_t.next(a)
                a.activation(groot[:, :, 0:10], gss[:, :, 0:10], ACT.Sqrt, bias=eps, scale=1.0 / 64)
                a.activation(groot[:, :, 10:26], gss[:, :, 10:26], ACT.Sqrt, bias=eps, scale=1.0 / 32).then_inc(group_roots, 1)
                ld_t.next(a)
                a.activation(lamv[:, 0:2], lamv[:, 0:2], ACT.Exp).then_inc(lam_exps, 1)
                for t in range(NT):
                    for b0 in range(0, 13, 4):
                        nb = min(4, 13 - b0)
                        ps = S.take(a)
                        S.give(a.activation(QKT[:, b0:b0 + nb, t * P:(t + 1) * P],
                                            ps[:, 0:nb * P].rearrange("p (b n) -> p b n", b=nb), ACT.Copy))
                units = b_units()

                def exps(u):
                    nk = b_keys(units[u][0])
                    bs_t.next(a)
                    for i in range(2):
                        row = b_s[:, u % 2, i, 0:nk + 1]
                        ins = a.activation(row, row, ACT.Exp, bias=bmax[:, u % 4, i:i + 1], scale=0.125,
                                           accum_out=bsum[:, u % 4, i:i + 1])
                    ins.then_inc(b_exps, 1)

                exps(0)
                exps(1)
                for u in range(len(units)):
                    nk = b_keys(units[u][0])
                    for i in range(2):
                        ps = S.take(a)
                        S.give(a.activation(b_et[:, u % 2, i, 0:nk], ps[:, 0:nk], ACT.Copy))
                    if u + 2 < len(units):
                        exps(u + 2)
                barrier()

                cu = c_units()

                def c_exp(u):
                    nk = c_keys(cu[u][0])
                    cs_t.next(a)
                    for i in range(2):
                        row = c_s[:, u % 2, i, 0:nk]
                        ins = a.activation(row, row, ACT.Exp, bias=cmax[:, u % 2, i:i + 1], scale=32 ** -0.5,
                                           accum_out=csum[:, u % 2, i:i + 1])
                    ins.then_inc(c_exps, 1)

                c_exp(0)
                c_exp(1)
                for u in range(len(cu)):
                    nk = c_keys(cu[u][0])
                    for b0 in range(0, nk, 512):
                        n = min(512, nk - b0)
                        ps = S.take(a)
                        S.give(a.activation(c_at[:, u % 2, b0:b0 + n], ps[:, 0:n], ACT.Copy))
                    if u + 2 < len(cu):
                        c_exp(u + 2)
                barrier()

                sg_t.next(a)
                a.activation(lft[:, :], lft[:, :], ACT.Exp)
                a.drain()
                a.activation(lft[:, :], lft[:, :], ACT.Ln, bias=ones[:, 0:1]).then_inc(softplus_ready, 1)
                au = a_units()
                k5 = args[:, :].rearrange("p (k d t h) -> p k d t h", k=5, d=2, t=NT)

                def key_weights(u):
                    seg, d, t = au[u]
                    for h in range(4):
                        ins = a.activation(cm[:, d, t, h, :], cm[:, d, t, h, :], ACT.Exp, bias=k5[:, 4, d, t, h:h + 1])
                    ins.then_inc(ml_exps, 1)

                ma_t.next(a)
                a.activation(args[:, 0:160], args[:, 0:160], ACT.Exp).then_inc(ml_exps, 1)
                key_weights(0)
                key_weights(1)
                for u in range(len(au)):
                    ps = S.take(a)
                    S.give(a.activation(pt[:, u % 2], ps[:, :].rearrange("p (h s) -> p h s", h=4), ACT.Copy))
                    if u + 2 < len(au):
                        key_weights(u + 2)
                barrier()

                hs_t.next(a)
                a.activation(PR[:, :, AO:AO + 256], PR[:, :, AO:AO + 256], ACT.Sigmoid)
                a.activation(hroot[:, :, :], hss[:, :, :], ACT.Sqrt, bias=eps, scale=1.0 / 64).then_inc(head_roots, 1)
                for t in range(NT):
                    for half in range(2):
                        ps = S.take(a)
                        S.give(a.activation(HTk[:, 4 * half:4 * half + 4, t * P:(t + 1) * P],
                                            ps[:, :].rearrange("p (k n) -> p k n", k=4), ACT.Copy))
                x_t.next(a)
                roots()
                a.wait_ge(x_spilled, 16 * (layer + 1))
                a.wait_ge(xn_ready, NT * (2 * layer + 2))
                modulated(HTF, 1)
                a.drain()
                a.wait_ge(half_ready, layer + 1)
                a.activation(HTH[:, :, :], HTF, ACT.Copy).then_inc(turned_ready, 1)
                def queries(c):
                    for j in range(2):
                        ps = S.take(a)
                        S.give(a.activation(QT[:, c % 2, j * HALF:(j + 1) * HALF], ps[:, 0:HALF], ACT.Copy))
                for c in range(HC + 1):
                    if c in (2, 6, 10):
                        n = c // 4 + 1
                        if n == 2:
                            a.wait_ge(split_ready, layer + 1)
                        a.wait_ge(wq_in[n % 2], 16 * (2 * layer + n // 2 + 1))
                        a.activation(WQH[n % 2][:, :, :, :], wq_slot[n % 2].rearrange("p (c k n) -> p c k n", c=4, k=KD),
                                     ACT.Copy).then_inc(wq_high, 1)
                    if c < HC:
                        queries(c)
                    if c >= 1:
                        for t0, n in ((0, 4), (4, 1)):
                            ps = S.take(a)
                            S.give(a.activation(SC[:, t0:t0 + n, c - 1, :], ps[:, 0:n * P].rearrange("p (t k) -> p t k", t=n),
                                                ACT.Copy))
                barrier()
                high_u(0)
                for t in range(NT):
                    first, turns = sum(PICK_BLOCKS[:t]), min(8, PICK_BLOCKS[t]) // 2
                    hidden_loop(first, turns)
                    tp_t.next(a)
                    a.activation(gate, gate, ACT.Exp).then_inc(top_exps, 1)
                    if PICK_BLOCKS[t] > 8:
                        hidden_loop(first + 8, (PICK_BLOCKS[t] - 8) // 2)
                barrier()

                turns, inner = N // (2 * GT), GT // TOK
                with a.Fori(0, turns) as i:
                    S.filled.enter(i, 16 * inner)
                    for x in kept + ur:
                        x.enter(i, 2 * inner * 16)
                    for x in stored:
                        x.enter(i, 16)
                    for slot in range(2):
                        stored[slot].n += 16
                        with a.Fori(0, inner) as j:
                            S.filled.enter(j, 8)
                            for x in kept + ur:
                                x.enter(j, 16)
                            for b in range(2):
                                hidden_block(i * (4 * inner) + (sum(PICK_BLOCKS) + slot * 2 * inner + b) + j * 2, b)
                            a.wait_ge(gates_stored[slot], stored[slot].at())
                            for b in range(4):
                                ps = S.take(a)
                                dst = GS[slot][:, :, bass.ds(j * TOK + 4 * b, 4)].rearrange("p b t -> p t b")
                                S.give(a.activation(dst, ps[:, :].rearrange("p (t b) -> p t b", t=4), ACT.Copy))
                            for x in [S.filled] + kept + ur:
                                x.leave(inner)
                        a.wait_ge(sca_drained, S.filled.at())
                        dst = io["gates"][bass.ds(i * 2 + slot, 1)].rearrange("o p b t -> p (o b) t")
                        a.dma_start(dst, GS[slot]).then_inc(gates_stored[slot], 16)
                    for x in [S.filled] + kept + stored + ur:
                        x.leave(turns)
                done = sum(PICK_BLOCKS) + 2 * N // TOK
                if NK - done > 2:
                    hidden_loop(done, (NK - done) // 2 - 1)
                for b in range(2):
                    hidden_block(NK - 2 + b, b, more=(b == 0))
                for x in stored + kept:
                    a.wait_ge(x.sem, x.n + 16)
                barrier()

                steps = NK // (2 * GROUP)
                with a.Fori(0, steps) as i:
                    gd_t.enter(i, 2 * GROUP)
                    for x in vr:
                        x.enter(i, 32)
                    for b in range(2 * GROUP):
                        gd_t.next(a)
                        a.activation(HWH[:, b, :], TMP[b % 2], ACT.Copy).then_inc(high_ready, 1)
                        vr[b % 4].n += 16
                        a.wait_ge(v_in[b % 4], vr[b % 4].at())
                        a.activation(VH[:, b, :], VR[b % 4][:, :], ACT.Copy).then_inc(v_high, 1)
                    for x in [gd_t] + vr:
                        x.leave(steps)
                barrier()

        @block.gpsimd
        def _(g):
            uh, vh = Tally(u_high), Tally(v_high)
            g.sem_inc(u_split, 2)
            g.sem_inc(v_split, 4)
            for layer in range(DEPTH):
                with g.Fori(0, NK // 2) as i:
                    uh.enter(i, 2)
                    for b in range(2):
                        uh.next(g)
                        g.tensor_tensor(UL[:, b, :, :], UR[b], UH[:, b, :, :].bitcast(F32), ALU.subtract)\
                            .then_inc(u_split, 1)
                    uh.leave(NK // 2)
                with g.Fori(0, NK // (2 * GROUP)) as i:
                    vh.enter(i, 2 * GROUP)
                    for b in range(2 * GROUP):
                        vh.next(g)
                        g.tensor_tensor(VL[:, b, :], VR[b % 4][:, :], VH[:, b, :].bitcast(F32), ALU.subtract)\
                            .then_inc(v_split, 1)
                    vh.leave(NK // (2 * GROUP))

        @block.sync
        def _(sp):
            sp.dma_start(cond[:, :, :], io["cond"]).then_inc(cond_in, 16)
            for slot in range(2):
                sp.sem_inc(gates_stored[slot], 16)
                sp.sem_inc(hidden_stored[slot], 16)
            sp.sem_inc(gated_ready, GROUP)
            n_slice = [0]
            outs = [0]

            def load(src, width):
                n = n_slice[0]
                n_slice[0] += 1
                if n >= 3:
                    sp.wait_ge(*slice_read[n - 3])
                sp.dma_start(wslot[n % 3][:, 0:width], src).then_inc(slice_in[n % 3], 16)

            def store(dst, src):
                sp.dma_start(dst, src).then_inc(out_done, 16)
                outs[0] += 16

            us = Tally(u_split)
            for layer in range(DEPTH):
                ph = 8 * layer
                if layer:
                    sp.wait_ge(vec_filled, out_filled[layer - 1])
                if layer == 0:
                    for n in range(2):
                        load(io["w_ada"][layer, n], KD * 512)
                    sp.dma_start(CON[:, :], io["consts"]).then_inc(setup_in, 16)
                    sp.dma_start(X[:, 0, :], io["x_prompt"]).then_inc(setup_in, 16)
                    sp.dma_start(X[:, 1:NT, :], io["x_sample"].rearrange("(t p) c -> p t c", p=P)).then_inc(setup_in, 16)
                sp.dma_start(ROWS[:, :], io["rows"][layer:layer + 1, :].broadcast_to([P, N_ROWS])).then_inc(vectors_in, 16)
                sp.dma_start(bada, io["b_ada"][layer:layer + 1, :].broadcast_to([2, 6 * D])).then_inc(vectors_in, 16)
                sp.dma_start(ngain[:, :, :], io["ngain"][layer]).then_inc(vectors_in, 16)
                for n in range(0 if layer else 2, ADA_SLICES):
                    load(io["w_ada"][layer, n], KD * 512)
                for n in range(IN_SLICES):
                    if n < 2:
                        sp.wait_ge(*slice_read[n_slice[0] - 3 + n])
                    else:
                        sp.wait_ge(vec_filled, wi_read[layer][n - 2])
                    sp.dma_start(WIR[n % 2].rearrange("p k n -> p (k n)"), io["w_in"][layer, n]).then_inc(wi_in[n % 2], 16)
                sp.wait_ge(phase_done, 3 * (ph + 1))
                sp.dma_start(kcb, io["cache_bk"][layer]).then_inc(caches_in, 16)
                sp.dma_start(kcc[:, :, :], io["cache_ck"][layer]).then_inc(caches_in, 16)
                sp.dma_start(vcb, io["cache_bv"][layer]).then_inc(caches_in, 16)
                sp.dma_start(vcc, io["cache_cv"][layer]).then_inc(caches_in, 16)
                sp.dma_start(mstate[:, 1], io["state_m"][layer:layer + 1].broadcast_to([P, 8])).then_inc(caches_in, 16)
                sp.wait_ge(qk_ready, NT * layer + 1)
                store(io["o_bk"][layer], PR[:, 0, BK:BK + 128])
                store(io["o_bv"][layer], PR[:, 0, BV:BV + 128])
                store(io["o_ck"][layer], PR[:, 0, CK:CK + 256])
                store(io["o_cv"][layer], PR[:, 0, CV:CV + 256])
                sp.wait_ge(qk_ready, NT * (layer + 1))
                sp.dma_start(cst[:, 1], io["state_C"][layer]).then_inc(caches_in, 16)
                sp.wait_ge(state_final, layer + 1)
                store(io["o_state"][layer], cst[:, 0])
                store(io["o_m"][layer:layer + 1], mstate[0:1, 0])
                sp.wait_ge(phase_done, 3 * (ph + 4))
                n_slice[0] += 1
                for n in range(2):
                    load(io["w_out"][layer, n], KD * 512)
                sp.wait_ge(mix_ready, layer + 1)
                sp.dma_start(SUBT[:, :, :], io["subkeys"][layer]).then_inc(subkeys_in, 16)
                for n in range(2):
                    sp.dma_start(wq_slot[n], io["wq"][layer, n]).then_inc(wq_in[n], 16)
                sp.wait_ge(x_ready, 2 * layer + 1)
                sp.dma_start(io["x"], X).then_inc(x_spilled, 16)
                for n in range(2, 4):
                    sp.wait_ge(sca_filled, wq_read[layer][n - 2])
                    sp.dma_start(wq_slot[n % 2], io["wq"][layer, n]).then_inc(wq_in[n % 2], 16)

                sp.wait_ge(phase_done, 3 * (ph + 5))
                us.n = 2 + layer * NK
                with sp.Fori(0, NK // 2) as i:
                    us.enter(i, 2)
                    for b in range(2):
                        sp.wait_ge(u_split, us.at(b - 1))
                        sp.dma_start(UR[b], io["u"][layer, bass.ds(i * 2 + b, 1)].rearrange("o p k e -> p (o k) e"))\
                            .then_inc(u_in[b], 16)
                    us.n += 2
                    us.leave(NK // 2)
                for slot in range(2):
                    sp.wait_ge(gates_stored[slot], 16 + 16 * (layer + 1) * (N // (2 * GT)))
                used = Tally(gated_ready, GROUP + layer * NK)
                vs = Tally(v_split, 4 + layer * NK)
                with sp.Fori(0, NK // (2 * GROUP)) as i:
                    used.enter(i, 2 * GROUP)
                    vs.enter(i, 2 * GROUP)
                    for b in range(2 * GROUP):
                        block_at = bass.ds(i * (2 * GROUP) + b, 1)
                        sp.wait_ge(gated_ready, used.at(b - GROUP + 1))
                        if b % GROUP == 0:
                            src = io["gates"][:, :, bass.ds(i * (2 * GROUP) + b, GROUP), :].rearrange("h p b t -> p h (b t)")
                            sp.dma_start(GG[b // GROUP].rearrange("p h b t -> p h (b t)"), src)\
                                .then_inc(gates_in[b // GROUP], 16)
                        sp.dma_start(HB[b % GROUP], io["hidden"][block_at].rearrange("o p t -> p (o t)"))\
                            .then_inc(hidden_in[b % GROUP], 16)
                        sp.wait_ge(v_split, vs.at(b - 3))
                        sp.dma_start(VR[b % 4][:, :], io["v"][layer, block_at].rearrange("o p c -> p (o c)"))\
                            .then_inc(v_in[b % 4], 16)
                    used.n += 2 * GROUP
                    vs.n += 2 * GROUP
                    used.leave(NK // (2 * GROUP))
                    vs.leave(NK // (2 * GROUP))
                sp.wait_ge(gated_ready, GROUP + (layer + 1) * NK)
                sp.dma_start(X, io["x"]).then_inc(x_back, 16)
            sp.wait_ge(x_final, 1)
            store(io["o_prompt"], X[:, 0, :])
            store(io["o_sample"].rearrange("(t p) c -> p t c", p=P), X[:, 1:NT, :])
            sp.wait_ge(out_done, outs[0])


def _constants():
    import numpy as np
    c = np.zeros((P, N_CONST), np.float32)
    i = np.arange(P)
    lower = i[:, None] >= i[None, :]
    c[:, C_ID:C_ID + P] = np.eye(P)
    c[:, C_TRIF:C_TRIF + P] = lower.T
    c[:, C_TRIB:C_TRIB + P] = lower
    c[:, C_ONE:C_ONE + P] = 1
    c[:, C_MF:C_MF + P] = np.where(lower, 0, NEG)
    c[:, C_MB:C_MB + P] = np.where(lower.T, 0, NEG)
    before, after = np.where(lower.T, 0, NEG), np.where(lower, 0, NEG)
    zero = np.zeros((P, P))
    c[:, C_BAND:C_BAND + 512] = np.concatenate([zero, before, zero, after], 1)
    c[:, C_BAND1:C_BAND1 + 384] = np.concatenate([zero, zero, after], 1)
    c[:, C_IOTA:C_IOTA + NK] = i
    t = np.arange(DEC_SEQ)
    place = np.stack([t // 64, t % 64], 1).astype(np.float32)
    for at, q in ((C_RB, 16), (C_RC, 8)):
        inv = (np.float32(10000.0) ** (-np.arange(q, dtype=np.float32) / np.float32(q))).astype(np.float32)
        ang = place[:, :, None] * inv
        for k, f in enumerate((np.cos, np.sin)):
            tab = f(ang).astype(np.float32).reshape(NT - 1, P, 2 * q).transpose(1, 0, 2).reshape(P, -1)
            c[:, at + k * 8 * q:at + (k + 1) * 8 * q] = tab
    for r in range(2):
        c[r, C_SEL + r * P:C_SEL + (r + 1) * P] = 1
    c[:, C_EPS] = EPS
    return c


def kernel(**inputs):
    import numpy as np
    import concourse.bacc as bacc
    from concourse.bass_utils import run_bass_kernel_spmd

    f = {k: np.asarray(v) for k, v in inputs.items()}
    L = DEPTH
    sizes = (256, 256, 256, 256, 16, 512, 128, 128, 256, 256, 256)
    starts = np.concatenate([[0], np.cumsum(sizes)])
    bq = starts[5] + np.concatenate([np.arange(64) + 64 * h for p in range(4) for h in (p, p + 4)])
    order = np.concatenate([np.arange(starts[5]), bq, np.arange(starts[6], starts[-1])])

    def chunks(w, width):
        n = w.shape[-1] // width
        return w.reshape(L, KD, P, n, width).transpose(0, 3, 2, 1, 4)

    def tiled(g, k):
        return np.tile(g.reshape(L, -1), (1, k))

    arrays = {
        "consts": _constants(),
        "cond": np.stack([f["c_ctx"].reshape(KD, P).T, f["c"].reshape(KD, P).T], -1),
        "x_prompt": f["x_prompt"][0],
        "x_sample": f["x_sample"][0],
        "rows": np.concatenate([f["b_in"][:, order], tiled(f["b_q_gain"], 8), tiled(f["b_k_gain"], 2),
                                tiled(f["c_q_gain"], 4), tiled(f["c_k_gain"], 4), f["a_out_gain"],
                                tiled(f["c_out_gain"], 4), f["b_sink"], f["c_lambda"].reshape(L, -1)], 1),
        "b_ada": f["b_ada"],
        "ngain": f["norm_gain"].reshape(L, 2, KD, P).transpose(0, 3, 1, 2),
        "w_ada": chunks(f["w_ada"], 512).reshape(L, ADA_SLICES, P, -1),
        "w_in": chunks(f["w_in"][:, :, order], IN_W).reshape(L, IN_SLICES, P, -1),
        "w_out": chunks(f["w_out"], 512).reshape(L, 2, P, -1),
        "wq": f["peer_wq"].reshape(L, KD, P, 4, 4, P).transpose(0, 3, 2, 4, 1, 5).reshape(L, 4, P, -1),
        "subkeys": f["peer_subkeys"].transpose(0, 4, 1, 2, 3).reshape(L, P, HC, NK),
        "cache_bk": f["cache_swa_k"][0].transpose(0, 2, 3, 1).reshape(L, P, PAST),
        "cache_bv": f["cache_swa_v"][0].reshape(L, PAST, 128),
        "cache_ck": f["cache_diff_k"][0].reshape(L, PAST, 2, P).transpose(0, 3, 2, 1),
        "cache_cv": f["cache_diff_v"][0].reshape(L, PAST, 256),
        "state_C": np.concatenate([f["state_mlstm_C"][0], f["state_mlstm_n"][0][..., None]], -1)
        .reshape(L, 2, 2, 2, 64, 65).transpose(0, 3, 4, 1, 2, 5).reshape(L, P, 2, 2, 65),
        "state_m": f["state_mlstm_m"][0].reshape(L, 8),
        "u": f["peer_u"].reshape(L, NK, P, KD, P).transpose(0, 1, 4, 3, 2),
        "v": f["peer_v"].reshape(L, NK, P, D),
    }
    outs = {"o_prompt": (SEQ, D), "o_sample": (DEC_SEQ, D), "o_bk": (L, P, 128), "o_bv": (L, P, 128),
            "o_ck": (L, P, 256), "o_cv": (L, P, 256), "o_state": (L, P, 2, 2, 65), "o_m": (L, 8)}
    nc = bacc.Bacc("TRN2", target_bir_lowering=False, num_devices=1)
    io, fed = {}, {}
    for name, a in arrays.items():
        a = np.ascontiguousarray(a)
        fed[f"in_{name}"] = a
        io[name] = nc.dram_tensor(f"in_{name}", a.shape, mybir.dt.from_np(a.dtype), kind="ExternalInput").ap()
    for name, shape in outs.items():
        io[name] = nc.dram_tensor(f"out_{name}", shape, F32, kind="ExternalOutput").ap()
    io["hidden"] = nc.dram_tensor("hidden", (NK, P, N), F32, kind="Internal").ap()
    io["x"] = nc.dram_tensor("x_kept", (P, NT, D), F32, kind="Internal").ap()
    io["gates"] = nc.dram_tensor("gates", (N // GT, P, NK, GT), F32, kind="Internal").ap()
    hybrid_step(nc, io)
    r = run_bass_kernel_spmd(nc, [fed], core_ids=[0]).results[0]
    g = {name: np.asarray(r[f"out_{name}"]) for name in outs}
    state = g["o_state"].reshape(L, 2, 64, 2, 2, 65).transpose(0, 3, 4, 1, 2, 5).reshape(1, L, 2, 4, 64, 65)
    return (g["o_prompt"][None], g["o_sample"][None],
            g["o_bk"].reshape(1, L, P, 2, 64), g["o_bv"].reshape(1, L, P, 2, 64),
            g["o_ck"].reshape(1, L, P, 4, 64), g["o_cv"].reshape(1, L, P, 4, 64),
            np.ascontiguousarray(state[..., :64]), np.ascontiguousarray(state[..., 64]),
            g["o_m"].reshape(1, L, 2, 4))
```
